# Optimizing a Trainium2 kernel written in Bass

```python
import jax, jax.numpy as jnp
from jax import lax
import numpy as np

D_MODEL = 1024
BATCH = 1
SEQ = 256
DEPTH = 2
DEC_BATCH = 8
DEC_SEQ = 1
PAST_LEN = 2048
PAGE_SIZE = 128

N_BRANCH = 4
BRANCH_W = D_MODEL // N_BRANCH
RWKV_N = 64
RWKV_H = BRANCH_W // RWKV_N
RWKV_W_LORA = 32
RWKV_A_LORA = 32
RWKV_G_LORA = 64
RWKV_COLS = 3 * BRANCH_W + RWKV_W_LORA + RWKV_A_LORA + RWKV_G_LORA
RWKV_GN_EPS = 64e-5
ML_DH = 64
ML_H = BRANCH_W // ML_DH
ML_CONV = 4
GLA_H = 4
GLA_DV = BRANCH_W // GLA_H
GLA_DK = GLA_DV // 2
GLA_LORA = 16
GLA_TAU = 16.0
RG_BLOCKS = 4
RG_BW = BRANCH_W // RG_BLOCKS
RG_CONV = 4
RG_C = 8.0
CHUNK = 64
D_FF = 2816
N_EXPERTS = 8
TOP_K = 2
N_DENSE = (DEPTH + 1) // 2
N_MOE = DEPTH // 2
DN_ALPHA = (2 * DEPTH) ** 0.25
DN_BETA = (8 * DEPTH) ** -0.25
LN_EPS = 1e-5

IN_SIZES = (
    RWKV_COLS,
    2 * BRANCH_W,
    BRANCH_W,
    BRANCH_W,
    ML_H,
    ML_H,
    GLA_H * GLA_DK,
    GLA_H * GLA_DK,
    BRANCH_W,
    BRANCH_W,
    GLA_LORA,
    BRANCH_W,
    BRANCH_W,
    N_BRANCH * D_MODEL,
)
IN_COLS = sum(IN_SIZES)

STATE_SHAPES = (
    (RWKV_COLS,),
    (RWKV_H, RWKV_N, RWKV_N),
    (ML_CONV - 1, 2 * BRANCH_W),
    (ML_H, ML_DH, ML_DH),
    (ML_H, ML_DH),
    (ML_H,),
    (GLA_H, GLA_DK, GLA_DV),
    (RG_CONV - 1, BRANCH_W),
    (BRANCH_W,),
)

kernel_name = 'hybrid_rwkv7_mlstm_gla_rglru_decode_step'

F32 = jnp.float32

def _split(u, sizes):
    idx = [int(i) for i in np.cumsum(sizes)[:-1]]
    return jnp.split(u, idx, axis=-1)

def _layer_norm(x, g, b):
    xf = x.astype(F32)
    mu = xf.mean(-1, keepdims=True)
    var = jnp.square(xf - mu).mean(-1, keepdims=True)
    return ((xf - mu) * lax.rsqrt(var + LN_EPS) * g + b).astype(x.dtype)

def _head_norm(x, eps):
    mu = x.mean(-1, keepdims=True)
    var = jnp.square(x - mu).mean(-1, keepdims=True)
    return (x - mu) * lax.rsqrt(var + eps)

def _head_rms(x, eps):
    return x * lax.rsqrt(jnp.square(x).mean(-1, keepdims=True) + eps)

def _causal_conv(u, buf, w, b):
    width = w.shape[0]
    L = u.shape[1]
    full = jnp.concatenate([buf.astype(u.dtype), u], axis=1)
    out = b
    for j in range(width):
        out = out + full[:, j:j + L] * w[j]
    return out, full[:, full.shape[1] - (width - 1):]

def _to_chunks(t, lc):
    B, L = t.shape[:2]
    t = t.reshape((B, L // lc, lc) + t.shape[2:])
    return jnp.moveaxis(jnp.moveaxis(t, 1, 0), 2, 3)

def _from_chunks(t):
    nc, B, H, lc, d = t.shape
    return jnp.swapaxes(jnp.moveaxis(t, 0, 1), 2, 3).reshape(B, nc * lc, H, d)

def _chunk_len(L):
    return CHUNK if L % CHUNK == 0 else L

def _rwkv7_scan(r, decay, k, v, kk, a, S0):
    def step(S, inp):
        r_t, w_t, k_t, v_t, kk_t, a_t = inp
        sa = jnp.einsum('bhij,bhj->bhi', S, -kk_t)
        S = (S * w_t[:, :, None, :] + sa[..., None] * (kk_t * a_t)[:, :, None, :]
             + v_t[..., None] * k_t[:, :, None, :])
        return S, jnp.einsum('bhij,bhj->bhi', S, r_t)
    xs = tuple(jnp.moveaxis(t, 1, 0) for t in (r, decay, k, v, kk, a))
    S, ys = lax.scan(step, S0, xs)
    return jnp.moveaxis(ys, 0, 1), S

def _rwkv7(u, shift_prev, S0, mu, w0, w_up, a0, a_up, g_up, k_k, k_a, r_k, ln_w, ln_b):
    B, L, _ = u.shape
    prev = jnp.concatenate([shift_prev[:, None].astype(u.dtype), u[:, :-1]], axis=1)
    um = u + mu * (prev - u)
    r, k, v, wd, ad, gd = _split(um, (BRANCH_W, BRANCH_W, BRANCH_W, RWKV_W_LORA, RWKV_A_LORA, RWKV_G_LORA))

    def heads(t):
        return t.astype(F32).reshape(B, L, RWKV_H, RWKV_N)

    w_log = -jax.nn.softplus(-(w0 + jnp.tanh(wd) @ w_up).astype(F32)) - 0.5
    decay = heads(jnp.exp(-jnp.exp(w_log)))
    a = heads(jax.nn.sigmoid((a0 + ad @ a_up).astype(F32)))
    g = (jax.nn.sigmoid(gd) @ g_up).astype(F32)
    r4, k4, v4 = heads(r), heads(k), heads(v)
    kk = k4 * k_k.astype(F32).reshape(RWKV_H, RWKV_N)
    kk = kk / jnp.maximum(jnp.sqrt(jnp.sum(kk * kk, -1, keepdims=True)), 1e-12)
    k4 = k4 * (1.0 + (a - 1.0) * k_a.astype(F32).reshape(RWKV_H, RWKV_N))
    o, S = _rwkv7_scan(r4, decay, k4, v4, kk, a, S0.astype(F32))
    o = (_head_norm(o, RWKV_GN_EPS) * ln_w.reshape(RWKV_H, RWKV_N)
         + ln_b.reshape(RWKV_H, RWKV_N))
    o = o + jnp.sum(r4 * k4 * r_k, -1, keepdims=True) * v4
    out = o.reshape(B, L, BRANCH_W) * g
    return out.astype(u.dtype), u[:, -1], S

def _mlstm_chunks(q, k, v, i_pre, logf, C0, n0, m0):
    L = q.shape[1]
    lc = _chunk_len(L)
    mask = jnp.tril(jnp.ones((lc, lc), bool))

    def step(carry, inp):
        C, n, m = carry
        qc, kc, vc, ic, fc = inp
        b = jnp.cumsum(fc, axis=-1)
        log_d = jnp.where(mask, b[..., :, None] - b[..., None, :] + ic[..., None, :], -jnp.inf)
        log_inter = b + m[..., None]
        m_t = jnp.maximum(log_inter, log_d.max(-1))
        dmat = jnp.exp(log_d - m_t[..., None])
        inter = jnp.exp(log_inter - m_t)
        s = jnp.einsum('bhtd,bhsd->bhts', qc, kc) * dmat
        num = (jnp.einsum('bhts,bhsv->bhtv', s, vc)
               + inter[..., None] * jnp.einsum('bhvk,bhtk->bhtv', C, qc))
        dot = s.sum(-1) + inter * jnp.einsum('bhk,bhtk->bht', n, qc)
        h = num / jnp.maximum(jnp.abs(dot), jnp.exp(-m_t))[..., None]
        m_new = m_t[..., -1]
        w_s = jnp.exp(b[..., -1:] - b + ic - m_new[..., None])
        keep = jnp.exp(b[..., -1] + m - m_new)
        C = keep[..., None, None] * C + jnp.einsum('bhs,bhsv,bhsk->bhvk', w_s, vc, kc)
        n = keep[..., None] * n + jnp.einsum('bhs,bhsk->bhk', w_s, kc)
        return (C, n, m_new), h

    xs = tuple(_to_chunks(t, lc) for t in (q, k, v, i_pre, logf))
    (C, n, m), hs = lax.scan(step, (C0, n0, m0), xs)
    return _from_chunks(hs), C, n, m

def _mlstm(qk_cols, v_cols, o_cols, i_cols, f_cols, conv_buf, C0, n0, m0, conv_w, conv_b, norm_w):
    B, L, _ = qk_cols.shape
    qk, new_buf = _causal_conv(qk_cols, conv_buf, conv_w, conv_b)
    qk = jax.nn.silu(qk).astype(F32)
    q, k = jnp.split(qk, 2, axis=-1)
    q = q.reshape(B, L, ML_H, ML_DH)
    k = k.reshape(B, L, ML_H, ML_DH) * (ML_DH ** -0.5)
    v = v_cols.astype(F32).reshape(B, L, ML_H, ML_DH)
    logf = jax.nn.log_sigmoid(f_cols.astype(F32))
    h, C, n, m = _mlstm_chunks(q, k, v, i_cols.astype(F32), logf,
                               C0.astype(F32), n0.astype(F32), m0.astype(F32))
    h = _head_norm(h, 1e-6).reshape(B, L, BRANCH_W) * norm_w * jax.nn.sigmoid(o_cols.astype(F32))
    return h.astype(qk_cols.dtype), new_buf, C, n, m

def _gla_chunks(q, k, v, log_a, S0):
    L = q.shape[1]
    lc = _chunk_len(L)
    mask = jnp.tril(jnp.ones((lc, lc), bool))[..., None]

    def step(S, inp):
        qc, kc, vc, lac = inp
        b = jnp.cumsum(lac, axis=2)
        diff = jnp.where(mask, b[:, :, :, None, :] - b[:, :, None, :, :], -jnp.inf)
        attn = jnp.einsum('bhtd,bhsd,bhtsd->bhts', qc, kc, jnp.exp(diff))
        o = (jnp.einsum('bhts,bhsv->bhtv', attn, vc)
             + jnp.einsum('bhtd,bhdv->bhtv', qc * jnp.exp(b), S))
        b_last = b[:, :, -1:, :]
        S = (jnp.exp(b_last[:, :, 0])[..., None] * S
             + jnp.einsum('bhsd,bhsv->bhdv', kc * jnp.exp(b_last - b), vc))
        return S, o

    xs = tuple(_to_chunks(t, lc) for t in (q, k, v, log_a))
    S, os_ = lax.scan(step, S0, xs)
    return _from_chunks(os_), S

def _gla(q_cols, k_cols, v_cols, g_cols, a_cols, S0, alpha_up, alpha_b, norm_w):
    B, L, _ = q_cols.shape
    q = q_cols.astype(F32).reshape(B, L, GLA_H, GLA_DK) * (GLA_DK ** -0.5)
    k = k_cols.astype(F32).reshape(B, L, GLA_H, GLA_DK)
    v = v_cols.astype(F32).reshape(B, L, GLA_H, GLA_DV)
    log_a = (jax.nn.log_sigmoid((a_cols @ alpha_up + alpha_b).astype(F32)) / GLA_TAU
             ).reshape(B, L, GLA_H, GLA_DK)
    o, S = _gla_chunks(q, k, v, log_a, S0.astype(F32))
    o = _head_rms(o, 1e-6).reshape(B, L, BRANCH_W) * norm_w * jax.nn.silu(g_cols.astype(F32))
    return o.astype(q_cols.dtype), S

def _rglru(x_cols, y_cols, conv_buf, h0, conv_w, conv_b, wa, ba, wx, bx, lam):
    B, L, _ = x_cols.shape
    xc, new_buf = _causal_conv(x_cols, conv_buf, conv_w, conv_b)
    xc = xc.astype(F32)
    xb = xc.reshape(B, L, RG_BLOCKS, RG_BW)
    r = jax.nn.sigmoid(jnp.einsum('blgi,gij->blgj', xb, wa).reshape(B, L, BRANCH_W) + ba)
    i = jax.nn.sigmoid(jnp.einsum('blgi,gij->blgj', xb, wx).reshape(B, L, BRANCH_W) + bx)
    log_a = -RG_C * r * jax.nn.softplus(-lam.astype(F32))
    a = jnp.exp(log_a)
    u = jnp.sqrt(-jnp.expm1(2.0 * log_a)) * (i * xc)
    u = u.at[:, 0].add(a[:, 0] * h0.astype(F32))

    def combine(p, q):
        return p[0] * q[0], q[0] * p[1] + q[1]

    _, h = lax.associative_scan(combine, (a, u), axis=1)
    y = h * jax.nn.gelu(y_cols.astype(F32))
    return y.astype(x_cols.dtype), new_buf, h[:, -1]

def _mixer(x, st, p, l):
    B, L, D = x.shape
    u = x @ p['w_in'][l] + p['b_in'][l]
    (rw, mqk, mv, mo, mi, mf, gq, gk, gv, gg, ga, rx, ry, gates) = _split(u, IN_SIZES)
    sh0, S0, mconv0, C0, n0, m0, gS0, rconv0, h0 = st
    o_a, sh1, S1 = _rwkv7(rw, sh0, S0, p['rwkv_mu'][l], p['rwkv_w0'][l], p['rwkv_w_up'][l],
                          p['rwkv_a0'][l], p['rwkv_a_up'][l], p['rwkv_g_up'][l], p['rwkv_k_k'][l],
                          p['rwkv_k_a'][l], p['rwkv_r_k'][l], p['rwkv_ln_w'][l], p['rwkv_ln_b'][l])
    o_b, mconv1, C1, n1, m1 = _mlstm(mqk, mv, mo, mi, mf, mconv0, C0, n0, m0,
                                     p['mlstm_conv_w'][l], p['mlstm_conv_b'][l], p['mlstm_norm_w'][l])
    o_c, gS1 = _gla(gq, gk, gv, gg, ga, gS0, p['gla_alpha_up'][l], p['gla_alpha_b'][l],
                    p['gla_norm_w'][l])
    o_d, rconv1, h1 = _rglru(rx, ry, rconv0, h0, p['rglru_conv_w'][l], p['rglru_conv_b'][l],
                             p['rglru_wa'][l], p['rglru_ba'][l], p['rglru_wx'][l], p['rglru_bx'][l],
                             p['rglru_lambda'][l])
    branches = jnp.stack([o_a, o_b, o_c, o_d], axis=2)
    up = jnp.einsum('blgc,gcd->blgd', branches, p['w_branch'][l])
    gate = jax.nn.sigmoid(gates.reshape(B, L, N_BRANCH, D))
    merged = jnp.einsum('blgd,blgd->bld', gate, up)
    out = merged @ p['w_out'][l]
    return out, (sh1, S1, mconv1, C1, n1, m1, gS1, rconv1, h1)

def _swiglu(x, wg, wu, wd):
    return (jax.nn.silu(x @ wg) * (x @ wu)) @ wd

def _moe(x, router, router_b, wg, wu, wd):
    B, L, D = x.shape
    xt = x.reshape(B * L, D)
    logits = (xt @ router).astype(F32) + router_b
    top_v, top_i = lax.top_k(logits, TOP_K)
    top_w = jax.nn.softmax(top_v, axis=-1)
    gate = jnp.sum(jax.nn.one_hot(top_i, N_EXPERTS, dtype=F32) * top_w[..., None], axis=1)
    y = jnp.zeros((B * L, D), F32)
    for e in range(N_EXPERTS):
        y = y + gate[:, e:e + 1] * _swiglu(xt, wg[e], wu[e], wd[e])
    return y.astype(x.dtype).reshape(B, L, D)

def _trunk(x, states, p):
    new = [[] for _ in STATE_SHAPES]
    for l in range(DEPTH):
        st = tuple(s[l] for s in states)
        m_out, st_new = _mixer(x, st, p, l)
        x = _layer_norm(DN_ALPHA * x + m_out, p['ln1_g'][l], p['ln1_b'][l])
        j = l // 2
        if l % 2 == 0:
            f = _swiglu(x, p['ffn_wg'][j], p['ffn_wu'][j], p['ffn_wd'][j])
        else:
            f = _moe(x, p['moe_router'][j], p['moe_router_b'][j], p['moe_wg'][j],
                     p['moe_wu'][j], p['moe_wd'][j])
        x = _layer_norm(DN_ALPHA * x + f, p['ln2_g'][l], p['ln2_b'][l])
        for idx, s in enumerate(st_new):
            new[idx].append(s.astype(x.dtype))
    return x, [jnp.stack(s, 0) for s in new]

def setup_inputs(seed: int = 0) -> dict:
    key = jax.random.key(seed)
    ks = iter(jax.random.split(key, 64))

    def nrm(shape, scale):
        return jax.random.normal(next(ks), shape, F32) * scale

    Ld, W, D = DEPTH, BRANCH_W, D_MODEL
    x_prompt = nrm((BATCH, SEQ, D), 1.0)
    x_sample = nrm((DEC_BATCH, DEC_SEQ, D), 1.0)
    state_rwkv_shift = nrm((Ld, DEC_BATCH, RWKV_COLS), 1.0)
    state_rwkv_S = nrm((Ld, DEC_BATCH, RWKV_H, RWKV_N, RWKV_N), 0.1)
    state_mlstm_conv = nrm((Ld, DEC_BATCH, ML_CONV - 1, 2 * W), 1.0)
    state_mlstm_C = nrm((Ld, DEC_BATCH, ML_H, ML_DH, ML_DH), 0.1)
    state_mlstm_n = nrm((Ld, DEC_BATCH, ML_H, ML_DH), 0.5)
    state_mlstm_m = nrm((Ld, DEC_BATCH, ML_H), 0.5)
    state_gla_S = nrm((Ld, DEC_BATCH, GLA_H, GLA_DK, GLA_DV), 0.1)
    state_rglru_conv = nrm((Ld, DEC_BATCH, RG_CONV - 1, W), 1.0)
    state_rglru_h = nrm((Ld, DEC_BATCH, W), 0.5)

    w_in = nrm((Ld, D, IN_COLS), D ** -0.5)
    f_off = int(sum(IN_SIZES[:5]))
    b_in = nrm((Ld, IN_COLS), 0.02).at[:, f_off:f_off + ML_H].add(jnp.linspace(3.0, 6.0, ML_H))
    rwkv_mu = jax.random.uniform(next(ks), (Ld, RWKV_COLS), F32)
    rwkv_w0 = jnp.tile(jnp.linspace(-5.0, 1.0, RWKV_N), RWKV_H)[None] + nrm((Ld, W), 0.1)
    rwkv_w_up = nrm((Ld, RWKV_W_LORA, W), 0.1)
    rwkv_a0 = nrm((Ld, W), 0.1)
    rwkv_a_up = nrm((Ld, RWKV_A_LORA, W), 0.1)
    rwkv_g_up = nrm((Ld, RWKV_G_LORA, W), RWKV_G_LORA ** -0.5)
    rwkv_k_k = 0.85 + nrm((Ld, W), 0.02)
    rwkv_k_a = 1.0 + nrm((Ld, W), 0.02)
    rwkv_r_k = nrm((Ld, RWKV_H, RWKV_N), 0.1)
    rwkv_ln_w = 1.0 + nrm((Ld, W), 0.02)
    rwkv_ln_b = nrm((Ld, W), 0.02)
    mlstm_conv_w = nrm((Ld, ML_CONV, 2 * W), 0.5)
    mlstm_conv_b = nrm((Ld, 2 * W), 0.02)
    mlstm_norm_w = 1.0 + nrm((Ld, W), 0.02)
    gla_alpha_up = nrm((Ld, GLA_LORA, GLA_H * GLA_DK), GLA_LORA ** -0.5)
    gla_alpha_b = 2.0 + nrm((Ld, GLA_H * GLA_DK), 0.1)
    gla_norm_w = 1.0 + nrm((Ld, W), 0.02)
    rglru_conv_w = nrm((Ld, RG_CONV, W), 0.5)
    rglru_conv_b = nrm((Ld, W), 0.02)
    rglru_wa = nrm((Ld, RG_BLOCKS, RG_BW, RG_BW), RG_BW ** -0.5)
    rglru_ba = nrm((Ld, W), 0.02)
    rglru_wx = nrm((Ld, RG_BLOCKS, RG_BW, RG_BW), RG_BW ** -0.5)
    rglru_bx = nrm((Ld, W), 0.02)
    a_pow = jax.random.uniform(next(ks), (Ld, W), F32, minval=0.9, maxval=0.999)
    s = a_pow ** (1.0 / RG_C)
    rglru_lambda = jnp.log(s) - jnp.log1p(-s)
    w_branch = nrm((Ld, N_BRANCH, W, D), (W ** -0.5) * DN_BETA)
    w_out = nrm((Ld, D, D), (D ** -0.5) * DN_BETA)
    ln1_g = 1.0 + nrm((Ld, D), 0.02)
    ln1_b = nrm((Ld, D), 0.02)
    ffn_wg = nrm((N_DENSE, D, D_FF), D ** -0.5)
    ffn_wu = nrm((N_DENSE, D, D_FF), D ** -0.5)
    ffn_wd = nrm((N_DENSE, D_FF, D), (D_FF ** -0.5) * DN_BETA)
    moe_router = nrm((N_MOE, D, N_EXPERTS), D ** -0.5)
    moe_router_b = nrm((N_MOE, N_EXPERTS), 0.01)
    moe_wg = nrm((N_MOE, N_EXPERTS, D, D_FF), D ** -0.5)
    moe_wu = nrm((N_MOE, N_EXPERTS, D, D_FF), D ** -0.5)
    moe_wd = nrm((N_MOE, N_EXPERTS, D_FF, D), (D_FF ** -0.5) * DN_BETA)
    ln2_g = 1.0 + nrm((Ld, D), 0.02)
    ln2_b = nrm((Ld, D), 0.02)
    return {
        'x_prompt': x_prompt, 'x_sample': x_sample,
        'state_rwkv_shift': state_rwkv_shift, 'state_rwkv_S': state_rwkv_S,
        'state_mlstm_conv': state_mlstm_conv, 'state_mlstm_C': state_mlstm_C,
        'state_mlstm_n': state_mlstm_n, 'state_mlstm_m': state_mlstm_m,
        'state_gla_S': state_gla_S, 'state_rglru_conv': state_rglru_conv,
        'state_rglru_h': state_rglru_h,
        'w_in': w_in, 'b_in': b_in,
        'rwkv_mu': rwkv_mu, 'rwkv_w0': rwkv_w0, 'rwkv_w_up': rwkv_w_up, 'rwkv_a0': rwkv_a0,
        'rwkv_a_up': rwkv_a_up, 'rwkv_g_up': rwkv_g_up, 'rwkv_k_k': rwkv_k_k, 'rwkv_k_a': rwkv_k_a,
        'rwkv_r_k': rwkv_r_k, 'rwkv_ln_w': rwkv_ln_w, 'rwkv_ln_b': rwkv_ln_b,
        'mlstm_conv_w': mlstm_conv_w, 'mlstm_conv_b': mlstm_conv_b, 'mlstm_norm_w': mlstm_norm_w,
        'gla_alpha_up': gla_alpha_up, 'gla_alpha_b': gla_alpha_b, 'gla_norm_w': gla_norm_w,
        'rglru_conv_w': rglru_conv_w, 'rglru_conv_b': rglru_conv_b, 'rglru_wa': rglru_wa,
        'rglru_ba': rglru_ba, 'rglru_wx': rglru_wx, 'rglru_bx': rglru_bx,
        'rglru_lambda': rglru_lambda,
        'w_branch': w_branch, 'w_out': w_out, 'ln1_g': ln1_g, 'ln1_b': ln1_b,
        'ffn_wg': ffn_wg, 'ffn_wu': ffn_wu, 'ffn_wd': ffn_wd,
        'moe_router': moe_router, 'moe_router_b': moe_router_b,
        'moe_wg': moe_wg, 'moe_wu': moe_wu, 'moe_wd': moe_wd,
        'ln2_g': ln2_g, 'ln2_b': ln2_b,
    }

def reference(x_prompt, x_sample, state_rwkv_shift, state_rwkv_S, state_mlstm_conv, state_mlstm_C,
              state_mlstm_n, state_mlstm_m, state_gla_S, state_rglru_conv, state_rglru_h,
              w_in, b_in, rwkv_mu, rwkv_w0, rwkv_w_up, rwkv_a0, rwkv_a_up, rwkv_g_up, rwkv_k_k,
              rwkv_k_a, rwkv_r_k, rwkv_ln_w, rwkv_ln_b, mlstm_conv_w, mlstm_conv_b, mlstm_norm_w,
              gla_alpha_up, gla_alpha_b, gla_norm_w, rglru_conv_w, rglru_conv_b, rglru_wa, rglru_ba,
              rglru_wx, rglru_bx, rglru_lambda, w_branch, w_out, ln1_g, ln1_b, ffn_wg, ffn_wu, ffn_wd,
              moe_router, moe_router_b, moe_wg, moe_wu, moe_wd, ln2_g, ln2_b):
    p = dict(w_in=w_in, b_in=b_in, rwkv_mu=rwkv_mu, rwkv_w0=rwkv_w0, rwkv_w_up=rwkv_w_up,
             rwkv_a0=rwkv_a0, rwkv_a_up=rwkv_a_up, rwkv_g_up=rwkv_g_up, rwkv_k_k=rwkv_k_k,
             rwkv_k_a=rwkv_k_a, rwkv_r_k=rwkv_r_k, rwkv_ln_w=rwkv_ln_w, rwkv_ln_b=rwkv_ln_b,
             mlstm_conv_w=mlstm_conv_w, mlstm_conv_b=mlstm_conv_b, mlstm_norm_w=mlstm_norm_w,
             gla_alpha_up=gla_alpha_up, gla_alpha_b=gla_alpha_b, gla_norm_w=gla_norm_w,
             rglru_conv_w=rglru_conv_w, rglru_conv_b=rglru_conv_b, rglru_wa=rglru_wa,
             rglru_ba=rglru_ba, rglru_wx=rglru_wx, rglru_bx=rglru_bx, rglru_lambda=rglru_lambda,
             w_branch=w_branch, w_out=w_out, ln1_g=ln1_g, ln1_b=ln1_b,
             ffn_wg=ffn_wg, ffn_wu=ffn_wu, ffn_wd=ffn_wd,
             moe_router=moe_router, moe_router_b=moe_router_b,
             moe_wg=moe_wg, moe_wu=moe_wu, moe_wd=moe_wd, ln2_g=ln2_g, ln2_b=ln2_b)
    zero_states = [jnp.zeros((DEPTH, x_prompt.shape[0]) + s, x_prompt.dtype) for s in STATE_SHAPES]
    y_prompt, ps = _trunk(x_prompt, zero_states, p)
    sample_states = [state_rwkv_shift, state_rwkv_S, state_mlstm_conv, state_mlstm_C, state_mlstm_n,
                     state_mlstm_m, state_gla_S, state_rglru_conv, state_rglru_h]
    y_sample, ss = _trunk(x_sample, sample_states, p)
    (p_rwkv_shift, p_rwkv_S, p_mlstm_conv, p_mlstm_C, p_mlstm_n, p_mlstm_m,
     p_gla_S, p_rglru_conv, p_rglru_h) = ps
    (s_rwkv_shift, s_rwkv_S, s_mlstm_conv, s_mlstm_C, s_mlstm_n, s_mlstm_m,
     s_gla_S, s_rglru_conv, s_rglru_h) = ss
    return (y_prompt, y_sample,
            p_rwkv_shift, p_rwkv_S, p_mlstm_conv, p_mlstm_C, p_mlstm_n, p_mlstm_m,
            p_gla_S, p_rglru_conv, p_rglru_h,
            s_rwkv_shift, s_rwkv_S, s_mlstm_conv, s_mlstm_C, s_mlstm_n, s_mlstm_m,
            s_gla_S, s_rglru_conv, s_rglru_h)


_drawn_inputs = setup_inputs


def setup_inputs(seed=0):
    import zlib

    import numpy as np

    out = dict(_drawn_inputs(seed))
    spreads = {}
    factors = {'rwkv_k_k': 38.4,
     'rwkv_k_a': 2.716,
     'rwkv_ln_w': 28.314,
     'rwkv_ln_b': 32.479,
     'mlstm_norm_w': 27.272,
     'gla_norm_w': 24.316,
     'rglru_ba': 8.0,
     'rglru_bx': 8.0,
     'moe_router_b': 3.941,
     'rwkv_r_k': 3.119}
    for name, (base, spread) in spreads.items():
        noise = np.random.default_rng([zlib.crc32(name.encode()), seed]).standard_normal(out[name].shape)
        drawn = base * np.exp(spread * noise) if base else spread * noise
        out[name] = __import__('jax').numpy.asarray(drawn.astype(out[name].dtype))
    for name, factor in factors.items():
        out[name] = (out[name] * factor).astype(out[name].dtype)
    return out
```

```python
from contextlib import ExitStack

import numpy as np

import concourse.bass as bass
from concourse import mybir

F32 = mybir.dt.float32
I32 = mybir.dt.int32
U32 = mybir.dt.uint32
ALU = mybir.AluOpType
ACT = mybir.ActivationFunctionType
AX_X = mybir.AxisListType.X

P = 128
D = 1024
KT = D // P
DEPTH = 2
TP, TD = 256, 8
T = TP + TD
FF = 2816
NE = 8
CH = 64
NC = TP // CH
ALPHA = (2 * DEPTH) ** 0.25
LN_EPS = 1e-5

TR, TK, TV, TLO, TMI, TMQ, TMK, TMV, TGQ, TGK, TMO, TGV, TGG, TRX, TRY = 0, 2, 4, 6, 7, 8, 10, 12, 14, 15, 16, 18, 20, 22, 24
NU = 26
NG = 32
NM = NU + NG
SLOTS = 9
SLOT = 2048
GR = 16
FC = FF // 256
FT = FF // P

PC = {}


def _cols():
    at = 0
    for name, n in (("bin", NU), ("bgate", NG), ("mu", 7), ("w0", 2), ("a0", 2), ("kk", 2), ("ka", 2), ("rk", 2),
                    ("lnw", 2), ("lnb", 2), ("mcw", 16), ("mcb", 4), ("mnw", 2), ("gab", 1), ("gnw", 2),
                    ("rcw", 8), ("rcb", 2), ("rba", 2), ("rbx", 2), ("lam", 2),
                    ("ln1g", KT), ("ln1b", KT), ("ln2g", KT), ("ln2b", KT)):
        PC[name] = at
        at += n
    return at


NPAR = _cols()

CC = {}


def _const_cols():
    at = 0
    for name, n in (("ident", P), ("bo", P), ("bom", P), ("mean", P), ("mb", 256), ("mk", 256), ("ml16", P), ("mlo", P),
                    ("i64", 64), ("neg", P), ("gv", 256), ("gy", 256), ("gm", 256), ("reset", TP), ("ones", TP),
                    ("tri", P), ("iota", P), ("iota8", NE)):
        CC[name] = at
        at += n
    return at


NCON = _const_cols()


def constants():
    c = np.zeros((P, NCON), np.float32)
    i = np.arange(P)
    s, t = i[:, None], i[None, :]

    def put(name, m):
        c[:m.shape[0], CC[name]:CC[name] + m.shape[1]] = m

    b64, b16 = s // 64 == t // 64, s // 16 == t // 16
    put("ident", np.eye(P))
    put("bo", b64 * 1.0)
    put("bom", b64 / 64.0)
    put("mean", np.full((P, P), 1.0 / D))
    put("mb", np.concatenate([-1.0 * (b16 & (s < t)), -1.0 * (b64 & (s <= t))], 1))
    put("mk", np.concatenate([1.0 * (b64 & (s < t)), 1.0 * (b64 & (s <= t))], 1))
    put("ml16", -1.0 * (b16 & (t < s)))
    put("mlo", -1.0 * (b64 & ~b16 & (t < s)))
    put("i64", 1.0 * (i[:, None] % 64 == np.arange(64)[None]))
    put("neg", np.where(s <= t, 0.0, -1e30))
    put("gv", np.concatenate([1.0 * (2 * j + s // 64 == t // 32) for j in range(2)], 1))
    put("gy", np.concatenate([1.0 * (2 * j + t // 64 == s // 32) for j in range(2)], 1))
    put("gm", 1.0 * (i[:, None] // 32 == np.arange(256)[None] // 64))
    put("reset", np.tile(1.0 * (np.arange(TP) % CH != 0), (P, 1)))
    put("ones", np.ones((P, TP)))
    put("tri", 1.0 * (s < t))
    put("iota", np.tile(np.arange(P), (P, 1)))
    put("iota8", np.tile(np.arange(NE), (P, 1)))
    return c




class Steps:

    def __init__(self, nc, ctx, engine, table):
        self.engine = engine
        self.first, self.count, self.sem, self.fired, self.seen = {}, {}, {}, {}, {}
        for name, n in table:
            g = self.group(name, n)
            if g not in self.sem:
                self.sem[g] = ctx.enter_context(nc.semaphore(f"{g}_{engine}"))
                self.count[g] = self.fired[g] = 0
            self.first[name] = g, self.count[g]
            self.count[g] += n

    @staticmethod
    def group(name, n):
        return name.split(".")[0] if n == 1 else name

    def step(self, name, i=0):
        if RECORD:
            self.seen[name] = self.seen.get(name, 0) + 1
            return self.scratch, 1
        g, first = self.first[name]
        assert self.fired[g] % self.count[g] == first + i, (self.engine, name, i, self.fired[g], self.count[g], first)
        self.fired[g] += 1
        return self.sem[g], 1

    def at(self, name, l, i=0):
        if RECORD:
            return self.scratch, 1
        g, first = self.first[name]
        return self.sem[g], l * self.count[g] + first + i + 1


RECORD = False
PE_TABLE = (
    ("u.tile", 26), ("lg.alpha", 1), ("gate.tile", 32), ("rg.gates", 1), ("ml.turn", 1),
    ("ml.logd", 4), ("ml.qk", 4), ("ml.num", 1), ("ml.emb", 1), ("ml.c", 1),
    ("ml.dvb", 1), ("ml.dnum", 1), ("gl.turn", 1), ("gl.attn", 1), ("gl.kv", 1),
    ("gl.y", 1), ("gl.dvb", 1), ("gl.dy", 1), ("rw.wa", 1), ("rw.g", 1),
    ("rw.ksum", 1), ("rw.bonus", 1), ("rw.dsa", 1), ("rw.dy", 1), ("rw.turn", 1),
    ("rw.bk", 2), ("rw.l", 2), ("rw.p2", 2), ("rw.p4", 2), ("rw.p8", 2),
    ("rw.q", 2), ("rw.et", 2), ("rw.e", 6), ("rw.wt", 2), ("rw.z", 4),
    ("rw.s", 4), ("rw.y", 2), ("hn.mean", 1), ("hn.var", 2), ("mg.up", 32),
    ("mg.out", 8), ("ln.mean", 2), ("ln.var", 2), ("ff.up", 11), ("ff.down", 8),
)
ACT_TABLE = (
    ("u.tile", 26), ("rg.tanh", 1), ("lg.exp", 1), ("gate.tile", 32), ("rg.exp", 1),
    ("rg.gelu", 1), ("rg.sqrt", 1), ("ml.silu", 1), ("ml.og", 1), ("ml.exps", 1),
    ("ml.d", 4), ("ml.abs", 1), ("gl.og", 1), ("gl.exp", 1), ("rw.lora", 1),
    ("rw.ksq", 1), ("rw.wa", 1), ("rw.g", 1), ("rw.ksqrt", 1), ("rw.exp", 1),
    ("rw.p2", 2), ("rw.p4", 2), ("rw.p8", 2), ("rw.et", 2), ("rw.wt", 2),
    ("hn.sq", 1), ("hn.sqrt", 1), ("ln.sq", 2), ("ln.sqrt", 2), ("ln.norm", 2),
    ("ff.tanh", 11),
)
DVE_TABLE = (
    ("u.half", 1), ("lg.in", 1), ("rg.conv", 1), ("rg.loga", 1), ("rg.gelu_in", 1),
    ("rg.var", 1), ("rg.out", 1), ("ml.conv", 1), ("ml.rows", 1), ("ml.qk", 1),
    ("ml.dec_rows", 1), ("ml.gcol", 1), ("ml.sd", 4), ("ml.kw", 4), ("ml.h", 1),
    ("ml.cout", 1), ("ml.dv", 1), ("ml.dq", 1), ("ml.out", 1), ("gl.cum", 1),
    ("gl.ops", 1), ("gl.turned", 1), ("gl.attn", 1), ("gl.state", 1), ("gl.dv", 1),
    ("gl.y", 1), ("gl.dec", 1), ("gl.dq", 1), ("gl.out", 1), ("rw.mixed", 1),
    ("rw.sg", 1), ("rw.rk", 1), ("rw.ksum", 1), ("rw.bonus", 1), ("rw.cum", 1),
    ("rw.dx", 1), ("rw.dec", 1), ("rw.dr", 1), ("rw.dout", 1), ("rw.ops", 1),
    ("rw.turned", 1), ("rw.bk", 2), ("rw.l", 2), ("rw.q0", 2), ("rw.q1", 2),
    ("rw.q2", 2), ("rw.v0", 2), ("rw.e", 6), ("rw.z", 4), ("rw.state", 4),
    ("rw.y", 2), ("hn.centred", 1), ("hn.var4", 1), ("hn.var", 1), ("br.ready", 1),
    ("mg.up", 32), ("mg.sum", 8), ("mg.out", 8), ("ln.centred", 2), ("ln.var", 2),
    ("ln.scaled", 2), ("ff.hid", 11), ("ff.down", 8),
)

def col(ap, n):
    return ap.unsqueeze(2).broadcast_to([ap.shape[0], ap.shape[1], n])


def mid(ap, n):
    return ap.unsqueeze(1).broadcast_to([ap.shape[0], n, ap.shape[1]])


def program(nc, A, O):
    with ExitStack() as ctx:
        def sb(name, shape, dt=F32):
            return ctx.enter_context(nc.sbuf_tensor(name, shape, dt))

        def sem(name):
            return ctx.enter_context(nc.semaphore(name))

        pe_of = Steps(nc, ctx, "pe", PE_TABLE)
        act_of = Steps(nc, ctx, "act", ACT_TABLE)
        dve_of = Steps(nc, ctx, "dve", DVE_TABLE)
        if RECORD:
            for st in (pe_of, act_of, dve_of):
                st.scratch = sem(f"rec_{st.engine}")
        act_link, dve_link = sem("act_link"), sem("dve_link")
        const_in, router_in, x_in, layer_in, state_out = sem("const_in"), sem("router_in"), sem("x_in"), sem("layer_in"), sem("state_out")
        slot_in = [sem(f"slot_in{i}") for i in range(SLOTS)]
        moe_setup_pe, moe_setup_dve, moe_setup_act = sem("moe_setup_pe"), sem("moe_setup_dve"), sem("moe_setup_act")
        rounds_known = sem("rounds_known")
        place_ready, placeT_pe, placeT_ready = sem("place_ready"), sem("placeT_pe"), sem("placeT_ready")
        gathered, gather_kept = sem("gathered"), sem("gather_kept")
        gate_done, up_done, down_done = sem("gate_done"), sem("up_done"), sem("down_done")
        tanh_done, hidden, down_kept = sem("tanh_done"), sem("hidden"), sem("down_kept")
        scattered, scatter_added = sem("scattered"), sem("scatter_added")
        placed, gated, round_over = sem("placed"), sem("gated"), sem("round_over")

        ring = sb("ring", [P, SLOTS, SLOT])
        con = sb("con", [P, NCON])
        par = sb("par", [P, NPAR])
        half = sb("half", [P, NPAR])
        lora = sb("lora", [P, 256])
        alup = sb("alup", [P, P])
        rgw = sb("rgw", [P, 4, P])
        X = sb("X", [P, KT, T])
        BIG = sb("BIG", [P, (NU + GR) * T])
        U = BIG[:, 0:NU * T].rearrange("p (n t) -> p n t", t=T)
        GT = BIG[:, NU * T:(NU + GR) * T].rearrange("p (n t) -> p n t", t=T)
        HS = BIG[:, 0:FT * T].rearrange("p (n t) -> p n t", t=T)
        V8 = sb("V8", [P, KT, T])
        SQ8 = sb("SQ8", [P, KT, T])
        SCR = sb("SCR", [P, 12416])
        small = sb("small", [P, 600])
        count_i = sb("count_i", [1, 4], I32)
        mA = ctx.enter_context(nc.psum_tensor("mA", [P, 4, 512], F32))
        mW = ctx.enter_context(nc.psum_tensor("mW", [P, 4, 512], F32))
        WF = mW[:, :, :].rearrange("p a b -> p (a b)")

        def C(name, n=P, rows=P):
            return con[0:rows, CC[name]:CC[name] + n]

        def pc(name, i=0, lo=0, hi=P, src=par):
            return src[lo:hi, PC[name] + i:PC[name] + i + 1]

        def hc(name, i=0, lo=0, hi=P):
            return pc(name, i, lo, hi, half)

        class Area:

            def __init__(self, base, at=0):
                self.base, self.at = base, at

            def __call__(self, *shape, rows=P):
                n = int(np.prod(shape))
                assert self.at + n <= self.base.shape[1], (self.at + n, self.base.shape)
                a = self.base[0:rows, self.at:self.at + n]
                self.at += n
                if len(shape) > 1:
                    k = "abcd"[:len(shape)]
                    a = a.rearrange(f"p ({' '.join(k)}) -> p {' '.join(k)}", **dict(zip(k, shape)))
                return a

        sm = Area(small)
        shift_in = sm(7, TD)
        shift_out = sm(7, 9)
        mbuf = sm(4, 3, TD)
        rbuf = sm(2, 3, TD)
        h0 = sm(2, TD)
        n0 = sm(2, TD)
        m0 = sm(TD, rows=P)[0:4, :]
        n_out = sm(2, 9)
        m_out = sm(9, rows=P)[0:4, :]
        h_out = sm(2, 9)
        mconv_out = sm(4, 3, 9)
        rconv_out = sm(2, 3, 9)
        lam4 = sm(2)
        PLAST = sm(2, NC)
        router = sm(KT, NE)
        rbias = sm(NE)
        sq8 = SQ8[:, :, :].rearrange("p a b -> p (a b)")

        ar = Area(SCR)
        LGN = 2 * T + 2
        LG, LE, LY, LZ = ar(LGN), ar(LGN), ar(LGN), ar(LGN)
        RC, RT, RA, RL, RE, RX = ar(2, T), ar(4, T), ar(2, T), ar(2, T), ar(2, T), ar(2, T)
        RS, RH = ar(2, T), ar(2, T)
        assert ar.at < 12416

        ar = Area(SCR, 2 * LGN)
        CV, TQ = ar(4, T), ar(4, T)
        MVT, MKT = ar(2, 256), ar(2, 256)
        MSD = ar(4, 384)
        MD = ar(2, 384)
        MR = ar(6 * T)
        MDEN = ar(2, T)
        MG = ar(2, 4)
        MDC = ar(2, 3, TD)
        ar_m = ar.at
        MS = ar(2, TD, 64)
        MX = ar(2, TD, 64)
        MCO = ar(2, 64)
        assert ar.at <= 12416, ar.at

        ar = Area(SCR, 2 * LGN)
        GB, GX = ar(TP), ar(4, TP)
        GQ, GK, GQH, GKH = ar(TP), ar(TP), ar(TP), ar(TP)
        GVT, GKT = ar(2, 256), ar(2, P)
        GAT = ar(2, 512)
        GKV = ar(NC, 256)
        GSS = ar(NC + 1, 256)
        GDX = ar(TD)
        GS, GXX = ar(TD, 64), ar(2, TD, 64)
        assert ar.at <= 12416, ar.at

        ar = Area(SCR)
        DL = ar(7, T)
        LW, AA, GG, TH = DL[:, 0:2, :], DL[:, 2:4, :], DL[:, 4:6, :], DL[:, 6, :]
        KKN, K4, RKV, NRM = ar(2, T), ar(2, T), ar(2, T), ar(2, T)
        AR = ar(2, 2, 2, P)
        BT, KTL, B2, K2 = ar(2, TP), ar(2, TP), ar(2, TP), ar(2, TP)
        ar_r = ar.at
        ATK, BTK, KTK, VTK = ar(2, 256), ar(2, 256), ar(2, 256), ar(2, 256)
        NB, MKS = ar(4, 256), ar(4, 256)
        VW = BIG[:, TRX * T:TRX * T + 512].rearrange("p (a b) -> p a b", a=2)
        WT = ar(2, P)
        ZZ = BIG[:, TGV * T:TGV * T + 512].rearrange("p (a b) -> p a b", a=2)
        SS = ar(2, NC + 1, 64)
        assert ar.at <= 12416, ar.at
        ar = Area(SCR, ar_r)
        DS, DX, DY = ar(2, TD, 64), ar(2, TD, 64), ar(2, TD, 64)
        DW = ar(2, TD)
        DKA = ar(2, TD)
        dead = BIG[:, TMQ * T:TMO * T]
        ND, NO, P2, P2T = (dead[:, 512 * i:512 * i + 512].rearrange("p (a b) -> p a b", a=4) for i in range(4))
        P4, P4T, QT, ET = (sq8[:, 512 * i:512 * i + 512].rearrange("p (a b) -> p a b", a=4) for i in range(4))
        EXPS = dead[:, 0:3 * 512].rearrange("p (a b t) -> p a b t", a=3, t=TP)

        OO = V8[:, 0:6, :]
        OT = SQ8[:, 0:6, :]
        MOG, GGS, BR = U[:, TMO:TMO + 2, :], U[:, TGG:TGG + 2, :], U[:, 0:8, :]
        RGY = U[:, TRY:TRY + 2, :]
        GTH = U[:, TRX:TRX + 2, :]
        YW = sq8[:, 0:512].rearrange("p (a b) -> p a b", a=2)
        BRANCH = [U[:, i, :] for i in range(6)] + [U[:, TRY, :], U[:, TRY + 1, :]]
        FTH = SCR[:, 0:4 * T].rearrange("p (a b t) -> p a b t", a=2, b=2)

        ar = Area(SCR)
        XT = ar(3, D)
        XE = ar(2, KT, P)
        HE = ar(2, 256)
        YE = ar(D)
        PL = ar(3, P)
        PG = ar(3, P)
        PGT = ar(2, T)
        LOG, TOP = ar(3, NE), ar(3, 8)
        TIX = ar(24).bitcast(U32).rearrange("p (a b) -> p a b", a=3)
        IXF = ar(3, 8)
        TW = ar(3, 2)
        MASK, TMPE = ar(3, NE), ar(3, NE)
        GATE, RANK = ar(3, 3 * NE + 1), ar(3, 3 * NE + 1)
        ETH = ar(2, 256)
        CNT = ar(8)

        chunks = []
        for l in range(DEPTH):
            gate_chunks = [(A["w_in"][l, NU // 2 + i], pe_of.at("gate.tile", l, 2 * i + 1)) for i in range(NG // 2)]
            chunks += [(A["w_in"][l, i], pe_of.at("u.tile", l, 2 * i + 1)) for i in range(NU // 2)] + gate_chunks[:GR // 2]
            for p in range(4):
                if p >= 2:
                    chunks += gate_chunks[4 * p:4 * p + 4]
                chunks.append((A["w_branch"][l, p], pe_of.at("mg.up", l, 8 * p + 7)))
            chunks += [(A["w_out"][l, p], pe_of.at("mg.out", l, 2 * p + 1)) for p in range(4)]
            if l == 0:
                chunks += [(A["ffn_up"][i], pe_of.at("ff.up", l, i // 2)) for i in range(2 * FC)]
                chunks += [(A["ffn_down"][i], pe_of.at("ff.down", l, 2 * (i // 3) + 1)) for i in range(12)]
        uses0 = [len(range(k, len(chunks), SLOTS)) for k in range(SLOTS)]
        PAIR = 6 * FC
        per_pair = [len(range(k, PAIR, SLOTS)) for k in range(SLOTS)]

        block = ctx.enter_context(nc.Block())

        def rounds_of(eng):
            eng.wait_ge(rounds_known, 1)
            return eng.value_load(count_i[0:1, 0:1], min_val=1, max_val=3)

        @block.sync
        def _(sp):
            sp.dma_start(con[:, :], A["const"]).then_inc(const_in, 16)
            sp.dma_start(X[:, :, :], A["x"]).then_inc(x_in, 16)
            for i, (src, _) in enumerate(chunks):
                if i >= SLOTS:
                    sp.wait_ge(*chunks[i - SLOTS][1])
                sp.dma_start(ring[:, i % SLOTS, :], src).then_inc(slot_in[i % SLOTS], 16)
            R = rounds_of(sp) if not RECORD else 1
            with sp.Fori(0, R) as r:
                with sp.Fori(0, NE // 2) as e2:
                    for i in range(PAIR):
                        last = (i - SLOTS) // 3
                        if i < SLOTS:
                            last = max(range(i, PAIR, SLOTS)) // 3 - 2 * FC
                        sp.wait_ge((gate_done, up_done, down_done)[i % 3], (r * (NE // 2) + e2) * (2 * FC) + (last + 1 + FC))
                        sp.dma_start(ring[:, i % SLOTS, :], A["moe"][bass.ds(e2 * PAIR + i, 1), :, :].rearrange("a p n -> (a p) n"))\
                            .then_inc(slot_in[i % SLOTS], 16)
            sp.wait_ge(*act_of.at("ln.norm", 1, 1))
            sp.dma_start(O["y"], X[:, :, :]).then_inc(state_out, 16)
            sp.wait_ge(state_out, 16 * (12 * DEPTH + 1))

        @block.gpsimd
        def _(pool):
            pool.dma_start(router, A["router"]).then_inc(router_in, 16)
            pool.dma_start(rbias, A["rbias"]).then_inc(router_in, 16)
            for l in range(DEPTH):
                if l:
                    pool.wait_ge(*act_of.at("ln.norm", l - 1, 1))
                for dst, src in ((par[:, :], "par"), (lora[:, :], "lora"), (alup[:, :], "alup"), (rgw[:, :, :], "rgw"), (shift_in, "shift"),
                                 (mbuf, "mconv"), (rbuf, "rconv"), (h0, "h0"), (n0, "n0"), (m0, "m0")):
                    pool.dma_start(dst, A[src][l]).then_inc(layer_in, 16)
                pool.wait_ge(*dve_of.at("rg.out", l))
                pool.dma_start(MS, A["mC"][l]).then_inc(layer_in, 16)
                pool.wait_ge(*dve_of.at("ml.out", l))
                pool.wait_ge(*pe_of.at("ml.c", l))
                pool.wait_ge(state_out, 16 * (12 * l + 8))
                pool.dma_start(GS, A["gS"][l]).then_inc(layer_in, 16)
                pool.wait_ge(*dve_of.at("gl.out", l))
                pool.wait_ge(state_out, 16 * (12 * l + 10))
                pool.dma_start(DS, A["rS"][l]).then_inc(layer_in, 16)

        LAYER_LOADS = 13

        LAYER_ACC = NU + NG + 4 * KT + KT
        FFN_ACC = 4 * FC + KT

        def acc_no(kind, l, i):
            base = l * (LAYER_ACC + FFN_ACC)
            if kind == "u":
                return base + i
            if kind == "gate":
                return base + NU + (i if i < GR else i + 8 * (i // 8))
            if kind == "up":
                return base + NU + GR + (i if i < 16 else i + 8 * (i // 8 - 1))
            if kind == "out":
                return base + NU + NG + 4 * KT + i
            return base + LAYER_ACC + (i if kind == "f" else 4 * FC + i)

        emptied = {}
        for l in range(DEPTH):
            for i in range(NU):
                emptied[acc_no("u", l, i)] = act_of.at("u.tile", l, i)
            for i in range(NG):
                emptied[acc_no("gate", l, i)] = act_of.at("gate.tile", l, i)
                emptied[acc_no("up", l, i)] = dve_of.at("mg.up", l, i)
            for i in range(KT):
                emptied[acc_no("out", l, i)] = dve_of.at("mg.out", l, i)
        for i in range(4 * FC):
            emptied[acc_no("f", 0, i)] = dve_of.at("ff.hid", 0, i // 4)
        for i in range(KT):
            emptied[acc_no("d", 0, i)] = dve_of.at("ff.down", 0, i)
        assert sorted(emptied) == list(range(len(emptied)))

        def acc(kind, l, i):
            return mA[:, acc_no(kind, l, i) % 4, 0:T]

        def loads(l, n):
            return layer_in, 16 * (LAYER_LOADS * l + n)

        @block.scalar
        def _(act):
            nact = nc.scalar
            linked = [0]

            def link(ins):
                linked[0] += 1
                ins.then_inc(act_link, 1)
                act.wait_ge(act_link, linked[0])

            def store(dst, src):
                act.dma_start(dst, src).then_inc(state_out, 16)

            for l in range(DEPTH):
                act.wait_ge(*loads(l, 10))
                if l:
                    act.wait_ge(state_out, 16 * 12 * l)
                for i in range(NU):
                    act.wait_ge(*pe_of.at("u.tile", l, i))
                    nact.activation(U[:, i, :], acc("u", l, i), ACT.Identity, bias=pc("bin", i)).then_inc(*act_of.step("u.tile", i))

                def gates(lo, hi):
                    for i in range(lo, hi):
                        act.wait_ge(*pe_of.at("gate.tile", l, i))
                        if i >= GR:
                            act.wait_ge(*dve_of.at("mg.up", l, i - GR))
                        nact.activation(GT[:, i % GR, :], acc("gate", l, i), ACT.Tanh, bias=hc("bgate", i), scale=0.5)\
                            .then_inc(*act_of.step("gate.tile", i))

                act.wait_ge(*dve_of.at("u.half", l))
                act.wait_ge(*act_of.at("u.tile", l, NU - 1))
                link(nact.activation(RX, RGY, ACT.Square))
                act.wait_ge(*pe_of.at("rg.gates", l))
                for j in range(4):
                    ins = nact.activation(RT[:, j, :], mW[:, j, 0:T], ACT.Tanh, scale=0.5,
                                          bias=hc("rba", j) if j < 2 else hc("rbx", j - 2))
                ins.then_inc(*act_of.step("rg.tanh"))
                act.wait_ge(*dve_of.at("lg.in", l))
                link(nact.activation(LE, LG, ACT.Abs))
                nact.activation(LE, LE, ACT.Exp, scale=-1.0).then_inc(*act_of.step("lg.exp"))
                gates(0, 2)
                act.wait_ge(*dve_of.at("rg.loga", l))
                nact.activation(RE, RL, ACT.Exp, scale=2.0)
                nact.activation(RS, RL, ACT.Tanh)
                nact.activation(RA, RL, ACT.Exp).then_inc(*act_of.step("rg.exp"))
                act.wait_ge(*dve_of.at("rg.gelu_in", l))
                nact.activation(RX, RX, ACT.Tanh, scale=0.7978845608028654).then_inc(*act_of.step("rg.gelu"))
                act.wait_ge(*dve_of.at("rg.var", l))
                nact.activation(RE, RE, ACT.Sqrt, scale=-1.0).then_inc(*act_of.step("rg.sqrt"))
                gates(2, 4)
                act.wait_ge(*dve_of.at("rg.out", l))
                store(O["h"][l], h_out)
                store(O["rconv"][l], rconv_out)
                store(O["shift"][l], shift_out)
                act.wait_ge(*dve_of.at("ml.conv", l))
                nact.activation(TQ, CV, ACT.Tanh, scale=0.5).then_inc(*act_of.step("ml.silu"))
                nact.activation(MOG, MOG, ACT.Tanh, scale=0.5).then_inc(*act_of.step("ml.og"))
                act.wait_ge(*dve_of.at("ml.rows", l))
                nact.activation(MR[0:4, 4 * T:5 * T], MR[0:4, T:2 * T], ACT.Exp, scale=-1.0)
                nact.activation(MR[0:4, 5 * T:5 * T + 16], MR[0:4, 5 * T:5 * T + 16], ACT.Exp)\
                    .then_inc(*act_of.step("ml.exps"))
                store(O["m"][l], m_out)
                store(O["mconv"][l], mconv_out)
                for h in range(4):
                    act.wait_ge(*pe_of.at("ml.logd", l, h))
                    if h >= 2:
                        act.wait_ge(*dve_of.at("ml.sd", l, h - 2))
                        act.wait_ge(*dve_of.at("ml.kw", l, h - 2))
                    act.wait_ge(*dve_of.at("ml.gcol", l))
                    nact.activation(MD[:, h % 2, 0:256], mW[:, h % 2, 0:256], ACT.Exp, bias=MG[:, 0, h:h + 1])
                    nact.activation(MD[:, h % 2, 256:384], mW[:, h % 2, 256:384], ACT.Exp, bias=MG[:, 1, h:h + 1])\
                        .then_inc(*act_of.step("ml.d", h))
                gates(4, 6)
                act.wait_ge(*pe_of.at("ml.num", l))
                nact.activation(MDEN[:, :, 0:256], mW[:, 2:4, 0:256], ACT.Abs).then_inc(*act_of.step("ml.abs"))
                gates(6, 8)
                act.wait_ge(*dve_of.at("ml.out", l))
                act.wait_ge(*dve_of.at("ml.cout", l))
                store(O["mC"][l], MCO)
                store(O["mCs"][l], MS)
                store(O["n"][l], n_out)
                nact.activation(GTH, GGS, ACT.Tanh, scale=0.5).then_inc(*act_of.step("gl.og"))
                act.wait_ge(*dve_of.at("gl.cum", l))
                nact.activation(GDX, LG[:, TP:T], ACT.Exp)
                nact.activation(GX, GX, ACT.Exp).then_inc(*act_of.step("gl.exp"))
                gates(8, 10)
                act.wait_ge(*dve_of.at("gl.dec", l))
                store(O["gSs"][l], GS)
                act.wait_ge(*dve_of.at("gl.state", l))
                store(O["gS"][l], GSS[:, NC, :])
                act.wait_ge(*dve_of.at("rw.mixed", l))
                nact.activation(TH[0:32, :], U[0:32, TLO, :], ACT.Tanh)
                nact.activation(TH[64:128, :], U[64:128, TLO, :], ACT.Tanh, scale=0.5).then_inc(*act_of.step("rw.lora"))
                nact.activation(NRM[:, 0, :], U[:, TK, :], ACT.Square, scale=pc("kk", 0))
                nact.activation(NRM[:, 1, :], U[:, TK + 1, :], ACT.Square, scale=pc("kk", 1)).then_inc(*act_of.step("rw.ksq"))
                act.wait_ge(*pe_of.at("rw.wa", l))
                for j in range(2):
                    nact.activation(LW[:, j, :], mW[:, j, 0:T], ACT.Tanh, scale=0.5, bias=hc("w0", j))
                    ins = nact.activation(AA[:, j, :], mW[:, 2 + j, 0:T], ACT.Tanh, scale=0.5, bias=hc("a0", j))
                ins.then_inc(*act_of.step("rw.wa"))
                act.wait_ge(*pe_of.at("rw.g", l))
                nact.activation(GG, mW[:, 0:2, 0:T], ACT.Copy).then_inc(*act_of.step("rw.g"))
                act.wait_ge(*dve_of.at("rw.ksum", l))
                nact.activation(NRM, NRM, ACT.Sqrt).then_inc(*act_of.step("rw.ksqrt"))
                act.wait_ge(*dve_of.at("rw.cum", l))
                nact.activation(DW, LW[:, :, TP:T], ACT.Exp)
                nact.activation(EXPS[:, 0, :, :], RKV[:, :, 0:TP], ACT.Exp)
                nact.activation(EXPS[:, 1, :, :], RKV[:, :, 0:TP], ACT.Exp, scale=-1.0)
                nact.activation(EXPS[:, 2, :, :], BT, ACT.Exp).then_inc(*act_of.step("rw.exp"))
                gates(10, 12)
                act.wait_ge(*dve_of.at("rw.dec", l))
                store(O["rSs"][l], DS)
                for g in range(2):
                    act.wait_ge(*pe_of.at("rw.p2", l, g))
                    nact.activation(P2, mW[:, 0, :], ACT.Copy)
                    nact.activation(P2T, mW[:, 1, :], ACT.Copy).then_inc(*act_of.step("rw.p2", g))
                    act.wait_ge(*pe_of.at("rw.p4", l, g))
                    nact.activation(P4, mW[:, 0, :], ACT.Copy)
                    nact.activation(P4T, mW[:, 1, :], ACT.Copy).then_inc(*act_of.step("rw.p4", g))
                    act.wait_ge(*pe_of.at("rw.p8", l, g))
                    nact.activation(P2, mW[:, 0, :], ACT.Copy).then_inc(*act_of.step("rw.p8", g))
                    act.wait_ge(*pe_of.at("rw.et", l, g))
                    nact.activation(ET, mW[:, 0, :], ACT.Copy).then_inc(*act_of.step("rw.et", g))
                    act.wait_ge(*pe_of.at("rw.wt", l, g))
                    nact.activation(WT, mW[:, 2, 0:256], ACT.Copy).then_inc(*act_of.step("rw.wt", g))
                    if g == 0:
                        gates(12, 16)
                act.wait_ge(*dve_of.at("rw.state", l, NC - 1))
                store(O["rS"][l], SS[:, :, NC, :])
                act.wait_ge(*dve_of.at("hn.centred", l))
                nact.activation(OT, OO, ACT.Square).then_inc(*act_of.step("hn.sq"))
                act.wait_ge(*dve_of.at("hn.var", l))
                nact.activation(OT, OT, ACT.Sqrt).then_inc(*act_of.step("hn.sqrt"))
                for p in range(2, 4):
                    gates(8 * p, 8 * p + 8)

                def norm(i):
                    act.wait_ge(*dve_of.at("ln.centred", l, i))
                    nact.activation(V8[:, :, :], SQ8[:, :, :], ACT.Square).then_inc(*act_of.step("ln.sq", i))
                    act.wait_ge(*dve_of.at("ln.var", l, i))
                    nact.activation(V8[:, 1, :], V8[:, 0, :], ACT.Sqrt).then_inc(*act_of.step("ln.sqrt", i))
                    act.wait_ge(*dve_of.at("ln.scaled", l, i))
                    for j in range(KT):
                        ins = nact.activation(X[:, j, :], SQ8[:, j, :], ACT.Identity, scale=pc(f"ln{i + 1}g", j),
                                              bias=pc(f"ln{i + 1}b", j))
                    ins.then_inc(*act_of.step("ln.norm", i))

                norm(0)
                if l == 0:
                    for c in range(FC):
                        act.wait_ge(*pe_of.at("ff.up", l, c))
                        if c >= 2:
                            act.wait_ge(*dve_of.at("ff.hid", l, c - 2))
                        for q in range(2):
                            ins = nact.activation(FTH[:, c % 2, q, :], acc("f", l, 4 * c + q), ACT.Tanh, scale=0.5)
                        ins.then_inc(*act_of.step("ff.tanh", c))
                else:
                    act.wait_ge(moe_setup_dve, 6)
                    for i in range(3):
                        n = P if i < 2 else TD
                        ins = nact.activation(TW[0:n, i, 0:1], TW[0:n, i, 0:1], ACT.Exp)
                    ins.then_inc(moe_setup_act, 1)
                    R = rounds_of(act)
                    halves_of = lambda x: (x[:, 0:4, :], x[:, 4:8, :])
                    for part in range(2):
                        act.wait_ge(gathered, part + 1)
                        nact.activation(halves_of(XE[:, 0, :, :])[part], mW[:, 3 - part, :], ACT.Copy).then_inc(gather_kept, 1)
                    with act.Fori(0, R * (NE // 2)) as m:
                        for u in range(2):
                            n = 2 * m + u
                            for c in range(FC):
                                if c in (7, 8):
                                    act.wait_ge(gathered, 2 * n + (c - 7 + 3))
                                    nact.activation(halves_of(XE[:, 1 - u, :, :])[c - 7], mW[:, 3 - (c - 7), :], ACT.Copy)\
                                        .then_inc(gather_kept, 1)
                                act.wait_ge(gate_done, n * FC + (c + 1 + FC))
                                if c >= 2:
                                    act.wait_ge(hidden, n * FC + (c - 1))
                                else:
                                    act.wait_ge(hidden, n * FC)
                                nact.activation(ETH[:, c % 2, :], mA[:, 2 * (c % 2), 0:256], ACT.Tanh, scale=0.5)\
                                    .then_inc(tanh_done, 1)
                            act.wait_ge(down_done, n * FC + 2 * FC)
                            nact.activation(YE, WF[:, 0:1024], ACT.Copy).then_inc(down_kept, 1)
                norm(1)


        def moe_vector(dve, v, link, linked):
            MUL, ADD, SUB, MAX, EQ = ALU.mult, ALU.add, ALU.subtract, ALU.max, ALU.is_equal
            v.memset(MASK, 0.0)
            v.memset(GATE, 0.0)
            v.memset(YE, 0.0)
            v.memset(PGT[:, 1, :], 0.0)
            link(v.memset(RANK, -1.0))
            link(v.tensor_scalar(SQ8[:, :, :], X[:, :, :], 2 * ALPHA, None, MUL))
            for i in range(3):
                n = P if i < 2 else TD
                dve.wait_ge(moe_setup_pe, i + 1)
                v.tensor_copy(XT[0:n, i, :], WF[0:n, 1024 * (i % 2):1024 * (i % 2) + 1024]).then_inc(moe_setup_dve, 1)
            dve.wait_ge(moe_setup_pe, 4)
            dve.wait_ge(router_in, 32)
            for i in range(3):
                n = P if i < 2 else TD
                link(v.tensor_tensor(LOG[0:n, i, :], mA[0:n, 0, NE * i:NE * i + NE], rbias[0:n, :], ADD))
                link(v.max(TOP[0:n, i, :], LOG[0:n, i, :]))
                link(v.max_index(TIX[0:n, i, :], TOP[0:n, i, :], LOG[0:n, i, :]))
                v.tensor_copy(IXF[0:n, i, :], TIX[0:n, i, :])
                ins = v.tensor_tensor(TW[0:n, i, 0:1], TOP[0:n, i, 1:2], TOP[0:n, i, 0:1], SUB)
                ins.then_inc(moe_setup_dve, 1)
            dve.wait_ge(moe_setup_act, 1)
            for i in range(3):
                n = P if i < 2 else TD
                link(v.tensor_scalar(TW[0:n, i, 1:2], TW[0:n, i, 0:1], 1.0, None, ADD))
                link(v.reciprocal(TW[0:n, i, 1:2], TW[0:n, i, 1:2]))
                link(v.tensor_tensor(TW[0:n, i, 0:1], TW[0:n, i, 0:1], TW[0:n, i, 1:2], MUL))
                i8 = C("iota8", NE, n)
                v.tensor_scalar(MASK[0:n, i, :], i8, IXF[0:n, i, 0:1], None, EQ)
                v.tensor_scalar(TMPE[0:n, i, :], i8, IXF[0:n, i, 1:2], None, EQ)
                v.tensor_scalar(GATE[0:n, i, 0:NE], i8, IXF[0:n, i, 0:1], TW[0:n, i, 1:2], EQ, MUL)
                link(v.tensor_scalar(LOG[0:n, i, :], i8, IXF[0:n, i, 1:2], TW[0:n, i, 0:1], EQ, MUL))
                v.tensor_tensor(GATE[0:n, i, 0:NE], GATE[0:n, i, 0:NE], LOG[0:n, i, :], ADD)
                v.tensor_tensor(MASK[0:n, i, :], MASK[0:n, i, :], TMPE[0:n, i, :], ADD).then_inc(moe_setup_dve, 1)
            dve.wait_ge(moe_setup_pe, 5)
            for i in range(3):
                n = P if i < 2 else TD
                ins = v.scalar_tensor_tensor(RANK[0:n, i, 0:NE], mA[0:n, 1, NE * i:NE * i + NE], 1.0, MASK[0:n, i, :], ADD, MUL)
            link(ins)
            for k in (1, 2):
                v.tensor_copy(GATE[:, :, NE * k:NE * k + NE], GATE[:, :, 0:NE])
            for i in range(3):
                n = P if i < 2 else TD
                link(v.tensor_scalar(RANK[0:n, i, 0:NE], RANK[0:n, i, 0:NE], -1.0, None, ADD))
            for k in (1, 2):
                v.tensor_scalar(RANK[:, :, NE * k:NE * k + NE], RANK[:, :, 0:NE], -float(P * k), None, ADD)
            link(v.tensor_reduce(CNT[0:1, 0:1], mA[0:1, 1, 3 * NE:4 * NE], AX_X, MAX))
            v.tensor_scalar(CNT[0:1, 1:2], CNT[0:1, 0:1], float(P), 1.0, ALU.is_gt, ADD)
            link(v.tensor_scalar(CNT[0:1, 2:3], CNT[0:1, 0:1], float(2 * P), None, ALU.is_gt))
            link(v.tensor_tensor(CNT[0:1, 1:2], CNT[0:1, 1:2], CNT[0:1, 2:3], ADD))
            v.tensor_copy(count_i[0:1, 0:1], CNT[0:1, 1:2]).then_inc(rounds_known, 1)
            R = rounds_of(dve)

            def place(n):
                dve.wait_ge(gathered, 2 * n)
                for i in range(3):
                    ins = v.tensor_scalar(PL[:, i, :], C("iota"), RANK[:, i, bass.ds(n, 1)], None, EQ)
                ins.then_inc(placed, 1)
                dve.wait_ge(placed, n + 1)
                for i in range(3):
                    ins = v.tensor_scalar(PG[:, i, :], PL[:, i, :], GATE[:, i, bass.ds(n, 1)], None, MUL)
                ins.then_inc(place_ready, 1)

            def turned(n, u):
                dve.wait_ge(placeT_pe, n + 1)
                v.tensor_copy(PGT[:, u, :], mW[:, 2, 0:T]).then_inc(placeT_ready, 1)

            def add(n, i):
                dve.wait_ge(scattered, n * KT + (i + 2))
                v.tensor_tensor(SQ8[:, i:i + 2, :], SQ8[:, i:i + 2, :], mW[:, 2:4, 0:T], ADD).then_inc(scatter_added, 1)

            dve.wait_ge(dve_link, linked[0])
            place(0)
            turned(0, 0)
            with dve.Fori(0, R * (NE // 2)) as m:
                for u in range(2):
                    n = 2 * m + u
                    for c in range(FC):
                        if 2 <= c < 6:
                            add(n, 2 * (c - 2))
                        if c == 5:
                            place(n + 1)
                        if c == 6:
                            dve.wait_ge(scatter_added, n * 4 + 4)
                            turned(n + 1, 1 - u)
                        dve.wait_ge(tanh_done, n * FC + (c + 1))
                        b = 2 * (c % 2)
                        v.scalar_tensor_tensor(ETH[:, c % 2, :], ETH[:, c % 2, :], 1.0, mA[:, b, 0:256], ADD, MUL)\
                            .then_inc(gated, 1)
                        dve.wait_ge(gated, n * FC + (c + 1))
                        dve.wait_ge(up_done, n * FC + (c + 1 + FC))
                        if c >= 2:
                            dve.wait_ge(down_done, n * FC + (c - 1 + FC))
                        else:
                            dve.wait_ge(down_done, n * FC + FC)
                        v.tensor_tensor(HE[:, c % 2, :], ETH[:, c % 2, :], mA[:, b + 1, 0:256], MUL).then_inc(hidden, 1)
            for i in range(0, KT, 2):
                add(R * NE, i)
            dve.wait_ge(scatter_added, R * (NE * 4) + 4)

        @block.vector
        def _(dve):
            v = nc.vector
            linked = [0]

            def link(ins):
                linked[0] += 1
                ins.then_inc(dve_link, 1)
                dve.wait_ge(dve_link, linked[0])

            def done(ins, name, i=0):
                ins.then_inc(*dve_of.step(name, i))
                dve.wait_ge(*dve_of.at(name, layer[0], i))

            layer = [0]
            MUL, ADD, SUB, MAX = ALU.mult, ALU.add, ALU.subtract, ALU.max

            def conv(dst, src, buf, w, b, n):
                for i in range(n):
                    ins = v.tensor_scalar(dst[:, i, :], src[:, i, :], pc(w, 4 * i + 3), pc(b, i), MUL, ADD)
                link(ins)
                for back in range(1, 4):
                    for i in range(n):
                        v.scalar_tensor_tensor(dst[:, i, back:TP], src[:, i, 0:TP - back], pc(w, 4 * i + 3 - back),
                                               dst[:, i, back:TP], MUL, ADD)
                        ins = v.scalar_tensor_tensor(dst[:, i, TP:T], buf[:, i, 3 - back, :], pc(w, 4 * i + 3 - back),
                                                     dst[:, i, TP:T], MUL, ADD)
                    if back < 3:
                        link(ins)
                return ins

            def last_rows(out, buf, src):
                v.tensor_copy(out[:, :, :, 0], src[:, :, TP - 3:TP])
                v.tensor_copy(out[:, :, 0:2, 1:9], buf[:, :, 1:3, :])
                return v.tensor_copy(out[:, :, 2, 1:9], src[:, :, TP:T])

            def over_v(x):
                return x.unsqueeze(3).broadcast_to([P, x.shape[1], TD, 64])

            def unit():
                return C("i64", 64).unsqueeze(1).unsqueeze(1).broadcast_to([P, 2, TD, 64])

            def w4(a, n=2):
                return WF[:, 512 * a:512 * (a + n)].rearrange("p (j b v) -> p j b v", j=n, b=TD)

            dve.wait_ge(const_in, 16)
            for l in range(DEPTH):
                layer[0] = l
                dve.wait_ge(*loads(l, 10))
                done(v.tensor_scalar(half[:, :], par[:, :], 0.5, None, MUL), "u.half")
                if l:
                    dve.wait_ge(*act_of.at("ln.norm", l - 1, 1))
                link(v.memset(LG[:, T:2 * T], 0.0))
                v.tensor_copy(LG[:, 2 * T:2 * T + 2], par[:, PC["lam"]:PC["lam"] + 2])
                dve.wait_ge(*act_of.at("u.tile", l, TMI))
                v.tensor_copy(LG[0:4, T:2 * T], U[32:36, TMI, :])
                dve.wait_ge(*pe_of.at("lg.alpha", l))
                done(v.tensor_scalar(LG[:, 0:T], mW[:, 0, 0:T], pc("gab"), None, ADD), "lg.in")
                dve.wait_ge(*act_of.at("u.tile", l, NU - 1))
                done(conv(RC, U[:, TRX:TRX + 2, :], rbuf, "rcw", "rcb", 2), "rg.conv")
                last_rows(rconv_out, rbuf, U[:, TRX:TRX + 2, :])
                link(v.tensor_copy(shift_out, U[:, 0:7, TP - 1:T]))
                dve.wait_ge(*act_of.at("lg.exp", l))
                link(v.tensor_scalar(LY, LE, 2.0, None, ADD))
                link(v.reciprocal(LY, LY))
                link(v.tensor_tensor(LY, LE, LY, MUL))
                link(v.tensor_tensor(LZ, LY, LY, MUL))
                link(v.tensor_scalar(LE, LZ, 1.0 / 15, None, MUL))
                for k in (13, 11, 9, 7, 5, 3):
                    link(v.scalar_tensor_tensor(LE, LE, 1.0 / k, LZ, ADD, MUL))
                v.tensor_scalar(LG, LG, 0.0, None, ALU.min)
                link(v.scalar_tensor_tensor(LE, LE, 1.0, LY, ADD, MUL))
                link(v.scalar_tensor_tensor(LG, LE, -2.0, LG, MUL, ADD))
                link(v.tensor_scalar(lam4, LG[:, 2 * T:2 * T + 2], 4.0, None, MUL))
                dve.wait_ge(*act_of.at("rg.tanh", l))
                for j in range(2):
                    ins = v.tensor_scalar(RL[:, j, :], RT[:, j, :], 1.0, lam4[:, j:j + 1], ADD, MUL)
                done(ins, "rg.loga")
                v.scalar_tensor_tensor(RT[:, 2:4, :], RT[:, 2:4, :], 1.0, RC, ADD, MUL)
                link(v.tensor_scalar(RX, RX, 0.044715, 1.0, MUL, ADD))
                done(v.tensor_tensor(RX, RX, RGY, MUL), "rg.gelu_in")
                dve.wait_ge(*act_of.at("rg.exp", l))
                done(v.scalar_tensor_tensor(RE, RE, 1.0, RS, ADD, MUL), "rg.var")
                dve.wait_ge(*act_of.at("rg.sqrt", l))
                link(v.scalar_tensor_tensor(RS, RE, 0.5, RT[:, 2:4, :], MUL, MUL))
                for j in range(2):
                    v.tensor_tensor_scan(RH[:, j, 0:TP], RA[:, j, 0:TP], RS[:, j, 0:TP], 0.0, MUL, ADD)
                link(v.tensor_tensor(RH[:, :, TP:T], RA[:, :, TP:T], h0, MUL))
                link(v.tensor_tensor(RH[:, :, TP:T], RH[:, :, TP:T], RS[:, :, TP:T], ADD))
                v.tensor_copy(h_out, RH[:, :, TP - 1:T])
                dve.wait_ge(*act_of.at("rg.gelu", l))
                link(v.scalar_tensor_tensor(RX, RX, 1.0, RGY, ADD, MUL))
                done(v.scalar_tensor_tensor(RGY, RH, 0.5, RX, MUL, MUL), "rg.out")
                done(conv(CV, U[:, TMQ:TMQ + 4, :], mbuf, "mcw", "mcb", 4), "ml.conv")
                last_rows(mconv_out, mbuf, U[:, TMQ:TMQ + 4, :])
                f, ip = LG[0:4, T:2 * T], U[0:4, TMI, :]

                def row(k, lo=0, hi=TP):
                    return MR[0:4, k * T + lo:k * T + hi]

                v.tensor_tensor_scan(row(0), C("ones", TP, 4), f[:, 0:TP], 0.0, MUL, ADD)
                v.tensor_tensor_scan(row(1), f[:, 0:TP], ip[:, 0:TP], 0.0, ADD, MAX)
                link(v.tensor_tensor(row(5, 0, TD), f[:, TP:T], m0, ADD))
                link(v.tensor_tensor(row(1, TP, T), row(5, 0, TD), ip[:, TP:T], MAX))
                v.tensor_tensor(row(5, 0, TD), row(5, 0, TD), row(1, TP, T), SUB)
                v.tensor_tensor(row(5, TD, 2 * TD), ip[:, TP:T], row(1, TP, T), SUB)
                v.tensor_tensor(row(2), ip[:, 0:TP], row(0), SUB)
                v.tensor_tensor(row(3), row(0), row(1), SUB)
                done(v.tensor_copy(m_out, row(1, TP - 1, T)), "ml.rows")
                dve.wait_ge(*act_of.at("ml.silu", l))
                link(v.scalar_tensor_tensor(CV, TQ, 1.0, CV, ADD, MUL))
                v.tensor_scalar(CV[:, 0:2, :], CV[:, 0:2, :], 0.5, None, MUL)
                done(v.tensor_scalar(CV[:, 2:4, :], CV[:, 2:4, :], 0.5 * 64 ** -0.5, None, MUL), "ml.qk")
                dve.wait_ge(*act_of.at("ml.exps", l))
                done(v.tensor_copy(row(5, 2 * TD, 3 * TD), row(4, TP, T)), "ml.dec_rows")
                dve.wait_ge(*pe_of.at("ml.turn", l))
                v.tensor_copy(MVT, mW[:, 0, :].rearrange("p (a b) -> p a b", a=2))
                v.tensor_copy(MKT, mW[:, 1, :].rearrange("p (a b) -> p a b", a=2))
                v.tensor_copy(MG, mW[:, 2, 0:8].rearrange("p (a b) -> p a b", a=2))
                done(v.tensor_copy(MDC, mW[:, 3, 0:48].rearrange("p (a b c) -> p a b c", a=2, b=3)), "ml.gcol")
                for h in range(4):
                    dve.wait_ge(*pe_of.at("ml.qk", l, h))
                    dve.wait_ge(*act_of.at("ml.d", l, h))
                    v.tensor_tensor(MSD[:, h, :], mW[:, 2 + h % 2, 0:384], MD[:, h % 2, :], MUL)\
                        .then_inc(*dve_of.step("ml.sd", h))
                    v.tensor_scalar(MKT[:, 0, 64 * h:64 * h + 64], MKT[:, 0, 64 * h:64 * h + 64], MD[:, h % 2, 255:256], None, MUL)
                    done(v.tensor_scalar(MKT[:, 1, 64 * h:64 * h + 64], MKT[:, 1, 64 * h:64 * h + 64],
                                         MD[:, h % 2, 383:384], None, MUL), "ml.kw", h)
                dve.wait_ge(*pe_of.at("ml.emb", l))
                link(v.tensor_tensor(MDEN[:, :, 0:TP], MDEN[:, :, 0:TP], mW[:, 2:4, 0:TP], MAX))
                link(v.reciprocal(MDEN[:, :, 0:TP], MDEN[:, :, 0:TP]))
                done(v.tensor_tensor(OO[:, 2:4, 0:TP], mW[:, 0:2, 0:TP], MDEN[:, :, 0:TP], MUL), "ml.h")
                dve.wait_ge(*pe_of.at("ml.c", l))
                v.tensor_copy(n_out[:, :, 0], mW[:, 0, 0:256].rearrange("p (j v) -> p j v", j=2)[:, :, 64])
                done(v.tensor_copy(MCO, mW[:, 0, 0:256].rearrange("p (j v) -> p j v", j=2)[:, :, 0:64]), "ml.cout")
                qd, kd, vd = CV[:, 0:2, TP:T], CV[:, 2:4, TP:T], U[:, TMV:TMV + 2, TP:T]
                done(v.tensor_tensor(MX, unit(), over_v(vd), MUL), "ml.dv")
                link(v.tensor_tensor(MDEN[:, :, 0:TD], kd, MDC[:, :, 1, :], MUL))
                link(v.tensor_tensor(n_out[:, :, 1:9], n0, MDC[:, :, 0, :], MUL))
                link(v.tensor_tensor(n_out[:, :, 1:9], n_out[:, :, 1:9], MDEN[:, :, 0:TD], ADD))
                link(v.tensor_tensor(MDEN[:, :, TD:2 * TD], n_out[:, :, 1:9], qd, MUL))
                dve.wait_ge(*loads(l, 11))
                link(v.tensor_tensor(MS, MS, over_v(MDC[:, :, 0, :]), MUL))
                dve.wait_ge(*pe_of.at("ml.dvb", l))
                link(v.tensor_tensor(MX, w4(0), over_v(MDEN[:, :, 0:TD]), MUL))
                link(v.tensor_tensor(MS, MS, MX, ADD))
                done(v.tensor_tensor(MX, MS, over_v(qd), MUL), "ml.dq")
                dve.wait_ge(*pe_of.at("ml.dnum", l))
                link(v.tensor_tensor(MX, w4(0), unit(), MUL))
                v.tensor_reduce(MDEN[:, :, 2 * TD:3 * TD], MX, AX_X, ADD)
                den = MDEN[:, :, 3 * TD:4 * TD]
                link(v.tensor_copy(den, mW[:, 2, 0:16].rearrange("p (j b) -> p j b", j=2)))
                link(v.scalar_tensor_tensor(den, den, -1.0, den, MUL, MAX))
                link(v.tensor_tensor(den, den, MDC[:, :, 2, :], MAX))
                link(v.reciprocal(den, den))
                done(v.tensor_tensor(OO[:, 2:4, TP:T], MDEN[:, :, 2 * TD:3 * TD], den, MUL), "ml.out")
                la = LG[:, 0:T]

                def chunks4(x):
                    return x.rearrange("p (c t) -> p c t", c=NC)

                def at_chunk(x, t):
                    return chunks4(x)[:, :, t:t + 1].broadcast_to([P, NC, CH])

                dve.wait_ge(*act_of.at("gl.og", l))
                link(v.scalar_tensor_tensor(GGS, GTH, 1.0, GGS, ADD, MUL))
                v.tensor_scalar(GGS, GGS, 0.5, None, MUL)
                v.tensor_scalar(MOG, MOG, 0.5, 0.5, MUL, ADD)
                link(v.tensor_scalar(la, la, 1.0 / 16, None, MUL))
                dve.wait_ge(state_out, 16 * (12 * l + 8))
                link(v.tensor_tensor_scan(GB, C("reset", TP), la[:, 0:TP], 0.0, MUL, ADD))
                link(v.tensor_tensor(chunks4(GX[:, 0, :]), chunks4(GB), at_chunk(GB, CH // 2 - 1), SUB))
                v.tensor_scalar(GX[:, 1, :], GX[:, 0, :], -1.0, None, MUL)
                v.tensor_copy(GX[:, 2, :], GB)
                done(v.tensor_tensor(chunks4(GX[:, 3, :]), at_chunk(GB, CH - 1), chunks4(GB), SUB), "gl.cum")
                dve.wait_ge(*act_of.at("gl.exp", l))
                q, k = U[:, TGQ, :], U[:, TGK, :]
                v.scalar_tensor_tensor(GQ, q[:, 0:TP], 32 ** -0.5, GX[:, 0, :], MUL, MUL)
                v.tensor_tensor(GK, k[:, 0:TP], GX[:, 1, :], MUL)
                v.scalar_tensor_tensor(GQH, q[:, 0:TP], 32 ** -0.5, GX[:, 2, :], MUL, MUL)
                done(v.tensor_tensor(GKH, k[:, 0:TP], GX[:, 3, :], MUL), "gl.ops")
                dve.wait_ge(*pe_of.at("gl.turn", l))
                v.tensor_copy(GVT, mW[:, 0, :].rearrange("p (a b) -> p a b", a=2))
                done(v.tensor_copy(GKT, mW[:, 1, 0:256].rearrange("p (a b) -> p a b", a=2)), "gl.turned")
                dve.wait_ge(*pe_of.at("gl.attn", l))
                for c2 in range(2):
                    ins = v.tensor_tensor(GAT[:, c2, :].rearrange("p (h t) -> p h t", h=4),
                                          mW[:, :, P * c2:P * c2 + P],
                                          mid(con[:, CC["mk"] + P:CC["mk"] + 2 * P], 4), MUL)
                done(ins, "gl.attn")
                dve.wait_ge(*pe_of.at("gl.kv", l))
                v.memset(GSS[:, 0, :], 0.0)
                for e in range(2):
                    ins = v.tensor_tensor(GKV[:, e::2, :], mW[:, e, :].rearrange("p (c n) -> p c n", c=2), mid(C("gm", 256), 2), MUL)
                link(ins)
                for c in range(NC):
                    ins = v.scalar_tensor_tensor(GSS[:, c + 1, :], GSS[:, c, :], GX[:, 2, CH * c + CH - 1:CH * c + CH],
                                                 GKV[:, c, :], MUL, ADD)
                    if c < NC - 1:
                        link(ins)
                done(ins, "gl.state")
                done(v.tensor_tensor(GXX, unit(), over_v(U[:, TGV:TGV + 2, TP:T]), MUL), "gl.dv")
                dve.wait_ge(*pe_of.at("gl.y", l))
                done(v.tensor_copy(OO[:, 4:6, 0:TP], mW[:, 2:4, 0:TP]), "gl.y")

                def over_gv(x):
                    return x.unsqueeze(2).broadcast_to([P, TD, 64])

                dve.wait_ge(*loads(l, 12))
                link(v.tensor_tensor(GS, GS, over_gv(GDX), MUL))
                dve.wait_ge(*pe_of.at("gl.dvb", l))
                g3 = mW[:, 0, :].rearrange("p (b v) -> p b v", b=TD)
                link(v.tensor_tensor(GXX[:, 0, :, :], g3, over_gv(k[:, TP:T]), MUL))
                done(v.tensor_tensor(GS, GS, GXX[:, 0, :, :], ADD), "gl.dec")
                link(v.tensor_tensor(GXX[:, 0, :, :], GS, over_gv(q[:, TP:T]), MUL))
                done(v.tensor_scalar(GXX[:, 0, :, :], GXX[:, 0, :, :], 32 ** -0.5, None, MUL), "gl.dq")
                dve.wait_ge(*pe_of.at("gl.dy", l))
                link(v.tensor_tensor(GXX, w4(0), unit(), MUL))
                done(v.tensor_reduce(OO[:, 4:6, TP:T], GXX, AX_X, ADD), "gl.out")
                um = U[:, 0:7, :]
                dve.wait_ge(state_out, 16 * (12 * l + 10))
                v.tensor_tensor(DL[:, :, 1:TP], um[:, :, 0:TP - 1], um[:, :, 1:TP], SUB)
                v.tensor_scalar(DL[:, :, 0:1], um[:, :, 0:1], -1.0, None, MUL)
                link(v.tensor_tensor(DL[:, :, TP:T], shift_in, um[:, :, TP:T], SUB))
                for i in range(7):
                    ins = v.scalar_tensor_tensor(um[:, i, :], DL[:, i, :], pc("mu", i), um[:, i, :], MUL, ADD)
                done(ins, "rw.mixed")
                rr, kx, vv = U[:, TR:TR + 2, :], U[:, TK:TK + 2, :], U[:, TV:TV + 2, :]
                dve.wait_ge(*act_of.at("rw.lora", l))
                done(v.tensor_scalar(TH[64:128, :], TH[64:128, :], 0.5, 0.5, MUL, ADD), "rw.sg")
                dve.wait_ge(*act_of.at("rw.wa", l))
                v.tensor_scalar(LW, LW, 1.0, -0.5 * float(np.exp(-0.5)), ADD, MUL)
                link(v.tensor_scalar(AA, AA, 0.5, 0.5, MUL, ADD))
                for j in range(2):
                    ins = v.tensor_scalar(K4[:, j, :], AA[:, j, :], -1.0, pc("ka", j), ADD, MUL)
                link(ins)
                link(v.scalar_tensor_tensor(K4, K4, 1.0, kx, ADD, MUL))
                for j in range(2):
                    ins = v.scalar_tensor_tensor(RKV[:, j, :], rr[:, j, :], pc("rk", j), K4[:, j, :], MUL, MUL)
                done(ins, "rw.rk")
                dve.wait_ge(*pe_of.at("rw.ksum", l))
                done(v.tensor_scalar(NRM, mW[:, 2:4, 0:T], 1e-24, None, MAX), "rw.ksum")
                dve.wait_ge(*act_of.at("rw.ksqrt", l))
                link(v.reciprocal(NRM, NRM))
                for j in range(2):
                    ins = v.scalar_tensor_tensor(KKN[:, j, :], kx[:, j, :], pc("kk", j), NRM[:, j, :], MUL, MUL)
                link(ins)
                dve.wait_ge(*pe_of.at("rw.bonus", l))
                done(v.tensor_tensor(kx, mW[:, 0:2, 0:T], vv, MUL), "rw.bonus")
                for j in range(2):
                    ins = v.tensor_tensor_scan(RKV[:, j, 0:TP], C("reset", TP), LW[:, j, 0:TP], 0.0, MUL, ADD)
                link(ins)
                done(v.tensor_tensor(BT, RKV[:, :, 0:TP], LW[:, :, 0:TP], SUB), "rw.cum")
                v.tensor_tensor(DKA, KKN[:, :, TP:T], AA[:, :, TP:T], MUL)
                link(v.tensor_tensor(DY, unit(), over_v(vv[:, :, TP:T]), MUL))
                dve.wait_ge(*loads(l, 13))
                done(v.tensor_tensor(DX, DS, over_v(KKN[:, :, TP:T]), MUL), "rw.dx")
                dve.wait_ge(*act_of.at("rw.exp", l))
                link(v.tensor_tensor(DS, DS, over_v(DW), MUL))
                dve.wait_ge(*pe_of.at("rw.dsa", l))
                link(v.tensor_tensor(DX, w4(0), over_v(DKA), MUL))
                link(v.tensor_tensor(DS, DS, DX, SUB))
                link(v.tensor_tensor(DX, w4(2), over_v(K4[:, :, TP:T]), MUL))
                done(v.tensor_tensor(DS, DS, DX, ADD), "rw.dec")
                done(v.tensor_tensor(DX, DS, over_v(rr[:, :, TP:T]), MUL), "rw.dr")
                dve.wait_ge(*pe_of.at("rw.dy", l))
                link(v.tensor_tensor(DX, w4(0), unit(), MUL))
                done(v.tensor_reduce(OO[:, 0:2, TP:T], DX, AX_X, ADD), "rw.dout")

                def halves(x):
                    return x[:, :, 0:TP].rearrange("p j (c t) -> p j c t", c=2)

                e_in, e_neg, e_ex = EXPS[:, 0, :, :], EXPS[:, 1, :, :], EXPS[:, 2, :, :]
                v.tensor_tensor(AR[:, :, :, 0, :], halves(KKN), halves(e_ex), MUL)
                v.tensor_tensor(AR[:, :, :, 1, :], halves(rr), halves(e_in), MUL)
                v.tensor_tensor(KTL, K4[:, :, 0:TP], e_neg, MUL)
                v.tensor_copy(PLAST, e_in.rearrange("p j (c t) -> p j c t", c=NC)[:, :, :, CH - 1])
                link(v.tensor_tensor(NRM[:, :, 0:TP], KKN[:, :, 0:TP], AA[:, :, 0:TP], MUL))
                link(v.tensor_tensor(BT, NRM[:, :, 0:TP], e_neg, MUL))
                for j in range(2):
                    plast = PLAST[:, j, :].unsqueeze(2).broadcast_to([P, NC, CH])
                    v.scalar_tensor_tensor(chunks4(B2[:, j, :]), chunks4(BT[:, j, :]), -1.0, plast, MUL, MUL)
                    ins = v.tensor_tensor(chunks4(K2[:, j, :]), chunks4(KTL[:, j, :]), plast, MUL)
                done(ins, "rw.ops")
                dve.wait_ge(*pe_of.at("rw.turn", l))
                dve.wait_ge(state_out, 16 * (12 * l + 11))
                for i, dst in enumerate((ATK, BTK, KTK, VTK)):
                    v.tensor_copy(dst, mW[:, i, :].rearrange("p (a b) -> p a b", a=2))
                done(v.memset(SS[:, :, 0, :], 0.0), "rw.turned")
                for g in range(2):
                    dve.wait_ge(*pe_of.at("rw.bk", l, g))
                    if g:
                        dve.wait_ge(*pe_of.at("rw.y", l, 0))
                    v.tensor_tensor(NB, WF[:, 0:1024].rearrange("p (h t) -> p h t", h=4), mid(C("mb", 256), 4), MUL)
                    done(v.tensor_tensor(MKS, WF[:, 1024:2048].rearrange("p (h t) -> p h t", h=4), mid(C("mk", 256), 4), MUL),
                         "rw.bk", g)
                    dve.wait_ge(*pe_of.at("rw.l", l, g))
                    for e in range(2):
                        m2 = mW[:, e, 0:256].rearrange("p (h t) -> p h t", h=2)
                        v.tensor_tensor(ND[:, 2 * e:2 * e + 2, :], m2, mid(C("ml16"), 2), MUL)
                        v.tensor_tensor(NO[:, 2 * e:2 * e + 2, :], m2, mid(C("mlo"), 2), MUL)
                    v.tensor_tensor(QT, NB[:, :, 0:P], mid(C("ident"), 4), ADD)
                    v.tensor_copy(VW[:, 0, :], ATK[:, g, :])
                    done(v.tensor_copy(VW[:, 1, :], mW[:, 2, 0:256]), "rw.l", g)
                    b2 = mW[:, 2, :].rearrange("p (h t) -> p h t", h=4)
                    for k in range(3):
                        dve.wait_ge(*pe_of.at(("rw.p4", "rw.p8", "rw.q")[k], l, g))
                        done(v.tensor_tensor(QT, QT, b2, ADD), f"rw.q{k}", g)
                    b1 = mW[:, 1, :].rearrange("p (a n) -> p a n", a=2)
                    b3 = mW[:, 3, :].rearrange("p (a n) -> p a n", a=2)
                    dve.wait_ge(*pe_of.at("rw.et", l, g))
                    done(v.tensor_copy(VW, b1), "rw.v0", g)
                    for k in range(3):
                        dve.wait_ge(*pe_of.at("rw.e", l, 3 * g + k))
                        done(v.tensor_tensor(YW, (b3, b1, b3)[k], VW, ADD), "rw.e", 3 * g + k)
                    for c in (2 * g, 2 * g + 1):
                        q0 = 64 * (c % 2)
                        dve.wait_ge(*pe_of.at("rw.z", l, c))
                        done(v.tensor_tensor(ZZ[q0:q0 + 64, g, :].rearrange("p (j e d) -> p e j d", e=2, j=2),
                                             mW[q0:q0 + 64, 1:4:2, 0:128].rearrange("p e (j d) -> p e j d", j=2),
                                             YW[q0:q0 + 64, 1, :].rearrange("p (j e d) -> p e j d", e=2, j=2), ADD),
                             "rw.z", c)
                        dve.wait_ge(*pe_of.at("rw.s", l, c))
                        for j in range(2):
                            ins = v.scalar_tensor_tensor(SS[:, j, c + 1, :], SS[:, j, c, :], PLAST[:, j, c:c + 1],
                                                         mW[:, 0, 64 * j:64 * j + 64], MUL, ADD)
                        done(ins, "rw.state", c)
                    dve.wait_ge(*pe_of.at("rw.y", l, g))
                    done(v.tensor_copy(OO[:, 0:2, P * g:P * g + P], mW[:, 2, 0:256].rearrange("p (j t) -> p j t", j=2)),
                         "rw.y", g)
                dve.wait_ge(*pe_of.at("hn.mean", l))
                done(v.tensor_tensor(OO[:, 0:4, :], OO[:, 0:4, :], mW[:, :, 0:T], SUB), "hn.centred")
                dve.wait_ge(*pe_of.at("hn.var", l, 0))
                v.tensor_scalar(OT[:, 0:2, :], mW[:, 0:2, 0:T], 64e-5, None, ADD)
                done(v.tensor_scalar(OT[:, 2:4, :], mW[:, 2:4, 0:T], 1e-6, None, ADD), "hn.var4")
                dve.wait_ge(*pe_of.at("hn.var", l, 1))
                done(v.tensor_scalar(OT[:, 4:6, :], mW[:, 0:2, 0:T], 1e-6, None, ADD), "hn.var")
                dve.wait_ge(*act_of.at("hn.sqrt", l))
                link(v.reciprocal(OT, OT))
                link(v.tensor_tensor(OO, OO, OT, MUL))
                for j in range(2):
                    v.tensor_scalar(OO[:, j, :], OO[:, j, :], pc("lnw", j), pc("lnb", j), MUL, ADD)
                    ins = v.scalar_tensor_tensor(U[:, 4 + j, :], OO[:, 4 + j, :], pc("gnw", j), GGS[:, j, :], MUL, MUL)
                link(ins)
                link(v.tensor_tensor(OO[:, 0:2, :], OO[:, 0:2, :], kx, ADD))
                v.tensor_tensor(U[:, 0:2, :], OO[:, 0:2, :], GG, MUL)
                for j in range(2):
                    ins = v.scalar_tensor_tensor(U[:, 2 + j, :], OO[:, 2 + j, :], pc("mnw", j), MOG[:, j, :], MUL, MUL)
                done(ins, "br.ready")
                for i in range(NG):
                    d, g = divmod(i, 4)
                    dve.wait_ge(*pe_of.at("mg.up", l, i))
                    dve.wait_ge(*act_of.at("gate.tile", l, i))
                    if g == 0:
                        done(v.scalar_tensor_tensor(V8[:, d, :], GT[:, i % GR, :], 1.0, acc("up", l, i), ADD, MUL), "mg.up", i)
                    else:
                        done(v.scalar_tensor_tensor(SQ8[:, i % 2, :], GT[:, i % GR, :], 1.0, acc("up", l, i), ADD, MUL), "mg.up", i)
                        ins = v.tensor_tensor(V8[:, d, :], V8[:, d, :], SQ8[:, i % 2, :], ADD)
                        if g < 3:
                            link(ins)
                        else:
                            done(ins, "mg.sum", d)
                for i in range(KT):
                    dve.wait_ge(*pe_of.at("mg.out", l, i))
                    done(v.scalar_tensor_tensor(SQ8[:, i, :], X[:, i, :], 2 * ALPHA, acc("out", l, i), MUL, ADD), "mg.out", i)

                def norm(i):
                    dve.wait_ge(*pe_of.at("ln.mean", l, i))
                    done(v.tensor_tensor(SQ8[:, :, :], SQ8[:, :, :], mid(mW[:, 0, 0:T], KT), SUB), "ln.centred", i)
                    dve.wait_ge(*pe_of.at("ln.var", l, i))
                    done(v.tensor_scalar(V8[:, 0, :], mW[:, 1, 0:T], 4 * LN_EPS, None, ADD), "ln.var", i)
                    dve.wait_ge(*act_of.at("ln.sqrt", l, i))
                    link(v.reciprocal(V8[:, 1, :], V8[:, 1, :]))
                    done(v.tensor_tensor(SQ8[:, :, :], SQ8[:, :, :], mid(V8[:, 1, :], KT), MUL), "ln.scaled", i)
                    dve.wait_ge(*act_of.at("ln.norm", l, i))

                norm(0)
                if l == 0:
                    for c in range(FC):
                        dve.wait_ge(*act_of.at("ff.tanh", l, c))
                        for q in range(2):
                            ins = v.scalar_tensor_tensor(FTH[:, c % 2, q, :], FTH[:, c % 2, q, :], 1.0,
                                                         acc("f", l, 4 * c + q), ADD, MUL)
                        link(ins)
                        for q in range(2):
                            ins = v.tensor_tensor(HS[:, 2 * c + q, :], FTH[:, c % 2, q, :], acc("f", l, 4 * c + 2 + q), MUL)
                        done(ins, "ff.hid", c)
                    for i in range(KT):
                        dve.wait_ge(*pe_of.at("ff.down", l, i))
                        done(v.scalar_tensor_tensor(SQ8[:, i, :], X[:, i, :], 2 * ALPHA, acc("d", l, i), MUL, ADD),
                             "ff.down", i)
                else:
                    moe_vector(dve, v, link, linked)
                norm(1)


        def moe_tensor(pe, mm, turn):
            for i in range(3):
                n = P if i < 2 else TD
                if i == 2:
                    pe.wait_ge(moe_setup_dve, 1)
                for k in range(KT):
                    ins = nc.tensor.transpose(WF[0:n, 1024 * (i % 2) + P * k:1024 * (i % 2) + P * k + P],
                                              X[:, k, P * i:P * i + n], C("ident"))
                ins.then_inc(moe_setup_pe, 1)
            pe.wait_ge(router_in, 32)
            for i in range(3):
                n = P if i < 2 else TD
                for k in range(KT):
                    ins = mm(mA[0:n, 0, NE * i:NE * i + NE], X[:, k, P * i:P * i + n], router[:, k, :], k == 0, k == KT - 1)
            ins.then_inc(moe_setup_pe, 1)
            pe.wait_ge(moe_setup_dve, 9)
            ones = C("ones", P)
            for i in range(4):
                m = (P, P, TD, P)[i]
                for k in range(min(i + 1, 3)):
                    n = P if k < 2 else TD
                    w = C("tri", m, n) if k == i else con[0:n, CC["ones"]:CC["ones"] + m]
                    ins = mm(mA[0:m, 1, NE * i:NE * i + NE], w, MASK[0:n, k, :], k == 0, k == min(i, 2))
            ins.then_inc(moe_setup_pe, 1)
            R = rounds_of(pe)

            def turn_placement(n):
                pe.wait_ge(place_ready, n + 1)
                for i in range(3):
                    m = P if i < 2 else TD
                    ins = nc.tensor.transpose(mW[:, 2, P * i:P * i + m], PG[0:m, i, :], C("ident", m, m))
                ins.then_inc(placeT_pe, 1)

            def gather(n, part):
                if part:
                    pe.wait_ge(placeT_ready, n + 1)
                for k in range(4):
                    for i in range(3):
                        m = P if i < 2 else TD
                        f = P * (4 * part + k)
                        ins = mm(mW[:, 3 - part, P * k:P * k + P], XT[0:m, i, f:f + P], PL[0:m, i, :], i == 0, i == 2)
                ins.then_inc(gathered, 1)

            def scatter(n, i, placed):
                pe.wait_ge(scatter_added, n * 4 + i // 2)
                for q in range(2):
                    mm(mW[:, 2 + q, 0:T], YE[:, P * (i + q):P * (i + q) + P], placed).then_inc(scattered, 1)

            turn_placement(0)
            gather(0, 0)
            gather(0, 1)
            with pe.Fori(0, R * (NE // 2)) as m:

                def slot(i):
                    k = i % SLOTS
                    pe.wait_ge(slot_in[k], (m * per_pair[k] + (uses0[k] + i // SLOTS + 1)) * 16)
                    return ring[:, k, :]

                for u in range(2):
                    n = 2 * m + u

                    def down(c):
                        pe.wait_ge(hidden, n * FC + (c + 1))
                        if c == 0:
                            pe.wait_ge(down_kept, n)
                        wt = slot(3 * FC * u + 3 * c + 2)
                        for q in range(2):
                            for b in range(2):
                                ins = mm(mW[:, b, :], HE[:, c % 2, P * q:P * q + P], wt[:, D * q + 512 * b:D * q + 512 * b + 512],
                                         c == 0 and q == 0, c == FC - 1 and q == 1)
                        ins.then_inc(down_done, 1)

                    for c in range(FC):
                        if c == 0:
                            pe.wait_ge(gather_kept, 2 * n + 2)
                        if 2 <= c < 6:
                            pe.wait_ge(down_kept, n)
                            scatter(n, 2 * (c - 2), PGT[:, 1 - u, :])
                        if c == 6:
                            pe.wait_ge(scatter_added, n * 4 + 4)
                            turn_placement(n + 1)
                        if c in (7, 8):
                            gather(n + 1, c - 7)
                        b = 2 * (c % 2)
                        pe.wait_ge(hidden, n * FC + (c - 1 if c >= 2 else 0))
                        for part in range(2):
                            wt = slot(3 * FC * u + 3 * c + part).rearrange("p (k n) -> p k n", k=KT)
                            for q in range(2):
                                for k in range(KT):
                                    ins = mm(mA[:, b + part, P * q:P * q + P], wt[:, k, P * q:P * q + P], XE[:, u, k, :],
                                             k == 0, k == KT - 1)
                            ins.then_inc((gate_done, up_done)[part], 1)
                        if c:
                            down(c - 1)
                    down(FC - 1)
            pe.wait_ge(down_kept, R * NE)
            for i in range(0, KT, 2):
                scatter(R * NE, i, PGT[:, 1, :])
            pe.wait_ge(scatter_added, R * (NE * 4) + 4)

        @block.tensor
        def _(pe):
            ck = [0]

            def mm(out, w, x, start=True, stop=True):
                return nc.tensor.matmul(out, w, x, start=start, stop=stop, skip_group_check=True)

            def turn(out, x, n=P):
                return nc.tensor.transpose(out, x, C("ident", n, n))

            def chunk():
                i = ck[0]
                ck[0] += 1
                pe.wait_ge(slot_in[i % SLOTS], 16 * (i // SLOTS + 1))
                return ring[:, i % SLOTS, :].rearrange("p (k n) -> p k n", k=KT)

            def free(n):
                if n >= 4:
                    pe.wait_ge(*emptied[n - 4])

            def tile(kind, l, i, w, x):
                free(acc_no(kind, l, i))
                for k, (wk, xk) in enumerate(zip(w, x)):
                    ins = mm(acc(kind, l, i), wk, xk, k == 0, k == len(w) - 1)
                return ins

            def pair(kind, name, l, i0, x, rows=KT):
                wt = chunk()
                for q in range(2):
                    tile(kind, l, i0 + q, [wt[:, k, P * q:P * q + P] for k in range(rows)], x)\
                        .then_inc(*pe_of.step(name, i0 + q))

            bo = C("bo")
            pe.wait_ge(const_in, 16)
            pe.wait_ge(x_in, 16)
            for l in range(DEPTH):
                xs = [X[:, k, :] for k in range(KT)]
                if l:
                    pe.wait_ge(*act_of.at("ln.norm", l - 1, 1))
                for p in range(NU // 2):
                    pair("u", "u.tile", l, 2 * p, xs)

                def gates(lo, hi):
                    for i in range(lo, hi, 2):
                        pair("gate", "gate.tile", l, i, xs)

                pe.wait_ge(*loads(l, 10))
                pe.wait_ge(*act_of.at("u.tile", l, TMI))
                mm(mW[:, 0, 0:T], alup[64:80, :], U[64:80, TMI, :]).then_inc(*pe_of.step("lg.alpha"))
                gates(0, 2)
                pe.wait_ge(*dve_of.at("rg.conv", l))
                pe.wait_ge(*dve_of.at("lg.in", l))
                for j in range(4):
                    ins = mm(mW[:, j, 0:T], rgw[:, j, :], RC[:, j % 2, :])
                ins.then_inc(*pe_of.step("rg.gates"))
                gates(2, 4)
                pe.wait_ge(*dve_of.at("ml.qk", l))
                pe.wait_ge(*act_of.at("rg.tanh", l))
                for j in range(2):
                    for c in range(2):
                        turn(mW[:, 0, 256 * c + P * j:256 * c + P * j + P], U[:, TMV + j, P * c:P * c + P])
                        turn(mW[:, 1, 256 * c + P * j:256 * c + P * j + P], CV[:, 2 + j, P * c:P * c + P])
                pe.wait_ge(*dve_of.at("ml.rows", l))
                pe.wait_ge(*act_of.at("ml.exps", l))
                for c in range(2):
                    turn(mW[:, 2, 4 * c:4 * c + 4], MR[0:4, 2 * T + P * c:2 * T + P * c + P], 4)
                pe.wait_ge(*dve_of.at("ml.dec_rows", l))

                def spread(bank, at, width, x):
                    for h in range(4):
                        j, p0 = h // 2, 64 * (h % 2)
                        one = con[0:4, CC["ident"] + h:CC["ident"] + h + 1].broadcast_to([4, 64])
                        ins = mm(mW[p0:p0 + 64, bank(j), at(j):at(j) + width], one, x)
                    return ins

                ins = spread(lambda j: 3, lambda j: 24 * j, 24, MR[0:4, 5 * T:5 * T + 24])
                ins.then_inc(*pe_of.step("ml.turn"))
                pe.wait_ge(*dve_of.at("ml.gcol", l))
                qq, kk = CV[:, 0:2, :], CV[:, 2:4, :]
                for h in range(4):
                    j, p0, b = h // 2, 64 * (h % 2), h % 2
                    if h >= 2:
                        pe.wait_ge(*act_of.at("ml.d", l, h - 2))
                    one = con[0:4, CC["ident"] + h:CC["ident"] + h + 1].broadcast_to([4, P])
                    mm(mW[:, b, 0:256], one, MR[0:4, 3 * T:3 * T + TP], True, False)
                    mm(mW[:, b, 0:128], C("ident"), C("neg"), False, True)
                    mm(mW[:, b, 256:384], one, MR[0:4, 3 * T + P:3 * T + TP], True, False)
                    mm(mW[:, b, 256:384], C("ident"), C("neg"), False, True).then_inc(*pe_of.step("ml.logd", h))
                    if h >= 2:
                        pe.wait_ge(*dve_of.at("ml.sd", l, h - 2))
                    mm(mW[:, 2 + b, 0:256], kk[p0:p0 + 64, j, 0:P], qq[p0:p0 + 64, j, 0:TP])
                    mm(mW[:, 2 + b, 256:384], kk[p0:p0 + 64, j, P:TP], qq[p0:p0 + 64, j, P:TP])\
                        .then_inc(*pe_of.step("ml.qk", h))
                gates(4, 6)
                pe.wait_ge(*dve_of.at("ml.kw", l, 3))
                for h in range(4):
                    j, p0 = h // 2, 64 * (h % 2)
                    for b, lhs in ((j, None), (2 + j, C("ones", 64))):
                        for c in range(2):
                            w = MVT[:, c, 64 * h:64 * h + 64] if lhs is None else lhs
                            ins = mm(mW[p0:p0 + 64, b, P * c:TP], w, MSD[:, h, 256 * c:256 + P * c], c == 0, c == 1)
                ins.then_inc(*pe_of.step("ml.num"))
                pe.wait_ge(*act_of.at("ml.abs", l))
                ins = spread(lambda j: 2 + j, lambda j: 0, TP, MR[0:4, 4 * T:4 * T + TP])
                ins.then_inc(*pe_of.step("ml.emb"))
                gates(6, 8)
                pe.wait_ge(*dve_of.at("ml.h", l))
                for h in range(4):
                    j, p0 = h // 2, 64 * (h % 2)
                    for c in range(2):
                        mm(mW[p0:p0 + 64, 0, P * j:P * j + 64], MKT[:, c, 64 * h:64 * h + 64], MVT[:, c, 64 * h:64 * h + 64],
                           c == 0, c == 1)
                    for c in range(2):
                        ins = mm(mW[p0:p0 + 64, 0, P * j + 64:P * j + 65], MKT[:, c, 64 * h:64 * h + 64], C("ones", 1),
                                 c == 0, c == 1)
                ins.then_inc(*pe_of.step("ml.c"))
                pe.wait_ge(*dve_of.at("ml.cout", l))
                pe.wait_ge(*dve_of.at("ml.dv", l))
                for j in range(2):
                    ins = mm(mW[:, j, :], bo, MX[:, j, :, :].rearrange("p b v -> p (b v)"))
                ins.then_inc(*pe_of.step("ml.dvb"))
                pe.wait_ge(*dve_of.at("ml.dq", l))
                for j in range(2):
                    mm(mW[:, j, :], bo, MX[:, j, :, :].rearrange("p b v -> p (b v)"))
                for j in range(2):
                    ins = mm(mW[:, 2, 8 * j:8 * j + 8], bo, MDEN[:, j, TD:2 * TD])
                ins.then_inc(*pe_of.step("ml.dnum"))
                pe.wait_ge(*dve_of.at("gl.ops", l))
                for c in range(2):
                    for j in range(2):
                        turn(mW[:, 0, 256 * c + P * j:256 * c + P * j + P], U[:, TGV + j, P * c:P * c + P])
                    ins = turn(mW[:, 1, P * c:P * c + P], GKH[:, P * c:P * c + P])
                ins.then_inc(*pe_of.step("gl.turn"))
                pe.wait_ge(*dve_of.at("gl.turned", l))
                for h in range(4):
                    for c in range(2):
                        ins = mm(mW[:, h, P * c:P * c + P], GK[32 * h:32 * h + 32, P * c:P * c + P],
                                 GQ[32 * h:32 * h + 32, P * c:P * c + P])
                ins.then_inc(*pe_of.step("gl.attn"))
                gates(8, 10)
                pe.wait_ge(*dve_of.at("gl.attn", l))
                for c in range(NC):
                    q0 = 64 * (c % 2)
                    ins = mm(mW[:, c % 2, 256 * (c // 2):256 * (c // 2) + 256], GKT[q0:q0 + 64, c // 2, :],
                             GVT[q0:q0 + 64, c // 2, :])
                ins.then_inc(*pe_of.step("gl.kv"))
                pe.wait_ge(*dve_of.at("gl.state", l))
                for j in range(2):
                    for c2 in range(2):
                        for h in (2 * j, 2 * j + 1):
                            p0 = 64 * (h % 2)
                            mm(mW[p0:p0 + 64, 2 + j, P * c2:P * c2 + P], GVT[:, c2, 64 * h:64 * h + 64],
                               GAT[:, c2, P * h:P * h + P], True, False)
                        for c in (2 * c2, 2 * c2 + 1):
                            ins = mm(mW[:, 2 + j, CH * c:CH * c + CH], GSS[:, c, P * j:P * j + P],
                                     GQH[:, CH * c:CH * c + CH], False, c % 2 == 1)
                ins.then_inc(*pe_of.step("gl.y"))
                pe.wait_ge(*dve_of.at("gl.dv", l))
                for j in range(2):
                    ins = mm(mW[:, 0, :], con[:, CC["gv"] + P * j:CC["gv"] + P * j + P],
                             GXX[:, j, :, :].rearrange("p b v -> p (b v)"), j == 0, j == 1)
                ins.then_inc(*pe_of.step("gl.dvb"))
                pe.wait_ge(*dve_of.at("gl.dq", l))
                for j in range(2):
                    ins = mm(mW[:, j, :], con[:, CC["gy"] + P * j:CC["gy"] + P * j + P],
                             GXX[:, 0, :, :].rearrange("p b v -> p (b v)"))
                ins.then_inc(*pe_of.step("gl.dy"))
                pe.wait_ge(*dve_of.at("gl.out", l))
                pe.wait_ge(*act_of.at("rw.lora", l))
                for j in range(2):
                    mm(mW[:, j, 0:T], lora[0:32, P * j:P * j + P], TH[0:32, :])
                    ins = mm(mW[:, 2 + j, 0:T], lora[32:64, P * j:P * j + P], U[32:64, TLO, :])
                ins.then_inc(*pe_of.step("rw.wa"))
                pe.wait_ge(*act_of.at("rw.wa", l))
                pe.wait_ge(*dve_of.at("rw.sg", l))
                for j in range(2):
                    ins = mm(mW[:, j, 0:T], lora[64:128, P * j:P * j + P], TH[64:128, :])
                ins.then_inc(*pe_of.step("rw.g"))
                for j in range(2):
                    ins = mm(mW[:, 2 + j, 0:T], bo, NRM[:, j, :])
                ins.then_inc(*pe_of.step("rw.ksum"))
                pe.wait_ge(*act_of.at("rw.g", l))
                pe.wait_ge(*dve_of.at("rw.rk", l))
                for j in range(2):
                    ins = mm(mW[:, j, 0:T], bo, RKV[:, j, :])
                ins.then_inc(*pe_of.step("rw.bonus"))
                gates(10, 12)
                pe.wait_ge(*dve_of.at("rw.dx", l))
                for j in range(2):
                    mm(mW[:, j, :], bo, DX[:, j, :, :].rearrange("p b v -> p (b v)"))
                for j in range(2):
                    ins = mm(mW[:, 2 + j, :], bo, DY[:, j, :, :].rearrange("p b v -> p (b v)"))
                ins.then_inc(*pe_of.step("rw.dsa"))
                pe.wait_ge(*dve_of.at("rw.dr", l))
                for j in range(2):
                    ins = mm(mW[:, j, :], bo, DX[:, j, :, :].rearrange("p b v -> p (b v)"))
                ins.then_inc(*pe_of.step("rw.dy"))
                pe.wait_ge(*dve_of.at("rw.ops", l))
                for c in range(2):
                    for j in range(2):
                        o = slice(256 * c + P * j, 256 * c + P * j + P)
                        turn(mW[:, 0, o], AR[:, j, c, 0, :])
                        turn(mW[:, 1, o], B2[:, j, P * c:P * c + P])
                        turn(mW[:, 2, o], K2[:, j, P * c:P * c + P])
                        ins = turn(mW[:, 3, o], U[:, TV + j, P * c:P * c + P])
                ins.then_inc(*pe_of.step("rw.turn"))
                pe.wait_ge(*dve_of.at("rw.turned", l))
                for g in range(2):
                    tok = slice(P * g, P * g + P)
                    if g:
                        pe.wait_ge(*dve_of.at("rw.y", l, 0))
                    for h in (0, 2, 1, 3):
                        j, e, p0 = h // 2, h % 2, 64 * (h % 2)
                        ar2 = AR[p0:p0 + 64, j, g, :, :].rearrange("p a t -> p (a t)")
                        mm(mW[:, e, 256 * j:256 * j + 256], BT[p0:p0 + 64, j, tok], ar2)
                        ins = mm(mW[:, 2 + e, 256 * j:256 * j + 256], KTL[p0:p0 + 64, j, tok], ar2)
                    ins.then_inc(*pe_of.step("rw.bk", g))
                    pe.wait_ge(*dve_of.at("rw.bk", l, g))
                    for n in range(4):
                        e, j = divmod(n, 2)
                        h = 2 * j + e
                        mm(mW[:, e, P * j:P * j + P], AR[64 * e:64 * e + 64, j, g, 0, :], BT[64 * e:64 * e + 64, j, tok])
                        ins = mm(mW[:, 2, 64 * h:64 * h + 64], MKS[:, n, 0:P], VTK[:, g, 64 * h:64 * h + 64])
                    ins.then_inc(*pe_of.step("rw.l", g))
                    pe.wait_ge(*dve_of.at("rw.l", l, g))

                    def four(bank, w, x):
                        for n in range(4):
                            ins = mm(mW[:, bank, P * n:P * n + P], w[:, n, 0:P], x[:, n, 0:P])
                        return ins

                    def apply(bank, w, x):
                        for n in range(4):
                            h = 2 * (n % 2) + n // 2
                            o = mW[:, bank, :].rearrange("p (a n) -> p a n", a=2)[:, :, 64 * h:64 * h + 64]
                            ins = mm(o, w[:, n, 0:P], x[:, :, 64 * h:64 * h + 64])
                        return ins

                    four(0, NB, ND)
                    four(1, ND, NB).then_inc(*pe_of.step("rw.p2", g))
                    pe.wait_ge(*act_of.at("rw.p2", l, g))
                    four(0, P2T, P2)
                    four(1, P2, P2T)
                    four(2, P2, QT).then_inc(*pe_of.step("rw.p4", g))
                    pe.wait_ge(*act_of.at("rw.p4", l, g))
                    pe.wait_ge(*dve_of.at("rw.q0", l, g))
                    four(0, P4T, P4)
                    four(2, P4, QT).then_inc(*pe_of.step("rw.p8", g))
                    pe.wait_ge(*act_of.at("rw.p8", l, g))
                    pe.wait_ge(*dve_of.at("rw.q1", l, g))
                    four(2, P2, QT).then_inc(*pe_of.step("rw.q", g))
                    pe.wait_ge(*dve_of.at("rw.q2", l, g))
                    four(0, NO, QT)
                    apply(1, QT, VW).then_inc(*pe_of.step("rw.et", g))
                    pe.wait_ge(*act_of.at("rw.et", l, g))
                    pe.wait_ge(*dve_of.at("rw.v0", l, g))
                    for k in range(3):
                        apply((3, 1, 3)[k], ET, YW if k else VW).then_inc(*pe_of.step("rw.e", 3 * g + k))
                        pe.wait_ge(*dve_of.at("rw.e", l, 3 * g + k))
                    for j in range(2):
                        ins = turn(mW[:, 2, P * j:P * j + P], YW[:, 0, P * j:P * j + P])
                    ins.then_inc(*pe_of.step("rw.wt", g))
                    pe.wait_ge(*act_of.at("rw.wt", l, g))
                    for c in (2 * g, 2 * g + 1):
                        q0 = 64 * (c % 2)
                        if c:
                            pe.wait_ge(*dve_of.at("rw.state", l, c - 1))
                        for n in range(4):
                            e, j = divmod(n, 2)
                            ins = mm(mW[q0:q0 + 64, 1 + 2 * e, 64 * j:64 * j + 64], WT[64 * e:64 * e + 64, j, q0:q0 + 64],
                                     SS[64 * e:64 * e + 64, j, c, :])
                        ins.then_inc(*pe_of.step("rw.z", c))
                        pe.wait_ge(*dve_of.at("rw.z", l, c))
                        for h in range(4):
                            j, e = divmod(h, 2)
                            out = mW[64 * e:64 * e + 64, 0, 64 * j:64 * j + 64]
                            mm(out, KTK[q0:q0 + 64, g, 64 * h:64 * h + 64], VTK[q0:q0 + 64, g, 64 * h:64 * h + 64], True, False)
                            ins = mm(out, BTK[q0:q0 + 64, g, 64 * h:64 * h + 64],
                                     ZZ[q0:q0 + 64, g, 64 * h:64 * h + 64], False, True)
                        ins.then_inc(*pe_of.step("rw.s", c))
                    for h in range(4):
                        j, e = divmod(h, 2)
                        n, p0 = 2 * e + j, 64 * e
                        mm(mW[p0:p0 + 64, 2, P * j:P * j + P], VTK[:, g, 64 * h:64 * h + 64], MKS[:, n, P:2 * P], True, False)
                        mm(mW[p0:p0 + 64, 2, P * j:P * j + P], ZZ[:, g, 64 * h:64 * h + 64], NB[:, n, P:2 * P], False, False)
                        for c in (0, 1):
                            ins = mm(mW[p0:p0 + 64, 2, P * j + 64 * c:P * j + 64 * c + 64], SS[p0:p0 + 64, j, 2 * g + c, :],
                                     AR[p0:p0 + 64, j, g, 1, 64 * c:64 * c + 64], False, c == 1)
                    ins.then_inc(*pe_of.step("rw.y", g))
                    if g == 0:
                        gates(12, 16)
                pe.wait_ge(*dve_of.at("rw.y", l, 1))
                for i in range(4):
                    ins = mm(mW[:, i, 0:T], C("bom"), OO[:, i, :])
                ins.then_inc(*pe_of.step("hn.mean"))
                pe.wait_ge(*act_of.at("hn.sq", l))
                for i in range(4):
                    ins = mm(mW[:, i, 0:T], C("bom"), OT[:, i, :])
                ins.then_inc(*pe_of.step("hn.var", 0))
                pe.wait_ge(*dve_of.at("hn.var4", l))
                for i in range(2):
                    ins = mm(mW[:, i, 0:T], C("bom"), OT[:, 4 + i, :])
                ins.then_inc(*pe_of.step("hn.var", 1))
                pe.wait_ge(*dve_of.at("br.ready", l))
                for p in range(4):
                    if p >= 2:
                        gates(8 * p, 8 * p + 8)
                    wt = chunk()
                    for i in range(8 * p, 8 * p + 8):
                        d, g = divmod(i, 4)
                        q = d % 2
                        tile("up", l, i, [wt[:, 2 * g + k, P * q:P * q + P] for k in range(2)], BRANCH[2 * g:2 * g + 2])\
                            .then_inc(*pe_of.step("mg.up", i))
                pe.wait_ge(*dve_of.at("mg.sum", l, KT - 1))
                for p in range(4):
                    pair("out", "mg.out", l, 2 * p, [V8[:, k, :] for k in range(KT)])

                def norm(i):
                    for k in range(KT):
                        ins = mm(mW[:, 0, 0:T], C("mean"), SQ8[:, k, :], k == 0, k == KT - 1)
                    ins.then_inc(*pe_of.step("ln.mean", i))
                    pe.wait_ge(*act_of.at("ln.sq", l, i))
                    for k in range(KT):
                        ins = mm(mW[:, 1, 0:T], C("mean"), V8[:, k, :], k == 0, k == KT - 1)
                    ins.then_inc(*pe_of.step("ln.var", i))
                    pe.wait_ge(*act_of.at("ln.norm", l, i))

                if l == DEPTH - 1:
                    pe.wait_ge(*pe_of.at("mg.out", l, KT - 1))
                    for done in (gate_done, up_done, down_done):
                        pe.sem_inc(done, FC)
                pe.wait_ge(*dve_of.at("mg.out", l, KT - 1))
                norm(0)
                if l == 0:
                    for c in range(FC):
                        for part in range(2):
                            wt = chunk()
                            for q in range(2):
                                ins = tile("f", l, 4 * c + 2 * part + q, [wt[:, k, P * q:P * q + P] for k in range(KT)], xs)
                        ins.then_inc(*pe_of.step("ff.up", c))
                    pe.wait_ge(*dve_of.at("ff.hid", l, FC - 1))
                    for p in range(4):
                        ws = [chunk() for _ in range(3)]
                        for q in range(2):
                            w = [ws[k // KT][:, k % KT, P * q:P * q + P] for k in range(FT)]
                            tile("d", l, 2 * p + q, w, [HS[:, k, :] for k in range(FT)])\
                                .then_inc(*pe_of.step("ff.down", 2 * p + q))
                    pe.wait_ge(*dve_of.at("ff.down", l, KT - 1))
                else:
                    moe_tensor(pe, mm, turn)
                norm(1)



IN_SIZES = (896, 512, 256, 256, 4, 4, 128, 128, 256, 256, 16, 256, 256, 4096)


def projection_columns():
    off = np.concatenate([[0], np.cumsum(IN_SIZES)])
    rw, mqk, mv, mo, mi, mf, gq, gk, gv, gg, ga, rx, ry, gates = off[:14]
    cols = -np.ones((NM, P), np.int64)
    r = np.arange(P)
    for first, n, tile in ((rw, 7, 0), (mqk, 4, TMQ), (mv, 2, TMV), (mo, 2, TMO), (gq, 1, TGQ), (gk, 1, TGK),
                           (gv, 2, TGV), (gg, 2, TGG), (rx, 2, TRX), (ry, 2, TRY)):
        for i in range(n):
            cols[tile + i] = first + P * i + r
    cols[TMI, 0:4] = mi + np.arange(4)
    cols[TMI, 32:36] = mf + np.arange(4)
    cols[TMI, 64:80] = ga + np.arange(16)
    for i in range(NG):
        d, g = divmod(i, 4)
        cols[NU + i] = gates + D * g + P * d + r
    return cols


def slots_of(w):
    *lead, rows, n = w.shape
    w = w.reshape(*lead, KT, P, n // 256, 256)
    k = len(lead)
    w = np.moveaxis(w, (k + 2, k + 1, k, k + 3), (k, k + 1, k + 2, k + 3))
    return w.reshape(*lead, n // 256, P, SLOT)


def by_partition(a):
    return np.swapaxes(a.reshape(*a.shape[:-1], -1, P), -1, -2)


def lay_out(i):
    f = {k: np.asarray(x) for k, x in i.items()}
    L = DEPTH
    out = {"const": constants()}
    x = np.concatenate([f["x_prompt"].reshape(TP, D), f["x_sample"].reshape(TD, D)], 0)
    out["x"] = np.ascontiguousarray(x.T.reshape(KT, P, T).transpose(1, 0, 2))
    cols = projection_columns()
    flat, there = cols.reshape(-1), cols.reshape(-1) >= 0
    w = np.zeros((L, D, NM * P), np.float32)
    w[:, :, there] = f["w_in"][:, :, flat[there]]
    out["w_in"] = slots_of(w)
    bias = np.zeros((L, NM * P), np.float32)
    bias[:, there] = f["b_in"][:, flat[there]]
    out["w_branch"] = slots_of(f["w_branch"].reshape(L, D, D))
    out["w_out"] = slots_of(f["w_out"])
    up = np.stack([slots_of(f["ffn_wg"])[0], slots_of(f["ffn_wu"])[0]], 1)
    out["ffn_up"] = up.reshape(2 * FC, P, SLOT)
    down = np.zeros((3 * KT * P, D), np.float32)
    down[:FF] = f["ffn_wd"][0]
    out["ffn_down"] = np.stack([slots_of(down[D * q:D * q + D]) for q in range(3)], 1).reshape(12, P, SLOT)
    moe = np.empty((NE, FC, 3, P, SLOT), np.float32)
    moe[:, :, 0] = slots_of(f["moe_wg"][0])
    moe[:, :, 1] = slots_of(f["moe_wu"][0])
    moe[:, :, 2] = f["moe_wd"][0].reshape(NE, FC, 2, P, D).transpose(0, 1, 3, 2, 4).reshape(NE, FC, P, SLOT)
    out["moe"] = moe.reshape(NE * FC * 3, P, SLOT)
    out["router"] = np.ascontiguousarray(f["moe_router"][0].reshape(KT, P, NE).transpose(1, 0, 2))
    out["rbias"] = np.ascontiguousarray(np.broadcast_to(f["moe_router_b"], (P, NE)))

    def taps(w, n):
        return w.reshape(L, 4, n, P).transpose(0, 3, 2, 1).reshape(L, P, 4 * n)

    par = {"bin": by_partition(bias[:, :NU * P]), "bgate": by_partition(bias[:, NU * P:]), "mcw": taps(f["mlstm_conv_w"], 4),
           "rcw": taps(f["rglru_conv_w"], 2), "rk": by_partition(f["rwkv_r_k"].reshape(L, -1))}
    for name, src in (("mu", "rwkv_mu"), ("w0", "rwkv_w0"), ("a0", "rwkv_a0"), ("kk", "rwkv_k_k"), ("ka", "rwkv_k_a"),
                      ("lnw", "rwkv_ln_w"), ("lnb", "rwkv_ln_b"), ("mcb", "mlstm_conv_b"), ("mnw", "mlstm_norm_w"),
                      ("gab", "gla_alpha_b"), ("gnw", "gla_norm_w"), ("rcb", "rglru_conv_b"), ("rba", "rglru_ba"),
                      ("rbx", "rglru_bx"), ("lam", "rglru_lambda"), ("ln1g", "ln1_g"), ("ln1b", "ln1_b"),
                      ("ln2g", "ln2_g"), ("ln2b", "ln2_b")):
        par[name] = by_partition(f[src])
    out["par"] = np.concatenate([par[name] for name in PC], -1)
    out["lora"] = np.concatenate([f["rwkv_w_up"], f["rwkv_a_up"], f["rwkv_g_up"]], 1)
    alup = np.zeros((L, P, P), np.float32)
    alup[:, 64:80] = f["gla_alpha_up"]
    out["alup"] = alup
    rgw = np.zeros((L, P, 4, P), np.float32)
    for k, name in enumerate(("rglru_wa", "rglru_wx")):
        for j in range(2):
            for e in range(2):
                rgw[:, 64 * e:64 * e + 64, 2 * k + j, 64 * e:64 * e + 64] = f[name][:, 2 * j + e]
    out["rgw"] = rgw
    t = np.transpose
    out["shift"] = t(f["state_rwkv_shift"].reshape(L, TD, 7, P), (0, 3, 2, 1))
    out["mconv"] = t(f["state_mlstm_conv"].reshape(L, TD, 3, 4, P), (0, 4, 3, 2, 1))
    out["rconv"] = t(f["state_rglru_conv"].reshape(L, TD, 3, 2, P), (0, 4, 3, 2, 1))
    out["h0"] = t(f["state_rglru_h"].reshape(L, TD, 2, P), (0, 3, 2, 1))
    out["n0"] = t(f["state_mlstm_n"].reshape(L, TD, 2, P), (0, 3, 2, 1))
    out["m0"] = t(f["state_mlstm_m"], (0, 2, 1))
    for name, src in (("mC", "state_mlstm_C"), ("rS", "state_rwkv_S")):
        out[name] = t(f[src].reshape(L, TD, 2, 2, 64, 64), (0, 3, 5, 2, 1, 4)).reshape(L, P, 2, TD, 64)
    out["gS"] = t(f["state_gla_S"], (0, 2, 3, 1, 4)).reshape(L, P, TD, 64)
    return {k: np.ascontiguousarray(x) for k, x in out.items()}


OUTS = {"y": (P, KT, T), "h": (DEPTH, P, 2, 9), "rconv": (DEPTH, P, 2, 3, 9), "shift": (DEPTH, P, 7, 9), "m": (DEPTH, 4, 9),
        "mconv": (DEPTH, P, 4, 3, 9), "mC": (DEPTH, P, 2, 64), "mCs": (DEPTH, P, 2, TD, 64), "n": (DEPTH, P, 2, 9),
        "gSs": (DEPTH, P, TD, 64), "gS": (DEPTH, P, 256), "rSs": (DEPTH, P, 2, TD, 64), "rS": (DEPTH, P, 2, 64)}


def take_out(o):
    L, t = DEPTH, np.transpose
    y = t(o["y"], (2, 1, 0)).reshape(T, D)
    cols = {"shift": t(o["shift"], (0, 3, 2, 1)).reshape(L, 9, 896), "h": t(o["h"], (0, 3, 2, 1)).reshape(L, 9, 256),
            "n": t(o["n"], (0, 3, 2, 1)).reshape(L, 9, 4, 64), "m": t(o["m"], (0, 2, 1)),
            "mconv": t(o["mconv"], (0, 4, 3, 2, 1)).reshape(L, 9, 3, 512),
            "rconv": t(o["rconv"], (0, 4, 3, 2, 1)).reshape(L, 9, 3, 256)}

    def square(x, n):
        return t(x.reshape(L, 2, 64, 2, n, 64), (0, 4, 3, 1, 5, 2)).reshape(L, n, 4, 64, 64)

    def states(lo, hi, rS, mC, gS):
        c = {k: np.ascontiguousarray(a[:, lo:hi]) for k, a in cols.items()}
        return c["shift"], rS, c["mconv"], mC, c["n"], c["m"], gS, c["rconv"], c["h"]

    gp = o["gS"].reshape(L, 4, 32, 4, 64)
    gp = np.stack([gp[:, h, :, h] for h in range(4)], 1)[:, None]
    gs = t(o["gSs"].reshape(L, 4, 32, TD, 64), (0, 3, 1, 2, 4))
    prompt = states(0, 1, square(o["rS"], 1), square(o["mC"], 1), gp)
    sample = states(1, 9, square(o["rSs"], TD), square(o["mCs"], TD), gs)
    out = (y[None, :TP], y[TP:, None]) + prompt + sample
    return tuple(np.ascontiguousarray(a) for a in out)


def kernel(**inputs):
    import concourse.bacc as _bacc
    from concourse.bass_utils import run_bass_kernel_spmd as _run

    nc = _bacc.Bacc("TRN2", target_bir_lowering=False, num_devices=1)
    arrays = {f"in_{k}_dram": a for k, a in lay_out(inputs).items()}
    A = {k[3:-5]: nc.dram_tensor(k, a.shape, F32, kind="ExternalInput").ap() for k, a in arrays.items()}
    O = {k: nc.dram_tensor(f"out_{k}_dram", shape, F32, kind="ExternalOutput").ap() for k, shape in OUTS.items()}
    program(nc, A, O)
    r = _run(nc, [arrays], core_ids=[0])
    return take_out({k: r.results[0][f"out_{k}_dram"] for k in OUTS})
```

```python
from contextlib import ExitStack

import numpy as np

import concourse.bass as bass
from concourse import mybir

F32 = mybir.dt.float32
I32 = mybir.dt.int32
U32 = mybir.dt.uint32
ALU = mybir.AluOpType
ACT = mybir.ActivationFunctionType
AX_X = mybir.AxisListType.X

P = 128
D = 1024
KT = D // P
DEPTH = 2
TP, TD = 256, 8
T = TP + TD
FF = 2816
NE = 8
CH = 64
NC = TP // CH
ALPHA = (2 * DEPTH) ** 0.25
LN_EPS = 1e-5

TR, TK, TV, TLO, TMI, TMQ, TMK, TMV, TGQ, TGK, TMO, TGV, TGG, TRX, TRY = 0, 2, 4, 6, 7, 8, 10, 12, 14, 15, 16, 18, 20, 22, 24
NU = 26
NG = 32
NM = NU + NG
SLOTS = 9
SLOT = 2048
GR = 8
RG, ML, GL, RW = 3, 1, 2, 0
FC = FF // 256
FT = FF // P

STREAM = ([("u", i) for i in (TMI - 1, TRX, TRY, TMQ, TMK, TMV, TMO, TGQ, TGV, TGG, TR, TK, TV)]
          + [("merge", g, q) for g in (RG, ML, GL) for q in range(4)]
          + [("gate", RW, q) for q in range(4)] + [("up", RW, q) for q in range(4)])
FILL = {"start": 3, "alpha": 1, "rg1": 2, "rg2": 1, "rg3": 2, "ml1": 2, "ml2": 2, "ml3": 1, "ml4": 1, "ml5": 1, "ml6": 1,
        "gl1": 1, "gl2": 1, "rw1": 1, "rw2": 1, "rw3": 1, "rw4": 1, "rw5": 1,
        "g0a": 1, "g0b": 0, "g0c": 1, "g0d": 0, "g1a": 1, "g1b": 0, "g1c": 1, "g1d": 0, "tail": 1, "end": 4}
assert sum(FILL.values()) == len(STREAM)

PC = {}


def _cols():
    at = 0
    for name, n in (("bin", NU), ("bgate", NG), ("mu", 7), ("w0", 2), ("a0", 2), ("kk", 2), ("ka", 2), ("rk", 2),
                    ("lnw", 2), ("lnb", 2), ("mcw", 16), ("mcb", 4), ("mnw", 2), ("gab", 1), ("gnw", 2),
                    ("rcw", 8), ("rcb", 2), ("rba", 2), ("rbx", 2), ("lam", 2),
                    ("ln1g", KT), ("ln1b", KT), ("ln2g", KT), ("ln2b", KT)):
        PC[name] = at
        at += n
    return at


NPAR = _cols()

CC = {}


def _const_cols():
    at = 0
    for name, n in (("ident", P), ("bo", P), ("bom", P), ("mean", P), ("mb", 256), ("mk", 256), ("ml16", P), ("mlo", P),
                    ("i64", 64), ("neg", P), ("gv", 256), ("gy", 256), ("gm", 256), ("reset", TP), ("ones", TP),
                    ("tri", P), ("iota", P), ("iota8", NE)):
        CC[name] = at
        at += n
    return at


NCON = _const_cols()


def constants():
    c = np.zeros((P, NCON), np.float32)
    i = np.arange(P)
    s, t = i[:, None], i[None, :]

    def put(name, m):
        c[:m.shape[0], CC[name]:CC[name] + m.shape[1]] = m

    b64, b16 = s // 64 == t // 64, s // 16 == t // 16
    put("ident", np.eye(P))
    put("bo", b64 * 1.0)
    put("bom", b64 / 64.0)
    put("mean", np.full((P, P), 1.0 / D))
    put("mb", np.concatenate([-1.0 * (b16 & (s < t)), -1.0 * (b64 & (s <= t))], 1))
    put("mk", np.concatenate([1.0 * (b64 & (s < t)), 1.0 * (b64 & (s <= t))], 1))
    put("ml16", -1.0 * (b16 & (t < s)))
    put("mlo", -1.0 * (b64 & ~b16 & (t < s)))
    put("i64", 1.0 * (i[:, None] % 64 == np.arange(64)[None]))
    put("neg", np.where(s <= t, 0.0, -1e30))
    put("gv", np.concatenate([1.0 * (2 * j + s // 64 == t // 32) for j in range(2)], 1))
    put("gy", np.concatenate([1.0 * (2 * j + t // 64 == s // 32) for j in range(2)], 1))
    put("gm", 1.0 * (i[:, None] // 32 == np.arange(256)[None] // 64))
    put("reset", np.tile(1.0 * (np.arange(TP) % CH != 0), (P, 1)))
    put("ones", np.ones((P, TP)))
    put("tri", 1.0 * (s < t))
    put("iota", np.tile(np.arange(P), (P, 1)))
    put("iota8", np.tile(np.arange(NE), (P, 1)))
    return c




class Steps:

    def __init__(self, nc, ctx, engine, table):
        self.engine = engine
        self.first, self.count, self.sem, self.fired, self.seen = {}, {}, {}, {}, {}
        for name, n in table:
            g = self.group(name, n)
            if g not in self.sem:
                self.sem[g] = ctx.enter_context(nc.semaphore(f"{g}_{engine}"))
                self.count[g] = self.fired[g] = 0
            self.first[name] = g, self.count[g]
            self.count[g] += n

    @staticmethod
    def group(name, n):
        return name.split(".")[0] if n == 1 else name

    def step(self, name, i=0):
        if RECORD:
            self.seen[name] = self.seen.get(name, 0) + 1
            return self.scratch, 1
        g, first = self.first[name]
        assert self.fired[g] % self.count[g] == first + i, (self.engine, name, i, self.fired[g], self.count[g], first)
        self.fired[g] += 1
        return self.sem[g], 1

    def at(self, name, l, i=0):
        if RECORD:
            return self.scratch, 1
        g, first = self.first[name]
        return self.sem[g], l * self.count[g] + first + i + 1


RECORD = False
PE_TABLE = (
    ("u.tile", 26), ("lg.alpha", 1), ("rg.gates", 1), ("ml.turn", 1), ("gate.tile", 32),
    ("mg.up", 32), ("ml.logd", 4), ("ml.qk", 4), ("ml.num", 1), ("ml.emb", 1),
    ("ml.c", 1), ("ml.dvb", 1), ("ml.dnum", 1), ("n1.mean", 1), ("n1.var", 1),
    ("gl.turn", 1), ("gl.attn", 1), ("gl.kv", 1), ("gl.y", 1), ("gl.dvb", 1),
    ("gl.dy", 1), ("n2.var", 1), ("rw.wa", 1), ("rw.g", 1), ("rw.ksum", 1),
    ("rw.bonus", 1), ("rw.dsa", 1), ("rw.dy", 1), ("rw.turn", 1), ("rw.bk", 2),
    ("rw.l", 2), ("rw.p2", 2), ("rw.p4", 2), ("rw.p8", 2), ("rw.q", 2),
    ("rw.et", 2), ("rw.e", 6), ("rw.wt", 2), ("rw.z", 4), ("rw.s", 4),
    ("rw.y", 2), ("n0.mean", 1), ("n0.var", 1), ("mg.out", 8), ("ln.mean", 2),
    ("ln.var", 2), ("ff.up", 11), ("ff.down", 8),
)
ACT_TABLE = (
    ("u.tile", 26), ("rg.tanh", 1), ("lg.exp", 1), ("rg.exp", 1), ("rg.gelu", 1),
    ("rg.sqrt", 1), ("ml.silu", 1), ("ml.exps", 1), ("ml.og", 1), ("gate.tile", 32),
    ("ml.d", 4), ("ml.abs", 1), ("n1.sq", 1), ("n1.sqrt", 1), ("gl.og", 1),
    ("gl.exp", 1), ("n2.sq", 1), ("n2.sqrt", 1), ("rw.lora", 1), ("rw.ksq", 1),
    ("rw.wa", 1), ("rw.g", 1), ("rw.ksqrt", 1), ("rw.exp", 1), ("rw.p2", 2),
    ("rw.p4", 2), ("rw.p8", 2), ("rw.et", 2), ("rw.wt", 2), ("n0.sq", 1),
    ("n0.sqrt", 1), ("ln.sq", 2), ("ln.sqrt", 2), ("ln.norm", 2), ("ff.tanh", 11),
)
DVE_TABLE = (
    ("u.half", 1), ("lg.in", 1), ("rg.conv", 1), ("rg.loga", 1), ("rg.gelu_in", 1),
    ("rg.var", 1), ("rg.out", 1), ("ml.conv", 1), ("ml.rows", 1), ("ml.qk", 1),
    ("ml.dec_rows", 1), ("ml.gcol", 1), ("mg.up", 32), ("ml.sd", 4), ("ml.kw", 4),
    ("ml.h", 1), ("ml.cout", 1), ("ml.dv", 1), ("ml.dq", 1), ("ml.out", 1),
    ("n1.centred", 1), ("n1.var", 1), ("ml.branch", 1), ("gl.cum", 1), ("gl.ops", 1),
    ("gl.turned", 1), ("gl.attn", 1), ("gl.state", 1), ("gl.dv", 1), ("gl.y", 1),
    ("gl.dec", 1), ("gl.dq", 1), ("gl.out", 1), ("n2.centred", 1), ("n2.var", 1),
    ("gl.branch", 1), ("rw.mixed", 1), ("rw.sg", 1), ("rw.rk", 1), ("rw.ksum", 1),
    ("rw.bonus", 1), ("rw.cum", 1), ("rw.dx", 1), ("rw.dec", 1), ("rw.dr", 1),
    ("rw.dout", 1), ("rw.ops", 1), ("rw.turned", 1), ("rw.bk", 2), ("rw.l", 2),
    ("rw.q0", 2), ("rw.q1", 2), ("rw.q2", 2), ("rw.v0", 2), ("rw.e", 6),
    ("rw.z", 4), ("rw.state", 4), ("rw.y", 2), ("n0.centred", 1), ("n0.var", 1),
    ("rw.branch", 1), ("ms.sum", 4), ("mg.out", 8), ("ln.centred", 2), ("ln.var", 2),
    ("ln.scaled", 2), ("ff.hid", 11), ("ff.down", 8),
)

def col(ap, n):
    return ap.unsqueeze(2).broadcast_to([ap.shape[0], ap.shape[1], n])


def mid(ap, n):
    return ap.unsqueeze(1).broadcast_to([ap.shape[0], n, ap.shape[1]])


def program(nc, A, O):
    with ExitStack() as ctx:
        def sb(name, shape, dt=F32):
            return ctx.enter_context(nc.sbuf_tensor(name, shape, dt))

        def sem(name):
            return ctx.enter_context(nc.semaphore(name))

        pe_of = Steps(nc, ctx, "pe", PE_TABLE)
        act_of = Steps(nc, ctx, "act", ACT_TABLE)
        dve_of = Steps(nc, ctx, "dve", DVE_TABLE)
        if RECORD:
            for st in (pe_of, act_of, dve_of):
                st.scratch = sem(f"rec_{st.engine}")
        act_link, dve_link = sem("act_link"), sem("dve_link")
        const_in, router_in, x_in, layer_in, state_out = sem("const_in"), sem("router_in"), sem("x_in"), sem("layer_in"), sem("state_out")
        slot_in = [sem(f"slot_in{i}") for i in range(SLOTS)]
        moe_setup_pe, moe_setup_dve, moe_setup_act = sem("moe_setup_pe"), sem("moe_setup_dve"), sem("moe_setup_act")
        rounds_known = sem("rounds_known")
        place_ready, placeT_pe, placeT_ready = sem("place_ready"), sem("placeT_pe"), sem("placeT_ready")
        gathered, gather_kept = sem("gathered"), sem("gather_kept")
        gate_done, up_done, down_done = sem("gate_done"), sem("up_done"), sem("down_done")
        tanh_done, hidden, down_kept = sem("tanh_done"), sem("hidden"), sem("down_kept")
        scattered, scatter_added = sem("scattered"), sem("scatter_added")
        placed, gated, round_over = sem("placed"), sem("gated"), sem("round_over")

        ring = sb("ring", [P, SLOTS, SLOT])
        con = sb("con", [P, NCON])
        par = sb("par", [P, NPAR])
        half = sb("half", [P, NPAR])
        lora = sb("lora", [P, 256])
        alup = sb("alup", [P, P])
        rgw = sb("rgw", [P, 4, P])
        X = sb("X", [P, KT, T])
        BIG = sb("BIG", [P, (NU + GR + KT) * T])
        U = BIG[:, 0:NU * T].rearrange("p (n t) -> p n t", t=T)
        GT = BIG[:, NU * T:(NU + GR) * T].rearrange("p (n t) -> p n t", t=T)
        MG = BIG[:, (NU + GR) * T:(NU + GR + KT) * T].rearrange("p (n t) -> p n t", t=T)
        HS = BIG[:, 0:FT * T].rearrange("p (n t) -> p n t", t=T)
        V8 = sb("V8", [P, KT, T])
        SQ8 = sb("SQ8", [P, KT, T])
        SCR = sb("SCR", [P, 12416])
        small = sb("small", [P, 612])
        count_i = sb("count_i", [1, 4], I32)
        mA = ctx.enter_context(nc.psum_tensor("mA", [P, 4, 512], F32))
        mW = ctx.enter_context(nc.psum_tensor("mW", [P, 4, 512], F32))
        WF = mW[:, :, :].rearrange("p a b -> p (a b)")

        def C(name, n=P, rows=P):
            return con[0:rows, CC[name]:CC[name] + n]

        def pc(name, i=0, lo=0, hi=P, src=par):
            return src[lo:hi, PC[name] + i:PC[name] + i + 1]

        def hc(name, i=0, lo=0, hi=P):
            return pc(name, i, lo, hi, half)

        class Area:

            def __init__(self, base, at=0):
                self.base, self.at = base, at

            def __call__(self, *shape, rows=P):
                n = int(np.prod(shape))
                assert self.at + n <= self.base.shape[1], (self.at + n, self.base.shape)
                a = self.base[0:rows, self.at:self.at + n]
                self.at += n
                if len(shape) > 1:
                    k = "abcd"[:len(shape)]
                    a = a.rearrange(f"p ({' '.join(k)}) -> p {' '.join(k)}", **dict(zip(k, shape)))
                return a

        sm = Area(small)
        shift_in = sm(7, TD)
        shift_out = sm(7, 9)
        mbuf = sm(4, 3, TD)
        rbuf = sm(2, 3, TD)
        h0 = sm(2, TD)
        n0 = sm(2, TD)
        m0 = sm(TD, rows=P)[0:4, :]
        n_out = sm(2, 9)
        m_out = sm(9, rows=P)[0:4, :]
        h_out = sm(2, 9)
        mconv_out = sm(4, 3, 9)
        rconv_out = sm(2, 3, 9)
        lam4 = sm(2)
        GYD = sm(2, TD)
        PLAST = sm(2, NC)
        router = sm(KT, NE)
        rbias = sm(NE)
        sq8 = SQ8[:, :, :].rearrange("p a b -> p (a b)")

        ar = Area(SCR)
        LGN = 2 * T + 2
        LG, LE, LY, LZ = ar(LGN), ar(LGN), ar(LGN), ar(LGN)
        RC, RT, RA, RL, RE, RX = ar(2, T), ar(4, T), ar(2, T), ar(2, T), ar(2, T), ar(2, T)
        RS, RH = ar(2, T), ar(2, T)
        assert ar.at < 12416

        ar = Area(SCR, 2 * LGN)
        CV, TQ = ar(4, T), ar(4, T)
        MVT, MKT = ar(2, 256), ar(2, 256)
        MSD = ar(4, 384)
        MD = ar(2, 384)
        MR = ar(6 * T)
        MDEN = ar(2, T)
        MGC = ar(2, 4)
        MDC = ar(2, 3, TD)
        ar_m = ar.at
        MS = ar(2, TD, 64)
        MX = ar(2, TD, 64)
        MCO = ar(2, 64)
        assert ar.at <= 12416, ar.at

        ar = Area(SCR, 2 * LGN)
        GB, GX = ar(TP), ar(4, TP)
        GQ, GK, GQH, GKH = ar(TP), ar(TP), ar(TP), ar(TP)
        GVT, GKT = ar(2, 256), ar(2, P)
        GAT = ar(2, 512)
        GKV = ar(NC, 256)
        GSS = ar(NC + 1, 256)
        GDX = ar(TD)
        GS, GXX = ar(TD, 64), ar(2, TD, 64)
        assert ar.at <= 12416, ar.at

        ar = Area(SCR)
        DL = ar(7, T)
        LW, AA, GG, TH = DL[:, 0:2, :], DL[:, 2:4, :], DL[:, 4:6, :], DL[:, 6, :]
        KKN, K4, RKV, NRM = ar(2, T), ar(2, T), ar(2, T), ar(2, T)
        AR = ar(2, 2, 2, P)
        BT, KTL, B2, K2 = ar(2, TP), ar(2, TP), ar(2, TP), ar(2, TP)
        ar_r = ar.at
        ATK, BTK, KTK, VTK = ar(2, 256), ar(2, 256), ar(2, 256), ar(2, 256)
        NB, MKS = ar(4, 256), ar(4, 256)
        VW = BIG[:, TRX * T:TRX * T + 512].rearrange("p (a b) -> p a b", a=2)
        WT = ar(2, P)
        ZZ = BIG[:, TGV * T:TGV * T + 512].rearrange("p (a b) -> p a b", a=2)
        SS = ar(2, NC + 1, 64)
        assert ar.at <= 12416, ar.at
        ar = Area(SCR, ar_r)
        DS, DX, DY = ar(2, TD, 64), ar(2, TD, 64), ar(2, TD, 64)
        DW = ar(2, TD)
        DKA = ar(2, TD)
        dead = BIG[:, TMQ * T:TMO * T]
        ND, NO, P2, P2T = (dead[:, 512 * i:512 * i + 512].rearrange("p (a b) -> p a b", a=4) for i in range(4))
        P4, P4T, QT, ET = (sq8[:, 512 * i:512 * i + 512].rearrange("p (a b) -> p a b", a=4) for i in range(4))
        EXPS = dead[:, 0:3 * 512].rearrange("p (a b t) -> p a b t", a=3, t=TP)

        OO = V8[:, 0:6, :]
        OT = SQ8[:, 0:6, :]
        MOG, GGS = U[:, TMO:TMO + 2, :], U[:, TGG:TGG + 2, :]
        RGY = U[:, TRY:TRY + 2, :]
        GTH = U[:, TRX:TRX + 2, :]
        YW = sq8[:, 0:512].rearrange("p (a b) -> p a b", a=2)
        BRANCH = {RG: RGY, ML: MOG, GL: GGS, RW: U[:, TR:TR + 2, :]}
        FTH = SCR[:, 0:4 * T].rearrange("p (a b t) -> p a b t", a=2, b=2)

        ar = Area(SCR)
        XT = ar(3, D)
        XE = ar(2, KT, P)
        HE = ar(2, 256)
        YE = ar(D)
        PL = ar(3, P)
        PG = ar(3, P)
        PGT = ar(2, T)
        LOG, TOP = ar(3, NE), ar(3, 8)
        TIX = ar(24).bitcast(U32).rearrange("p (a b) -> p a b", a=3)
        IXF = ar(3, 8)
        TW = ar(3, 2)
        MASK, TMPE = ar(3, NE), ar(3, NE)
        GATE, RANK = ar(3, 3 * NE + 1), ar(3, 3 * NE + 1)
        ETH = ar(2, 256)
        CNT = ar(8)

        chunks = []
        for l in range(DEPTH):
            tiles = gates = 0
            for item in STREAM:
                if item[0] == "u":
                    tiles += 2
                    chunks.append((A["w_in"][l, item[1] // 2], pe_of.at("u.tile", l, tiles - 1)))
                    continue
                kind, g, q = item
                if q == 0 and kind != "gate":
                    chunks.append((A["w_branch"][l, g], pe_of.at("mg.up", l, KT * (RG, ML, GL, RW).index(g) + KT - 1)))
                if kind != "up":
                    gates += 2
                    chunks.append((A["w_in"][l, NU // 2 + 4 * g + q], pe_of.at("gate.tile", l, gates - 1)))
            chunks += [(A["w_out"][l, p], pe_of.at("mg.out", l, 2 * p + 1)) for p in range(4)]
            if l == 0:
                chunks += [(A["ffn_up"][i], pe_of.at("ff.up", l, i // 2)) for i in range(2 * FC)]
                chunks += [(A["ffn_down"][i], pe_of.at("ff.down", l, 2 * (i // 3) + 1)) for i in range(12)]
        uses0 = [len(range(k, len(chunks), SLOTS)) for k in range(SLOTS)]
        PAIR = 6 * FC
        per_pair = [len(range(k, PAIR, SLOTS)) for k in range(SLOTS)]

        block = ctx.enter_context(nc.Block())

        def rounds_of(eng):
            eng.wait_ge(rounds_known, 1)
            return eng.value_load(count_i[0:1, 0:1], min_val=1, max_val=3)

        @block.sync
        def _(sp):
            sp.dma_start(con[:, :], A["const"]).then_inc(const_in, 16)
            sp.dma_start(X[:, :, :], A["x"]).then_inc(x_in, 16)
            for i, (src, _) in enumerate(chunks):
                if i >= SLOTS:
                    sp.wait_ge(*chunks[i - SLOTS][1])
                sp.dma_start(ring[:, i % SLOTS, :], src).then_inc(slot_in[i % SLOTS], 16)
            R = rounds_of(sp) if not RECORD else 1
            with sp.Fori(0, R) as r:
                with sp.Fori(0, NE // 2) as e2:
                    for i in range(PAIR):
                        last = (i - SLOTS) // 3
                        if i < SLOTS:
                            last = max(range(i, PAIR, SLOTS)) // 3 - 2 * FC
                        sp.wait_ge((gate_done, up_done, down_done)[i % 3], (r * (NE // 2) + e2) * (2 * FC) + (last + 1 + FC))
                        sp.dma_start(ring[:, i % SLOTS, :], A["moe"][bass.ds(e2 * PAIR + i, 1), :, :].rearrange("a p n -> (a p) n"))\
                            .then_inc(slot_in[i % SLOTS], 16)
            sp.wait_ge(*act_of.at("ln.norm", 1, 1))
            sp.dma_start(O["y"], X[:, :, :]).then_inc(state_out, 16)
            sp.wait_ge(state_out, 16 * (12 * DEPTH + 1))

        @block.gpsimd
        def _(pool):
            pool.dma_start(router, A["router"]).then_inc(router_in, 16)
            pool.dma_start(rbias, A["rbias"]).then_inc(router_in, 16)
            for l in range(DEPTH):
                if l:
                    pool.wait_ge(*act_of.at("ln.norm", l - 1, 1))
                for dst, src in ((par[:, :], "par"), (lora[:, :], "lora"), (alup[:, :], "alup"), (rgw[:, :, :], "rgw"), (shift_in, "shift"),
                                 (mbuf, "mconv"), (rbuf, "rconv"), (h0, "h0"), (n0, "n0"), (m0, "m0")):
                    pool.dma_start(dst, A[src][l]).then_inc(layer_in, 16)
                pool.wait_ge(*dve_of.at("rg.out", l))
                pool.dma_start(MS, A["mC"][l]).then_inc(layer_in, 16)
                pool.wait_ge(*dve_of.at("ml.out", l))
                pool.wait_ge(*pe_of.at("ml.c", l))
                pool.wait_ge(state_out, 16 * (12 * l + 7))
                pool.dma_start(GS, A["gS"][l]).then_inc(layer_in, 16)
                pool.wait_ge(*dve_of.at("gl.out", l))
                pool.wait_ge(state_out, 16 * (12 * l + 9))
                pool.dma_start(DS, A["rS"][l]).then_inc(layer_in, 16)

        LAYER_LOADS = 13

        def loads(l, n):
            return layer_in, 16 * (LAYER_LOADS * l + n)

        numbers, emptied = {}, []

        def number(kind, l, i, emptied_by):
            numbers[kind, l, i] = len(emptied)
            emptied.append(emptied_by)

        for l in range(DEPTH):
            tiles = gates = ups = 0
            for item in STREAM:
                for _ in range(2):
                    if item[0] == "u":
                        number("u", l, tiles, act_of.at("u.tile", l, tiles))
                        tiles += 1
                for _ in range(2):
                    if item[0] in ("merge", "gate"):
                        number("gate", l, gates, act_of.at("gate.tile", l, gates))
                        gates += 1
                for _ in range(2):
                    if item[0] in ("merge", "up"):
                        number("up", l, ups, dve_of.at("mg.up", l, ups))
                        ups += 1
            for i in range(KT):
                number("out", l, i, dve_of.at("mg.out", l, i))
            if l == 0:
                for i in range(KT):
                    number("d", l, i, dve_of.at("ff.down", l, i))

        def acc(kind, l, i):
            return mA[:, numbers[kind, l, i] % 4, 0:T]

        def ff_acc(c, i):
            return (mA, mW)[c % 2][:, i, 0:T]

        def filler(do):
            at = {"n": 0, "u": 0, "gate": 0, "up": 0}

            def fill(point):
                for _ in range(FILL[point]):
                    item = STREAM[at["n"]]
                    at["n"] += 1
                    kinds = {"u": ("u",), "merge": ("gate", "up"), "gate": ("gate",), "up": ("up",)}[item[0]]
                    for kind in kinds:
                        do(kind, at[kind], item)
                        at[kind] += 2
            return fill

        @block.scalar
        def _(act):
            nact = nc.scalar
            linked = [0]

            def link(ins):
                linked[0] += 1
                ins.then_inc(act_link, 1)
                act.wait_ge(act_link, linked[0])

            def store(dst, src):
                act.dma_start(dst, src).then_inc(state_out, 16)

            for l in range(DEPTH):
                act.wait_ge(*loads(l, 10))
                if l:
                    act.wait_ge(state_out, 16 * 12 * l)
                act.wait_ge(*dve_of.at("u.half", l))

                def streamed(kind, i, item):
                    for q in range(2):
                        if kind == "u":
                            act.wait_ge(*pe_of.at("u.tile", l, i + q))
                            nact.activation(U[:, item[1] + q, :], acc("u", l, i + q), ACT.Identity, bias=pc("bin", item[1] + q))\
                                .then_inc(*act_of.step("u.tile", i + q))
                        if kind == "gate":
                            act.wait_ge(*pe_of.at("gate.tile", l, i + q))
                            if i + q >= GR:
                                act.wait_ge(*dve_of.at("mg.up", l, i + q - GR))
                            nact.activation(GT[:, (i + q) % GR, :], acc("gate", l, i + q), ACT.Tanh, scale=0.5,
                                            bias=hc("bgate", KT * item[1] + 2 * item[2] + q)).then_inc(*act_of.step("gate.tile", i + q))

                fill = filler(streamed)

                def head_norm(name, tiles):
                    act.wait_ge(*dve_of.at(f"{name}.centred", l))
                    nact.activation(OT[:, tiles, :], OO[:, tiles, :], ACT.Square).then_inc(*act_of.step(f"{name}.sq"))
                    act.wait_ge(*dve_of.at(f"{name}.var", l))
                    nact.activation(OT[:, tiles, :], OT[:, tiles, :], ACT.Sqrt).then_inc(*act_of.step(f"{name}.sqrt"))

                fill("start")
                act.wait_ge(*act_of.at("u.tile", l, 5))
                link(nact.activation(RX, RGY, ACT.Square))
                fill("alpha")
                act.wait_ge(*pe_of.at("rg.gates", l))
                for j in range(4):
                    ins = nact.activation(RT[:, j, :], mW[:, j, 0:T], ACT.Tanh, scale=0.5,
                                          bias=hc("rba", j) if j < 2 else hc("rbx", j - 2))
                ins.then_inc(*act_of.step("rg.tanh"))
                act.wait_ge(*dve_of.at("lg.in", l))
                link(nact.activation(LE, LG, ACT.Abs))
                nact.activation(LE, LE, ACT.Exp, scale=-1.0).then_inc(*act_of.step("lg.exp"))
                fill("rg1")
                act.wait_ge(*dve_of.at("rg.loga", l))
                nact.activation(RE, RL, ACT.Exp, scale=2.0)
                nact.activation(RS, RL, ACT.Tanh)
                nact.activation(RA, RL, ACT.Exp).then_inc(*act_of.step("rg.exp"))
                act.wait_ge(*dve_of.at("rg.gelu_in", l))
                nact.activation(RX, RX, ACT.Tanh, scale=0.7978845608028654).then_inc(*act_of.step("rg.gelu"))
                fill("rg2")
                act.wait_ge(*dve_of.at("rg.var", l))
                nact.activation(RE, RE, ACT.Sqrt, scale=-1.0).then_inc(*act_of.step("rg.sqrt"))
                fill("rg3")
                act.wait_ge(*dve_of.at("ml.conv", l))
                nact.activation(TQ, CV, ACT.Tanh, scale=0.5).then_inc(*act_of.step("ml.silu"))
                fill("ml1")
                act.wait_ge(*dve_of.at("ml.rows", l))
                nact.activation(MR[0:4, 4 * T:5 * T], MR[0:4, T:2 * T], ACT.Exp, scale=-1.0)
                nact.activation(MR[0:4, 5 * T:5 * T + 16], MR[0:4, 5 * T:5 * T + 16], ACT.Exp)\
                    .then_inc(*act_of.step("ml.exps"))
                nact.activation(MOG, MOG, ACT.Tanh, scale=0.5).then_inc(*act_of.step("ml.og"))
                store(O["h"][l], h_out)
                store(O["rconv"][l], rconv_out)
                fill("ml2")
                store(O["m"][l], m_out)
                store(O["mconv"][l], mconv_out)
                fill("ml3")
                for h in range(4):
                    act.wait_ge(*pe_of.at("ml.logd", l, h))
                    if h >= 2:
                        act.wait_ge(*dve_of.at("ml.sd", l, h - 2))
                        act.wait_ge(*dve_of.at("ml.kw", l, h - 2))
                    act.wait_ge(*dve_of.at("ml.gcol", l))
                    nact.activation(MD[:, h % 2, 0:256], mW[:, h % 2, 0:256], ACT.Exp, bias=MGC[:, 0, h:h + 1])
                    nact.activation(MD[:, h % 2, 256:384], mW[:, h % 2, 256:384], ACT.Exp, bias=MGC[:, 1, h:h + 1])\
                        .then_inc(*act_of.step("ml.d", h))
                fill("ml4")
                act.wait_ge(*pe_of.at("ml.num", l))
                nact.activation(MDEN[:, :, 0:256], mW[:, 2:4, 0:256], ACT.Abs).then_inc(*act_of.step("ml.abs"))
                fill("ml5")
                fill("ml6")
                act.wait_ge(*dve_of.at("ml.out", l))
                store(O["mC"][l], MCO)
                store(O["mCs"][l], MS)
                store(O["n"][l], n_out)
                head_norm("n1", slice(2, 4))
                nact.activation(GTH, GGS, ACT.Tanh, scale=0.5).then_inc(*act_of.step("gl.og"))
                act.wait_ge(*dve_of.at("gl.cum", l))
                nact.activation(GDX, LG[:, TP:T], ACT.Exp)
                nact.activation(GX, GX, ACT.Exp).then_inc(*act_of.step("gl.exp"))
                fill("gl1")
                act.wait_ge(*dve_of.at("gl.state", l))
                store(O["gS"][l], GSS[:, NC, :])
                fill("gl2")
                act.wait_ge(*dve_of.at("gl.dec", l))
                store(O["gSs"][l], GS)
                head_norm("n2", slice(4, 6))
                act.wait_ge(*dve_of.at("rw.mixed", l))
                store(O["shift"][l], shift_out)
                nact.activation(TH[0:32, :], U[0:32, TLO, :], ACT.Tanh)
                nact.activation(TH[64:128, :], U[64:128, TLO, :], ACT.Tanh, scale=0.5).then_inc(*act_of.step("rw.lora"))
                nact.activation(NRM[:, 0, :], U[:, TK, :], ACT.Square, scale=pc("kk", 0))
                nact.activation(NRM[:, 1, :], U[:, TK + 1, :], ACT.Square, scale=pc("kk", 1)).then_inc(*act_of.step("rw.ksq"))
                fill("rw1")
                act.wait_ge(*pe_of.at("rw.wa", l))
                for j in range(2):
                    nact.activation(LW[:, j, :], mW[:, j, 0:T], ACT.Tanh, scale=0.5, bias=hc("w0", j))
                    ins = nact.activation(AA[:, j, :], mW[:, 2 + j, 0:T], ACT.Tanh, scale=0.5, bias=hc("a0", j))
                ins.then_inc(*act_of.step("rw.wa"))
                act.wait_ge(*pe_of.at("rw.g", l))
                nact.activation(GG, mW[:, 0:2, 0:T], ACT.Copy).then_inc(*act_of.step("rw.g"))
                act.wait_ge(*dve_of.at("rw.ksum", l))
                nact.activation(NRM, NRM, ACT.Sqrt).then_inc(*act_of.step("rw.ksqrt"))
                fill("rw2")
                act.wait_ge(*dve_of.at("rw.cum", l))
                nact.activation(DW, LW[:, :, TP:T], ACT.Exp)
                nact.activation(EXPS[:, 0, :, :], RKV[:, :, 0:TP], ACT.Exp)
                nact.activation(EXPS[:, 1, :, :], RKV[:, :, 0:TP], ACT.Exp, scale=-1.0)
                nact.activation(EXPS[:, 2, :, :], BT, ACT.Exp).then_inc(*act_of.step("rw.exp"))
                fill("rw3")
                act.wait_ge(*dve_of.at("rw.dec", l))
                store(O["rSs"][l], DS)
                fill("rw4")
                fill("rw5")
                for g in range(2):
                    fill(f"g{g}a")
                    act.wait_ge(*pe_of.at("rw.p2", l, g))
                    nact.activation(P2, mW[:, 0, :], ACT.Copy)
                    nact.activation(P2T, mW[:, 1, :], ACT.Copy).then_inc(*act_of.step("rw.p2", g))
                    act.wait_ge(*pe_of.at("rw.p4", l, g))
                    nact.activation(P4, mW[:, 0, :], ACT.Copy)
                    nact.activation(P4T, mW[:, 1, :], ACT.Copy).then_inc(*act_of.step("rw.p4", g))
                    fill(f"g{g}b")
                    act.wait_ge(*pe_of.at("rw.p8", l, g))
                    nact.activation(P2, mW[:, 0, :], ACT.Copy).then_inc(*act_of.step("rw.p8", g))
                    act.wait_ge(*pe_of.at("rw.et", l, g))
                    nact.activation(ET, mW[:, 0, :], ACT.Copy).then_inc(*act_of.step("rw.et", g))
                    fill(f"g{g}c")
                    act.wait_ge(*pe_of.at("rw.wt", l, g))
                    nact.activation(WT, mW[:, 2, 0:256], ACT.Copy).then_inc(*act_of.step("rw.wt", g))
                    fill(f"g{g}d")
                fill("tail")
                act.wait_ge(*dve_of.at("rw.state", l, NC - 1))
                store(O["rS"][l], SS[:, :, NC, :])
                head_norm("n0", slice(0, 2))
                fill("end")

                def norm(i):
                    act.wait_ge(*dve_of.at("ln.centred", l, i))
                    nact.activation(V8[:, :, :], SQ8[:, :, :], ACT.Square).then_inc(*act_of.step("ln.sq", i))
                    act.wait_ge(*dve_of.at("ln.var", l, i))
                    nact.activation(V8[:, 1, :], V8[:, 0, :], ACT.Sqrt).then_inc(*act_of.step("ln.sqrt", i))
                    act.wait_ge(*dve_of.at("ln.scaled", l, i))
                    for j in range(KT):
                        ins = nact.activation(X[:, j, :], SQ8[:, j, :], ACT.Identity, scale=pc(f"ln{i + 1}g", j),
                                              bias=pc(f"ln{i + 1}b", j))
                    ins.then_inc(*act_of.step("ln.norm", i))

                norm(0)
                if l == 0:
                    for c in range(FC):
                        act.wait_ge(*pe_of.at("ff.up", l, c))
                        if c >= 2:
                            act.wait_ge(*dve_of.at("ff.hid", l, c - 2))
                        for q in range(2):
                            ins = nact.activation(FTH[:, c % 2, q, :], ff_acc(c, q), ACT.Tanh, scale=0.5)
                        ins.then_inc(*act_of.step("ff.tanh", c))
                else:
                    act.wait_ge(moe_setup_dve, 6)
                    for i in range(3):
                        n = P if i < 2 else TD
                        ins = nact.activation(TW[0:n, i, 0:1], TW[0:n, i, 0:1], ACT.Exp)
                    ins.then_inc(moe_setup_act, 1)
                    R = rounds_of(act)
                    halves_of = lambda x: (x[:, 0:4, :], x[:, 4:8, :])
                    for part in range(2):
                        act.wait_ge(gathered, part + 1)
                        nact.activation(halves_of(XE[:, 0, :, :])[part], mW[:, 3 - part, :], ACT.Copy).then_inc(gather_kept, 1)
                    with act.Fori(0, R * (NE // 2)) as m:
                        for u in range(2):
                            n = 2 * m + u
                            for c in range(FC):
                                if c in (7, 8):
                                    act.wait_ge(gathered, 2 * n + (c - 7 + 3))
                                    nact.activation(halves_of(XE[:, 1 - u, :, :])[c - 7], mW[:, 3 - (c - 7), :], ACT.Copy)\
                                        .then_inc(gather_kept, 1)
                                act.wait_ge(gate_done, n * FC + (c + 1 + FC))
                                if c >= 2:
                                    act.wait_ge(hidden, n * FC + (c - 1))
                                else:
                                    act.wait_ge(hidden, n * FC)
                                nact.activation(ETH[:, c % 2, :], mA[:, 2 * (c % 2), 0:256], ACT.Tanh, scale=0.5)\
                                    .then_inc(tanh_done, 1)
                            act.wait_ge(down_done, n * FC + 2 * FC)
                            nact.activation(YE, WF[:, 0:1024], ACT.Copy).then_inc(down_kept, 1)
                norm(1)


        def moe_vector(dve, v, link, linked):
            MUL, ADD, SUB, MAX, EQ = ALU.mult, ALU.add, ALU.subtract, ALU.max, ALU.is_equal
            v.memset(MASK, 0.0)
            v.memset(GATE, 0.0)
            v.memset(YE, 0.0)
            v.memset(PGT[:, 1, :], 0.0)
            link(v.memset(RANK, -1.0))
            link(v.tensor_scalar(SQ8[:, :, :], X[:, :, :], 2 * ALPHA, None, MUL))
            for i in range(3):
                n = P if i < 2 else TD
                dve.wait_ge(moe_setup_pe, i + 1)
                v.tensor_copy(XT[0:n, i, :], WF[0:n, 1024 * (i % 2):1024 * (i % 2) + 1024]).then_inc(moe_setup_dve, 1)
            dve.wait_ge(moe_setup_pe, 4)
            dve.wait_ge(router_in, 32)
            for i in range(3):
                n = P if i < 2 else TD
                link(v.tensor_tensor(LOG[0:n, i, :], mA[0:n, 0, NE * i:NE * i + NE], rbias[0:n, :], ADD))
                link(v.max(TOP[0:n, i, :], LOG[0:n, i, :]))
                link(v.max_index(TIX[0:n, i, :], TOP[0:n, i, :], LOG[0:n, i, :]))
                v.tensor_copy(IXF[0:n, i, :], TIX[0:n, i, :])
                ins = v.tensor_tensor(TW[0:n, i, 0:1], TOP[0:n, i, 1:2], TOP[0:n, i, 0:1], SUB)
                ins.then_inc(moe_setup_dve, 1)
            dve.wait_ge(moe_setup_act, 1)
            for i in range(3):
                n = P if i < 2 else TD
                link(v.tensor_scalar(TW[0:n, i, 1:2], TW[0:n, i, 0:1], 1.0, None, ADD))
                link(v.reciprocal(TW[0:n, i, 1:2], TW[0:n, i, 1:2]))
                link(v.tensor_tensor(TW[0:n, i, 0:1], TW[0:n, i, 0:1], TW[0:n, i, 1:2], MUL))
                i8 = C("iota8", NE, n)
                v.tensor_scalar(MASK[0:n, i, :], i8, IXF[0:n, i, 0:1], None, EQ)
                v.tensor_scalar(TMPE[0:n, i, :], i8, IXF[0:n, i, 1:2], None, EQ)
                v.tensor_scalar(GATE[0:n, i, 0:NE], i8, IXF[0:n, i, 0:1], TW[0:n, i, 1:2], EQ, MUL)
                link(v.tensor_scalar(LOG[0:n, i, :], i8, IXF[0:n, i, 1:2], TW[0:n, i, 0:1], EQ, MUL))
                v.tensor_tensor(GATE[0:n, i, 0:NE], GATE[0:n, i, 0:NE], LOG[0:n, i, :], ADD)
                v.tensor_tensor(MASK[0:n, i, :], MASK[0:n, i, :], TMPE[0:n, i, :], ADD).then_inc(moe_setup_dve, 1)
            dve.wait_ge(moe_setup_pe, 5)
            for i in range(3):
                n = P if i < 2 else TD
                ins = v.scalar_tensor_tensor(RANK[0:n, i, 0:NE], mA[0:n, 1, NE * i:NE * i + NE], 1.0, MASK[0:n, i, :], ADD, MUL)
            link(ins)
            for k in (1, 2):
                v.tensor_copy(GATE[:, :, NE * k:NE * k + NE], GATE[:, :, 0:NE])
            for i in range(3):
                n = P if i < 2 else TD
                link(v.tensor_scalar(RANK[0:n, i, 0:NE], RANK[0:n, i, 0:NE], -1.0, None, ADD))
            for k in (1, 2):
                v.tensor_scalar(RANK[:, :, NE * k:NE * k + NE], RANK[:, :, 0:NE], -float(P * k), None, ADD)
            link(v.tensor_reduce(CNT[0:1, 0:1], mA[0:1, 1, 3 * NE:4 * NE], AX_X, MAX))
            v.tensor_scalar(CNT[0:1, 1:2], CNT[0:1, 0:1], float(P), 1.0, ALU.is_gt, ADD)
            link(v.tensor_scalar(CNT[0:1, 2:3], CNT[0:1, 0:1], float(2 * P), None, ALU.is_gt))
            link(v.tensor_tensor(CNT[0:1, 1:2], CNT[0:1, 1:2], CNT[0:1, 2:3], ADD))
            v.tensor_copy(count_i[0:1, 0:1], CNT[0:1, 1:2]).then_inc(rounds_known, 1)
            R = rounds_of(dve)

            def place(n):
                dve.wait_ge(gathered, 2 * n)
                for i in range(3):
                    ins = v.tensor_scalar(PL[:, i, :], C("iota"), RANK[:, i, bass.ds(n, 1)], None, EQ)
                ins.then_inc(placed, 1)
                dve.wait_ge(placed, n + 1)
                for i in range(3):
                    ins = v.tensor_scalar(PG[:, i, :], PL[:, i, :], GATE[:, i, bass.ds(n, 1)], None, MUL)
                ins.then_inc(place_ready, 1)

            def turned(n, u):
                dve.wait_ge(placeT_pe, n + 1)
                v.tensor_copy(PGT[:, u, :], mW[:, 2, 0:T]).then_inc(placeT_ready, 1)

            def add(n, i):
                dve.wait_ge(scattered, n * KT + (i + 2))
                v.tensor_tensor(SQ8[:, i:i + 2, :], SQ8[:, i:i + 2, :], mW[:, 2:4, 0:T], ADD).then_inc(scatter_added, 1)

            dve.wait_ge(dve_link, linked[0])
            place(0)
            turned(0, 0)
            with dve.Fori(0, R * (NE // 2)) as m:
                for u in range(2):
                    n = 2 * m + u
                    for c in range(FC):
                        if 2 <= c < 6:
                            add(n, 2 * (c - 2))
                        if c == 5:
                            place(n + 1)
                        if c == 6:
                            dve.wait_ge(scatter_added, n * 4 + 4)
                            turned(n + 1, 1 - u)
                        dve.wait_ge(tanh_done, n * FC + (c + 1))
                        b = 2 * (c % 2)
                        v.scalar_tensor_tensor(ETH[:, c % 2, :], ETH[:, c % 2, :], 1.0, mA[:, b, 0:256], ADD, MUL)\
                            .then_inc(gated, 1)
                        dve.wait_ge(gated, n * FC + (c + 1))
                        dve.wait_ge(up_done, n * FC + (c + 1 + FC))
                        if c >= 2:
                            dve.wait_ge(down_done, n * FC + (c - 1 + FC))
                        else:
                            dve.wait_ge(down_done, n * FC + FC)
                        v.tensor_tensor(HE[:, c % 2, :], ETH[:, c % 2, :], mA[:, b + 1, 0:256], MUL).then_inc(hidden, 1)
            for i in range(0, KT, 2):
                add(R * NE, i)
            dve.wait_ge(scatter_added, R * (NE * 4) + 4)

        @block.vector
        def _(dve):
            v = nc.vector
            linked = [0]

            def link(ins):
                linked[0] += 1
                ins.then_inc(dve_link, 1)
                dve.wait_ge(dve_link, linked[0])

            def done(ins, name, i=0):
                ins.then_inc(*dve_of.step(name, i))
                dve.wait_ge(*dve_of.at(name, layer[0], i))

            layer = [0]
            MUL, ADD, SUB, MAX = ALU.mult, ALU.add, ALU.subtract, ALU.max

            def conv(dst, src, buf, w, b, n):
                for i in range(n):
                    ins = v.tensor_scalar(dst[:, i, :], src[:, i, :], pc(w, 4 * i + 3), pc(b, i), MUL, ADD)
                link(ins)
                for back in range(1, 4):
                    for i in range(n):
                        v.scalar_tensor_tensor(dst[:, i, back:TP], src[:, i, 0:TP - back], pc(w, 4 * i + 3 - back),
                                               dst[:, i, back:TP], MUL, ADD)
                        ins = v.scalar_tensor_tensor(dst[:, i, TP:T], buf[:, i, 3 - back, :], pc(w, 4 * i + 3 - back),
                                                     dst[:, i, TP:T], MUL, ADD)
                    if back < 3:
                        link(ins)
                return ins

            def last_rows(out, buf, src):
                v.tensor_copy(out[:, :, :, 0], src[:, :, TP - 3:TP])
                v.tensor_copy(out[:, :, 0:2, 1:9], buf[:, :, 1:3, :])
                return v.tensor_copy(out[:, :, 2, 1:9], src[:, :, TP:T])

            def over_v(x):
                return x.unsqueeze(3).broadcast_to([P, x.shape[1], TD, 64])

            def unit():
                return C("i64", 64).unsqueeze(1).unsqueeze(1).broadcast_to([P, 2, TD, 64])

            def w4(a, n=2):
                return WF[:, 512 * a:512 * (a + n)].rearrange("p (j b v) -> p j b v", j=n, b=TD)

            def streamed(kind, i, item):
                if kind != "up":
                    return
                l, (_, g, q2) = layer[0], item
                for q in range(2):
                    dt = 2 * q2 + q
                    dve.wait_ge(*pe_of.at("mg.up", l, i + q))
                    dve.wait_ge(*act_of.at("gate.tile", l, i + q))
                    dst = MG[:, dt, :] if g == RG else V8[:, 6 + q, :]
                    ins = v.scalar_tensor_tensor(dst, GT[:, (i + q) % GR, :], 1.0, acc("up", l, i + q), ADD, MUL)
                    ins.then_inc(*dve_of.step("mg.up", i + q))
                if g != RG:
                    dve.wait_ge(*dve_of.at("mg.up", l, i + 1))
                    ins = v.tensor_tensor(MG[:, 2 * q2:2 * q2 + 2, :], MG[:, 2 * q2:2 * q2 + 2, :], V8[:, 6:8, :], ADD)
                    if g == RW:
                        done(ins, "ms.sum", q2)
                    else:
                        link(ins)

            def head_norm(name, tiles, eps, centre=True):
                l = layer[0]
                if centre:
                    dve.wait_ge(*pe_of.at(f"{name}.mean", l))
                    done(v.tensor_tensor(OO[:, tiles, :], OO[:, tiles, :], mW[:, 0:2, 0:T], SUB), f"{name}.centred")
                else:
                    done(v.tensor_copy(OO[:, tiles, TP:T], GYD), f"{name}.centred")
                dve.wait_ge(*pe_of.at(f"{name}.var", l))
                done(v.tensor_scalar(OT[:, tiles, :], mW[:, 2:4, 0:T], eps, None, ADD), f"{name}.var")
                dve.wait_ge(*act_of.at(f"{name}.sqrt", l))
                link(v.reciprocal(OT[:, tiles, :], OT[:, tiles, :]))
                link(v.tensor_tensor(OO[:, tiles, :], OO[:, tiles, :], OT[:, tiles, :], MUL))

            dve.wait_ge(const_in, 16)
            for l in range(DEPTH):
                layer[0] = l
                fill = filler(streamed)
                dve.wait_ge(*loads(l, 10))
                done(v.tensor_scalar(half[:, :], par[:, :], 0.5, None, MUL), "u.half")
                if l:
                    dve.wait_ge(*act_of.at("ln.norm", l - 1, 1))
                link(v.memset(LG[:, T:2 * T], 0.0))
                v.tensor_copy(LG[:, 2 * T:2 * T + 2], par[:, PC["lam"]:PC["lam"] + 2])
                dve.wait_ge(*act_of.at("u.tile", l, 1))
                v.tensor_copy(LG[0:4, T:2 * T], U[32:36, TMI, :])
                dve.wait_ge(*pe_of.at("lg.alpha", l))
                done(v.tensor_scalar(LG[:, 0:T], mW[:, 0, 0:T], pc("gab"), None, ADD), "lg.in")
                dve.wait_ge(*act_of.at("u.tile", l, 5))
                fill("start")
                fill("alpha")
                done(conv(RC, U[:, TRX:TRX + 2, :], rbuf, "rcw", "rcb", 2), "rg.conv")
                last_rows(rconv_out, rbuf, U[:, TRX:TRX + 2, :])
                dve.wait_ge(*act_of.at("lg.exp", l))
                link(v.tensor_scalar(LY, LE, 2.0, None, ADD))
                link(v.reciprocal(LY, LY))
                link(v.tensor_tensor(LY, LE, LY, MUL))
                link(v.tensor_tensor(LZ, LY, LY, MUL))
                link(v.tensor_scalar(LE, LZ, 1.0 / 15, None, MUL))
                for k in (13, 11, 9, 7, 5, 3):
                    link(v.scalar_tensor_tensor(LE, LE, 1.0 / k, LZ, ADD, MUL))
                v.tensor_scalar(LG, LG, 0.0, None, ALU.min)
                link(v.scalar_tensor_tensor(LE, LE, 1.0, LY, ADD, MUL))
                link(v.scalar_tensor_tensor(LG, LE, -2.0, LG, MUL, ADD))
                link(v.tensor_scalar(lam4, LG[:, 2 * T:2 * T + 2], 4.0, None, MUL))
                dve.wait_ge(*act_of.at("rg.tanh", l))
                for j in range(2):
                    ins = v.tensor_scalar(RL[:, j, :], RT[:, j, :], 1.0, lam4[:, j:j + 1], ADD, MUL)
                done(ins, "rg.loga")
                v.scalar_tensor_tensor(RT[:, 2:4, :], RT[:, 2:4, :], 1.0, RC, ADD, MUL)
                link(v.tensor_scalar(RX, RX, 0.044715, 1.0, MUL, ADD))
                done(v.tensor_tensor(RX, RX, RGY, MUL), "rg.gelu_in")
                dve.wait_ge(*act_of.at("rg.exp", l))
                done(v.scalar_tensor_tensor(RE, RE, 1.0, RS, ADD, MUL), "rg.var")
                dve.wait_ge(*act_of.at("rg.sqrt", l))
                link(v.scalar_tensor_tensor(RS, RE, 0.5, RT[:, 2:4, :], MUL, MUL))
                for j in range(2):
                    v.tensor_tensor_scan(RH[:, j, 0:TP], RA[:, j, 0:TP], RS[:, j, 0:TP], 0.0, MUL, ADD)
                link(v.tensor_tensor(RH[:, :, TP:T], RA[:, :, TP:T], h0, MUL))
                link(v.tensor_tensor(RH[:, :, TP:T], RH[:, :, TP:T], RS[:, :, TP:T], ADD))
                v.tensor_copy(h_out, RH[:, :, TP - 1:T])
                dve.wait_ge(*act_of.at("rg.gelu", l))
                link(v.scalar_tensor_tensor(RX, RX, 1.0, RGY, ADD, MUL))
                done(v.scalar_tensor_tensor(RGY, RH, 0.5, RX, MUL, MUL), "rg.out")
                for point in ("rg1", "rg2", "rg3"):
                    fill(point)
                dve.wait_ge(*act_of.at("u.tile", l, 9))
                done(conv(CV, U[:, TMQ:TMQ + 4, :], mbuf, "mcw", "mcb", 4), "ml.conv")
                last_rows(mconv_out, mbuf, U[:, TMQ:TMQ + 4, :])
                f, ip = LG[0:4, T:2 * T], U[0:4, TMI, :]

                def row(k, lo=0, hi=TP):
                    return MR[0:4, k * T + lo:k * T + hi]

                v.tensor_tensor_scan(row(0), C("ones", TP, 4), f[:, 0:TP], 0.0, MUL, ADD)
                v.tensor_tensor_scan(row(1), f[:, 0:TP], ip[:, 0:TP], 0.0, ADD, MAX)
                link(v.tensor_tensor(row(5, 0, TD), f[:, TP:T], m0, ADD))
                link(v.tensor_tensor(row(1, TP, T), row(5, 0, TD), ip[:, TP:T], MAX))
                v.tensor_tensor(row(5, 0, TD), row(5, 0, TD), row(1, TP, T), SUB)
                v.tensor_tensor(row(5, TD, 2 * TD), ip[:, TP:T], row(1, TP, T), SUB)
                v.tensor_tensor(row(2), ip[:, 0:TP], row(0), SUB)
                v.tensor_tensor(row(3), row(0), row(1), SUB)
                done(v.tensor_copy(m_out, row(1, TP - 1, T)), "ml.rows")
                dve.wait_ge(*act_of.at("ml.silu", l))
                link(v.scalar_tensor_tensor(CV, TQ, 1.0, CV, ADD, MUL))
                v.tensor_scalar(CV[:, 0:2, :], CV[:, 0:2, :], 0.5, None, MUL)
                done(v.tensor_scalar(CV[:, 2:4, :], CV[:, 2:4, :], 0.5 * 64 ** -0.5, None, MUL), "ml.qk")
                dve.wait_ge(*act_of.at("ml.exps", l))
                done(v.tensor_copy(row(5, 2 * TD, 3 * TD), row(4, TP, T)), "ml.dec_rows")
                fill("ml1")
                fill("ml2")
                dve.wait_ge(*pe_of.at("ml.turn", l))
                v.tensor_copy(MVT, mW[:, 0, :].rearrange("p (a b) -> p a b", a=2))
                v.tensor_copy(MKT, mW[:, 1, :].rearrange("p (a b) -> p a b", a=2))
                v.tensor_copy(MGC, mW[:, 2, 0:8].rearrange("p (a b) -> p a b", a=2))
                done(v.tensor_copy(MDC, mW[:, 3, 0:48].rearrange("p (a b c) -> p a b c", a=2, b=3)), "ml.gcol")
                fill("ml3")
                for h in range(4):
                    dve.wait_ge(*pe_of.at("ml.qk", l, h))
                    dve.wait_ge(*act_of.at("ml.d", l, h))
                    v.tensor_tensor(MSD[:, h, :], mW[:, 2 + h % 2, 0:384], MD[:, h % 2, :], MUL)\
                        .then_inc(*dve_of.step("ml.sd", h))
                    v.tensor_scalar(MKT[:, 0, 64 * h:64 * h + 64], MKT[:, 0, 64 * h:64 * h + 64], MD[:, h % 2, 255:256], None, MUL)
                    done(v.tensor_scalar(MKT[:, 1, 64 * h:64 * h + 64], MKT[:, 1, 64 * h:64 * h + 64],
                                         MD[:, h % 2, 383:384], None, MUL), "ml.kw", h)
                fill("ml4")
                dve.wait_ge(*pe_of.at("ml.emb", l))
                link(v.tensor_tensor(MDEN[:, :, 0:TP], MDEN[:, :, 0:TP], mW[:, 2:4, 0:TP], MAX))
                link(v.reciprocal(MDEN[:, :, 0:TP], MDEN[:, :, 0:TP]))
                done(v.tensor_tensor(OO[:, 2:4, 0:TP], mW[:, 0:2, 0:TP], MDEN[:, :, 0:TP], MUL), "ml.h")
                fill("ml5")
                dve.wait_ge(*pe_of.at("ml.c", l))
                v.tensor_copy(n_out[:, :, 0], mW[:, 0, 0:256].rearrange("p (j v) -> p j v", j=2)[:, :, 64])
                done(v.tensor_copy(MCO, mW[:, 0, 0:256].rearrange("p (j v) -> p j v", j=2)[:, :, 0:64]), "ml.cout")
                qd, kd, vd = CV[:, 0:2, TP:T], CV[:, 2:4, TP:T], U[:, TMV:TMV + 2, TP:T]
                done(v.tensor_tensor(MX, unit(), over_v(vd), MUL), "ml.dv")
                link(v.tensor_tensor(MDEN[:, :, 0:TD], kd, MDC[:, :, 1, :], MUL))
                link(v.tensor_tensor(n_out[:, :, 1:9], n0, MDC[:, :, 0, :], MUL))
                link(v.tensor_tensor(n_out[:, :, 1:9], n_out[:, :, 1:9], MDEN[:, :, 0:TD], ADD))
                link(v.tensor_tensor(MDEN[:, :, TD:2 * TD], n_out[:, :, 1:9], qd, MUL))
                dve.wait_ge(*loads(l, 11))
                link(v.tensor_tensor(MS, MS, over_v(MDC[:, :, 0, :]), MUL))
                fill("ml6")
                dve.wait_ge(*pe_of.at("ml.dvb", l))
                link(v.tensor_tensor(MX, w4(0), over_v(MDEN[:, :, 0:TD]), MUL))
                link(v.tensor_tensor(MS, MS, MX, ADD))
                done(v.tensor_tensor(MX, MS, over_v(qd), MUL), "ml.dq")
                dve.wait_ge(*pe_of.at("ml.dnum", l))
                link(v.tensor_tensor(MX, w4(0), unit(), MUL))
                v.tensor_reduce(MDEN[:, :, 2 * TD:3 * TD], MX, AX_X, ADD)
                den = MDEN[:, :, 3 * TD:4 * TD]
                link(v.tensor_copy(den, mW[:, 2, 0:16].rearrange("p (j b) -> p j b", j=2)))
                link(v.scalar_tensor_tensor(den, den, -1.0, den, MUL, MAX))
                link(v.tensor_tensor(den, den, MDC[:, :, 2, :], MAX))
                link(v.reciprocal(den, den))
                done(v.tensor_tensor(OO[:, 2:4, TP:T], MDEN[:, :, 2 * TD:3 * TD], den, MUL), "ml.out")
                head_norm("n1", slice(2, 4), 1e-6)
                link(v.tensor_scalar(MOG, MOG, 0.5, 0.5, MUL, ADD))
                for j in range(2):
                    ins = v.scalar_tensor_tensor(MOG[:, j, :], OO[:, 2 + j, :], pc("mnw", j), MOG[:, j, :], MUL, MUL)
                done(ins, "ml.branch")
                la = LG[:, 0:T]

                def chunks4(x):
                    return x.rearrange("p (c t) -> p c t", c=NC)

                def at_chunk(x, t):
                    return chunks4(x)[:, :, t:t + 1].broadcast_to([P, NC, CH])

                dve.wait_ge(*act_of.at("gl.og", l))
                link(v.scalar_tensor_tensor(GGS, GTH, 1.0, GGS, ADD, MUL))
                v.tensor_scalar(GGS, GGS, 0.5, None, MUL)
                link(v.tensor_scalar(la, la, 1.0 / 16, None, MUL))
                dve.wait_ge(state_out, 16 * (12 * l + 7))
                link(v.tensor_tensor_scan(GB, C("reset", TP), la[:, 0:TP], 0.0, MUL, ADD))
                link(v.tensor_tensor(chunks4(GX[:, 0, :]), chunks4(GB), at_chunk(GB, CH // 2 - 1), SUB))
                v.tensor_scalar(GX[:, 1, :], GX[:, 0, :], -1.0, None, MUL)
                v.tensor_copy(GX[:, 2, :], GB)
                done(v.tensor_tensor(chunks4(GX[:, 3, :]), at_chunk(GB, CH - 1), chunks4(GB), SUB), "gl.cum")
                dve.wait_ge(*act_of.at("gl.exp", l))
                q, k = U[:, TGQ, :], U[:, TGK, :]
                v.scalar_tensor_tensor(GQ, q[:, 0:TP], 32 ** -0.5, GX[:, 0, :], MUL, MUL)
                v.tensor_tensor(GK, k[:, 0:TP], GX[:, 1, :], MUL)
                v.scalar_tensor_tensor(GQH, q[:, 0:TP], 32 ** -0.5, GX[:, 2, :], MUL, MUL)
                done(v.tensor_tensor(GKH, k[:, 0:TP], GX[:, 3, :], MUL), "gl.ops")
                dve.wait_ge(*pe_of.at("gl.turn", l))
                v.tensor_copy(GVT, mW[:, 0, :].rearrange("p (a b) -> p a b", a=2))
                done(v.tensor_copy(GKT, mW[:, 1, 0:256].rearrange("p (a b) -> p a b", a=2)), "gl.turned")
                dve.wait_ge(*pe_of.at("gl.attn", l))
                for c2 in range(2):
                    ins = v.tensor_tensor(GAT[:, c2, :].rearrange("p (h t) -> p h t", h=4),
                                          mW[:, :, P * c2:P * c2 + P],
                                          mid(con[:, CC["mk"] + P:CC["mk"] + 2 * P], 4), MUL)
                done(ins, "gl.attn")
                fill("gl1")
                dve.wait_ge(*pe_of.at("gl.kv", l))
                v.memset(GSS[:, 0, :], 0.0)
                for e in range(2):
                    ins = v.tensor_tensor(GKV[:, e::2, :], mW[:, e, :].rearrange("p (c n) -> p c n", c=2), mid(C("gm", 256), 2), MUL)
                link(ins)
                for c in range(NC):
                    ins = v.scalar_tensor_tensor(GSS[:, c + 1, :], GSS[:, c, :], GX[:, 2, CH * c + CH - 1:CH * c + CH],
                                                 GKV[:, c, :], MUL, ADD)
                    if c < NC - 1:
                        link(ins)
                done(ins, "gl.state")
                done(v.tensor_tensor(GXX, unit(), over_v(U[:, TGV:TGV + 2, TP:T]), MUL), "gl.dv")
                dve.wait_ge(*pe_of.at("gl.y", l))
                done(v.tensor_copy(OO[:, 4:6, 0:TP], mW[:, 2:4, 0:TP]), "gl.y")

                def over_gv(x):
                    return x.unsqueeze(2).broadcast_to([P, TD, 64])

                fill("gl2")
                dve.wait_ge(*loads(l, 12))
                link(v.tensor_tensor(GS, GS, over_gv(GDX), MUL))
                dve.wait_ge(*pe_of.at("gl.dvb", l))
                g3 = mW[:, 0, :].rearrange("p (b v) -> p b v", b=TD)
                link(v.tensor_tensor(GXX[:, 0, :, :], g3, over_gv(k[:, TP:T]), MUL))
                done(v.tensor_tensor(GS, GS, GXX[:, 0, :, :], ADD), "gl.dec")
                link(v.tensor_tensor(GXX[:, 0, :, :], GS, over_gv(q[:, TP:T]), MUL))
                done(v.tensor_scalar(GXX[:, 0, :, :], GXX[:, 0, :, :], 32 ** -0.5, None, MUL), "gl.dq")
                dve.wait_ge(*pe_of.at("gl.dy", l))
                link(v.tensor_tensor(GXX, w4(0), unit(), MUL))
                done(v.tensor_reduce(GYD, GXX, AX_X, ADD), "gl.out")
                head_norm("n2", slice(4, 6), 1e-6, centre=False)
                for j in range(2):
                    ins = v.scalar_tensor_tensor(GGS[:, j, :], OO[:, 4 + j, :], pc("gnw", j), GGS[:, j, :], MUL, MUL)
                done(ins, "gl.branch")
                um = U[:, 0:7, :]
                dve.wait_ge(state_out, 16 * (12 * l + 9))
                dve.wait_ge(*act_of.at("u.tile", l, NU - 1))
                v.tensor_copy(shift_out, U[:, 0:7, TP - 1:T])
                v.tensor_tensor(DL[:, :, 1:TP], um[:, :, 0:TP - 1], um[:, :, 1:TP], SUB)
                v.tensor_scalar(DL[:, :, 0:1], um[:, :, 0:1], -1.0, None, MUL)
                link(v.tensor_tensor(DL[:, :, TP:T], shift_in, um[:, :, TP:T], SUB))
                for i in range(7):
                    ins = v.scalar_tensor_tensor(um[:, i, :], DL[:, i, :], pc("mu", i), um[:, i, :], MUL, ADD)
                done(ins, "rw.mixed")
                rr, kx, vv = U[:, TR:TR + 2, :], U[:, TK:TK + 2, :], U[:, TV:TV + 2, :]
                dve.wait_ge(*act_of.at("rw.lora", l))
                done(v.tensor_scalar(TH[64:128, :], TH[64:128, :], 0.5, 0.5, MUL, ADD), "rw.sg")
                fill("rw1")
                dve.wait_ge(*act_of.at("rw.wa", l))
                v.tensor_scalar(LW, LW, 1.0, -0.5 * float(np.exp(-0.5)), ADD, MUL)
                link(v.tensor_scalar(AA, AA, 0.5, 0.5, MUL, ADD))
                for j in range(2):
                    ins = v.tensor_scalar(K4[:, j, :], AA[:, j, :], -1.0, pc("ka", j), ADD, MUL)
                link(ins)
                link(v.scalar_tensor_tensor(K4, K4, 1.0, kx, ADD, MUL))
                for j in range(2):
                    ins = v.scalar_tensor_tensor(RKV[:, j, :], rr[:, j, :], pc("rk", j), K4[:, j, :], MUL, MUL)
                done(ins, "rw.rk")
                dve.wait_ge(*pe_of.at("rw.ksum", l))
                done(v.tensor_scalar(NRM, mW[:, 2:4, 0:T], 1e-24, None, MAX), "rw.ksum")
                dve.wait_ge(*act_of.at("rw.ksqrt", l))
                link(v.reciprocal(NRM, NRM))
                for j in range(2):
                    ins = v.scalar_tensor_tensor(KKN[:, j, :], kx[:, j, :], pc("kk", j), NRM[:, j, :], MUL, MUL)
                link(ins)
                dve.wait_ge(*pe_of.at("rw.bonus", l))
                done(v.tensor_tensor(kx, mW[:, 0:2, 0:T], vv, MUL), "rw.bonus")
                for j in range(2):
                    ins = v.tensor_tensor_scan(RKV[:, j, 0:TP], C("reset", TP), LW[:, j, 0:TP], 0.0, MUL, ADD)
                link(ins)
                done(v.tensor_tensor(BT, RKV[:, :, 0:TP], LW[:, :, 0:TP], SUB), "rw.cum")
                fill("rw2")
                v.tensor_tensor(DKA, KKN[:, :, TP:T], AA[:, :, TP:T], MUL)
                link(v.tensor_tensor(DY, unit(), over_v(vv[:, :, TP:T]), MUL))
                dve.wait_ge(*loads(l, 13))
                done(v.tensor_tensor(DX, DS, over_v(KKN[:, :, TP:T]), MUL), "rw.dx")
                dve.wait_ge(*act_of.at("rw.exp", l))
                fill("rw3")
                link(v.tensor_tensor(DS, DS, over_v(DW), MUL))
                dve.wait_ge(*pe_of.at("rw.dsa", l))
                link(v.tensor_tensor(DX, w4(0), over_v(DKA), MUL))
                link(v.tensor_tensor(DS, DS, DX, SUB))
                link(v.tensor_tensor(DX, w4(2), over_v(K4[:, :, TP:T]), MUL))
                done(v.tensor_tensor(DS, DS, DX, ADD), "rw.dec")
                done(v.tensor_tensor(DX, DS, over_v(rr[:, :, TP:T]), MUL), "rw.dr")
                fill("rw4")
                dve.wait_ge(*pe_of.at("rw.dy", l))
                link(v.tensor_tensor(DX, w4(0), unit(), MUL))
                done(v.tensor_reduce(OO[:, 0:2, TP:T], DX, AX_X, ADD), "rw.dout")

                def halves(x):
                    return x[:, :, 0:TP].rearrange("p j (c t) -> p j c t", c=2)

                e_in, e_neg, e_ex = EXPS[:, 0, :, :], EXPS[:, 1, :, :], EXPS[:, 2, :, :]
                v.tensor_tensor(AR[:, :, :, 0, :], halves(KKN), halves(e_ex), MUL)
                v.tensor_tensor(AR[:, :, :, 1, :], halves(rr), halves(e_in), MUL)
                v.tensor_tensor(KTL, K4[:, :, 0:TP], e_neg, MUL)
                v.tensor_copy(PLAST, e_in.rearrange("p j (c t) -> p j c t", c=NC)[:, :, :, CH - 1])
                link(v.tensor_tensor(NRM[:, :, 0:TP], KKN[:, :, 0:TP], AA[:, :, 0:TP], MUL))
                link(v.tensor_tensor(BT, NRM[:, :, 0:TP], e_neg, MUL))
                for j in range(2):
                    plast = PLAST[:, j, :].unsqueeze(2).broadcast_to([P, NC, CH])
                    v.scalar_tensor_tensor(chunks4(B2[:, j, :]), chunks4(BT[:, j, :]), -1.0, plast, MUL, MUL)
                    ins = v.tensor_tensor(chunks4(K2[:, j, :]), chunks4(KTL[:, j, :]), plast, MUL)
                done(ins, "rw.ops")
                fill("rw5")
                dve.wait_ge(*pe_of.at("rw.turn", l))
                dve.wait_ge(state_out, 16 * (12 * l + 11))
                for i, dst in enumerate((ATK, BTK, KTK, VTK)):
                    v.tensor_copy(dst, mW[:, i, :].rearrange("p (a b) -> p a b", a=2))
                done(v.memset(SS[:, :, 0, :], 0.0), "rw.turned")
                for g in range(2):
                    dve.wait_ge(*pe_of.at("rw.bk", l, g))
                    if g:
                        dve.wait_ge(*pe_of.at("rw.y", l, 0))
                    v.tensor_tensor(NB, WF[:, 0:1024].rearrange("p (h t) -> p h t", h=4), mid(C("mb", 256), 4), MUL)
                    done(v.tensor_tensor(MKS, WF[:, 1024:2048].rearrange("p (h t) -> p h t", h=4), mid(C("mk", 256), 4), MUL),
                         "rw.bk", g)
                    dve.wait_ge(*pe_of.at("rw.l", l, g))
                    for e in range(2):
                        m2 = mW[:, e, 0:256].rearrange("p (h t) -> p h t", h=2)
                        v.tensor_tensor(ND[:, 2 * e:2 * e + 2, :], m2, mid(C("ml16"), 2), MUL)
                        v.tensor_tensor(NO[:, 2 * e:2 * e + 2, :], m2, mid(C("mlo"), 2), MUL)
                    v.tensor_tensor(QT, NB[:, :, 0:P], mid(C("ident"), 4), ADD)
                    v.tensor_copy(VW[:, 0, :], ATK[:, g, :])
                    done(v.tensor_copy(VW[:, 1, :], mW[:, 2, 0:256]), "rw.l", g)
                    fill(f"g{g}a")
                    b2 = mW[:, 2, :].rearrange("p (h t) -> p h t", h=4)
                    for k in range(3):
                        dve.wait_ge(*pe_of.at(("rw.p4", "rw.p8", "rw.q")[k], l, g))
                        done(v.tensor_tensor(QT, QT, b2, ADD), f"rw.q{k}", g)
                    fill(f"g{g}b")
                    b1 = mW[:, 1, :].rearrange("p (a n) -> p a n", a=2)
                    b3 = mW[:, 3, :].rearrange("p (a n) -> p a n", a=2)
                    dve.wait_ge(*pe_of.at("rw.et", l, g))
                    done(v.tensor_copy(VW, b1), "rw.v0", g)
                    for k in range(3):
                        dve.wait_ge(*pe_of.at("rw.e", l, 3 * g + k))
                        done(v.tensor_tensor(YW, (b3, b1, b3)[k], VW, ADD), "rw.e", 3 * g + k)
                    fill(f"g{g}c")
                    fill(f"g{g}d")
                    for c in (2 * g, 2 * g + 1):
                        q0 = 64 * (c % 2)
                        dve.wait_ge(*pe_of.at("rw.z", l, c))
                        done(v.tensor_tensor(ZZ[q0:q0 + 64, g, :].rearrange("p (j e d) -> p e j d", e=2, j=2),
                                             mW[q0:q0 + 64, 1:4:2, 0:128].rearrange("p e (j d) -> p e j d", j=2),
                                             YW[q0:q0 + 64, 1, :].rearrange("p (j e d) -> p e j d", e=2, j=2), ADD),
                             "rw.z", c)
                        dve.wait_ge(*pe_of.at("rw.s", l, c))
                        for j in range(2):
                            ins = v.scalar_tensor_tensor(SS[:, j, c + 1, :], SS[:, j, c, :], PLAST[:, j, c:c + 1],
                                                         mW[:, 0, 64 * j:64 * j + 64], MUL, ADD)
                        done(ins, "rw.state", c)
                    dve.wait_ge(*pe_of.at("rw.y", l, g))
                    done(v.tensor_copy(OO[:, 0:2, P * g:P * g + P], mW[:, 2, 0:256].rearrange("p (j t) -> p j t", j=2)),
                         "rw.y", g)
                fill("tail")
                head_norm("n0", slice(0, 2), 64e-5)
                for j in range(2):
                    ins = v.tensor_scalar(OO[:, j, :], OO[:, j, :], pc("lnw", j), pc("lnb", j), MUL, ADD)
                link(ins)
                link(v.tensor_tensor(OO[:, 0:2, :], OO[:, 0:2, :], kx, ADD))
                done(v.tensor_tensor(rr, OO[:, 0:2, :], GG, MUL), "rw.branch")
                fill("end")
                for i in range(KT):
                    dve.wait_ge(*pe_of.at("mg.out", l, i))
                    done(v.scalar_tensor_tensor(SQ8[:, i, :], X[:, i, :], 2 * ALPHA, acc("out", l, i), MUL, ADD), "mg.out", i)

                def norm(i):
                    dve.wait_ge(*pe_of.at("ln.mean", l, i))
                    done(v.tensor_tensor(SQ8[:, :, :], SQ8[:, :, :], mid(mW[:, 0, 0:T], KT), SUB), "ln.centred", i)
                    dve.wait_ge(*pe_of.at("ln.var", l, i))
                    done(v.tensor_scalar(V8[:, 0, :], mW[:, 1, 0:T], 4 * LN_EPS, None, ADD), "ln.var", i)
                    dve.wait_ge(*act_of.at("ln.sqrt", l, i))
                    link(v.reciprocal(V8[:, 1, :], V8[:, 1, :]))
                    done(v.tensor_tensor(SQ8[:, :, :], SQ8[:, :, :], mid(V8[:, 1, :], KT), MUL), "ln.scaled", i)
                    dve.wait_ge(*act_of.at("ln.norm", l, i))

                norm(0)
                if l == 0:
                    for c in range(FC):
                        dve.wait_ge(*act_of.at("ff.tanh", l, c))
                        for q in range(2):
                            ins = v.scalar_tensor_tensor(FTH[:, c % 2, q, :], FTH[:, c % 2, q, :], 1.0,
                                                         ff_acc(c, q), ADD, MUL)
                        link(ins)
                        for q in range(2):
                            ins = v.tensor_tensor(HS[:, 2 * c + q, :], FTH[:, c % 2, q, :], ff_acc(c, 2 + q), MUL)
                        done(ins, "ff.hid", c)
                    for i in range(KT):
                        dve.wait_ge(*pe_of.at("ff.down", l, i))
                        done(v.scalar_tensor_tensor(SQ8[:, i, :], X[:, i, :], 2 * ALPHA, acc("d", l, i), MUL, ADD),
                             "ff.down", i)
                else:
                    moe_vector(dve, v, link, linked)
                norm(1)


        def moe_tensor(pe, mm, turn):
            for i in range(3):
                n = P if i < 2 else TD
                if i == 2:
                    pe.wait_ge(moe_setup_dve, 1)
                for k in range(KT):
                    ins = nc.tensor.transpose(WF[0:n, 1024 * (i % 2) + P * k:1024 * (i % 2) + P * k + P],
                                              X[:, k, P * i:P * i + n], C("ident"))
                ins.then_inc(moe_setup_pe, 1)
            pe.wait_ge(router_in, 32)
            for i in range(3):
                n = P if i < 2 else TD
                for k in range(KT):
                    ins = mm(mA[0:n, 0, NE * i:NE * i + NE], X[:, k, P * i:P * i + n], router[:, k, :], k == 0, k == KT - 1)
            ins.then_inc(moe_setup_pe, 1)
            pe.wait_ge(moe_setup_dve, 9)
            ones = C("ones", P)
            for i in range(4):
                m = (P, P, TD, P)[i]
                for k in range(min(i + 1, 3)):
                    n = P if k < 2 else TD
                    w = C("tri", m, n) if k == i else con[0:n, CC["ones"]:CC["ones"] + m]
                    ins = mm(mA[0:m, 1, NE * i:NE * i + NE], w, MASK[0:n, k, :], k == 0, k == min(i, 2))
            ins.then_inc(moe_setup_pe, 1)
            R = rounds_of(pe)

            def turn_placement(n):
                pe.wait_ge(place_ready, n + 1)
                for i in range(3):
                    m = P if i < 2 else TD
                    ins = nc.tensor.transpose(mW[:, 2, P * i:P * i + m], PG[0:m, i, :], C("ident", m, m))
                ins.then_inc(placeT_pe, 1)

            def gather(n, part):
                if part:
                    pe.wait_ge(placeT_ready, n + 1)
                for k in range(4):
                    for i in range(3):
                        m = P if i < 2 else TD
                        f = P * (4 * part + k)
                        ins = mm(mW[:, 3 - part, P * k:P * k + P], XT[0:m, i, f:f + P], PL[0:m, i, :], i == 0, i == 2)
                ins.then_inc(gathered, 1)

            def scatter(n, i, placed):
                pe.wait_ge(scatter_added, n * 4 + i // 2)
                for q in range(2):
                    mm(mW[:, 2 + q, 0:T], YE[:, P * (i + q):P * (i + q) + P], placed).then_inc(scattered, 1)

            turn_placement(0)
            gather(0, 0)
            gather(0, 1)
            with pe.Fori(0, R * (NE // 2)) as m:

                def slot(i):
                    k = i % SLOTS
                    pe.wait_ge(slot_in[k], (m * per_pair[k] + (uses0[k] + i // SLOTS + 1)) * 16)
                    return ring[:, k, :]

                for u in range(2):
                    n = 2 * m + u

                    def down(c):
                        pe.wait_ge(hidden, n * FC + (c + 1))
                        if c == 0:
                            pe.wait_ge(down_kept, n)
                        wt = slot(3 * FC * u + 3 * c + 2)
                        for q in range(2):
                            for b in range(2):
                                ins = mm(mW[:, b, :], HE[:, c % 2, P * q:P * q + P], wt[:, D * q + 512 * b:D * q + 512 * b + 512],
                                         c == 0 and q == 0, c == FC - 1 and q == 1)
                        ins.then_inc(down_done, 1)

                    for c in range(FC):
                        if c == 0:
                            pe.wait_ge(gather_kept, 2 * n + 2)
                        if 2 <= c < 6:
                            pe.wait_ge(down_kept, n)
                            scatter(n, 2 * (c - 2), PGT[:, 1 - u, :])
                        if c == 6:
                            pe.wait_ge(scatter_added, n * 4 + 4)
                            turn_placement(n + 1)
                        if c in (7, 8):
                            gather(n + 1, c - 7)
                        b = 2 * (c % 2)
                        pe.wait_ge(hidden, n * FC + (c - 1 if c >= 2 else 0))
                        for part in range(2):
                            wt = slot(3 * FC * u + 3 * c + part).rearrange("p (k n) -> p k n", k=KT)
                            for q in range(2):
                                for k in range(KT):
                                    ins = mm(mA[:, b + part, P * q:P * q + P], wt[:, k, P * q:P * q + P], XE[:, u, k, :],
                                             k == 0, k == KT - 1)
                            ins.then_inc((gate_done, up_done)[part], 1)
                        if c:
                            down(c - 1)
                    down(FC - 1)
            pe.wait_ge(down_kept, R * NE)
            for i in range(0, KT, 2):
                scatter(R * NE, i, PGT[:, 1, :])
            pe.wait_ge(scatter_added, R * (NE * 4) + 4)

        @block.tensor
        def _(pe):
            ck = [0]

            def mm(out, w, x, start=True, stop=True):
                return nc.tensor.matmul(out, w, x, start=start, stop=stop, skip_group_check=True)

            def turn(out, x, n=P):
                return nc.tensor.transpose(out, x, C("ident", n, n))

            def chunk():
                i = ck[0]
                ck[0] += 1
                pe.wait_ge(slot_in[i % SLOTS], 16 * (i // SLOTS + 1))
                return ring[:, i % SLOTS, :].rearrange("p (k n) -> p k n", k=KT)

            def free(n):
                if n >= 4:
                    pe.wait_ge(*emptied[n - 4])

            def tile(kind, l, i, w, x):
                free(numbers[kind, l, i])
                for k, (wk, xk) in enumerate(zip(w, x)):
                    ins = mm(acc(kind, l, i), wk, xk, k == 0, k == len(w) - 1)
                return ins

            def pair(kind, name, l, i0, x, rows=KT):
                wt = chunk()
                for q in range(2):
                    tile(kind, l, i0 + q, [wt[:, k, P * q:P * q + P] for k in range(rows)], x)\
                        .then_inc(*pe_of.step(name, i0 + q))

            bo = C("bo")
            pe.wait_ge(const_in, 16)
            pe.wait_ge(x_in, 16)
            for l in range(DEPTH):
                xs = [X[:, k, :] for k in range(KT)]
                if l:
                    pe.wait_ge(*act_of.at("ln.norm", l - 1, 1))
                slot_of = {}

                def streamed(kind, i, item):
                    if kind == "u":
                        pair("u", "u.tile", l, i, xs)
                        return
                    _, g, q2 = item
                    if q2 == 0 and item[0] != "gate" and g not in slot_of:
                        slot_of[g] = chunk().rearrange("p k n -> p (k n)").rearrange("p (k n) -> p k n", k=2)
                        pe.wait_ge(*dve_of.at({RG: "rg.out", ML: "ml.branch", GL: "gl.branch", RW: "rw.branch"}[g], l))
                    if kind == "gate":
                        pair("gate", "gate.tile", l, i, xs)
                        return
                    for q in range(2):
                        f = P * (2 * q2 + q)
                        tile("up", l, i + q, [slot_of[g][:, k, f:f + P] for k in range(2)], [BRANCH[g][:, k, :] for k in range(2)])\
                            .then_inc(*pe_of.step("mg.up", i + q))

                fill = filler(streamed)

                def head_norm(name, tiles, centre=True):
                    if centre:
                        for k, i in enumerate(tiles):
                            ins = mm(mW[:, k, 0:T], C("bom"), OO[:, i, :])
                        ins.then_inc(*pe_of.step(f"{name}.mean"))
                    pe.wait_ge(*act_of.at(f"{name}.sq", l))
                    for k, i in enumerate(tiles):
                        ins = mm(mW[:, 2 + k, 0:T], C("bom"), OT[:, i, :])
                    ins.then_inc(*pe_of.step(f"{name}.var"))

                fill("start")
                pe.wait_ge(*loads(l, 10))
                pe.wait_ge(*act_of.at("u.tile", l, 1))
                mm(mW[:, 0, 0:T], alup[64:80, :], U[64:80, TMI, :]).then_inc(*pe_of.step("lg.alpha"))
                fill("alpha")
                pe.wait_ge(*dve_of.at("rg.conv", l))
                pe.wait_ge(*dve_of.at("lg.in", l))
                for j in range(4):
                    ins = mm(mW[:, j, 0:T], rgw[:, j, :], RC[:, j % 2, :])
                ins.then_inc(*pe_of.step("rg.gates"))
                for point in ("rg1", "rg2", "rg3", "ml1"):
                    fill(point)
                pe.wait_ge(*dve_of.at("ml.qk", l))
                pe.wait_ge(*act_of.at("rg.tanh", l))
                for j in range(2):
                    for c in range(2):
                        turn(mW[:, 0, 256 * c + P * j:256 * c + P * j + P], U[:, TMV + j, P * c:P * c + P])
                        turn(mW[:, 1, 256 * c + P * j:256 * c + P * j + P], CV[:, 2 + j, P * c:P * c + P])
                pe.wait_ge(*dve_of.at("ml.rows", l))
                pe.wait_ge(*act_of.at("ml.exps", l))
                for c in range(2):
                    turn(mW[:, 2, 4 * c:4 * c + 4], MR[0:4, 2 * T + P * c:2 * T + P * c + P], 4)
                fill("ml2")
                pe.wait_ge(*dve_of.at("ml.dec_rows", l))

                def spread(bank, at, width, x):
                    for h in range(4):
                        j, p0 = h // 2, 64 * (h % 2)
                        one = con[0:4, CC["ident"] + h:CC["ident"] + h + 1].broadcast_to([4, 64])
                        ins = mm(mW[p0:p0 + 64, bank(j), at(j):at(j) + width], one, x)
                    return ins

                ins = spread(lambda j: 3, lambda j: 24 * j, 24, MR[0:4, 5 * T:5 * T + 24])
                ins.then_inc(*pe_of.step("ml.turn"))
                fill("ml3")
                pe.wait_ge(*dve_of.at("ml.gcol", l))
                qq, kk = CV[:, 0:2, :], CV[:, 2:4, :]
                for h in range(4):
                    j, p0, b = h // 2, 64 * (h % 2), h % 2
                    if h >= 2:
                        pe.wait_ge(*act_of.at("ml.d", l, h - 2))
                    one = con[0:4, CC["ident"] + h:CC["ident"] + h + 1].broadcast_to([4, P])
                    mm(mW[:, b, 0:256], one, MR[0:4, 3 * T:3 * T + TP], True, False)
                    mm(mW[:, b, 0:128], C("ident"), C("neg"), False, True)
                    mm(mW[:, b, 256:384], one, MR[0:4, 3 * T + P:3 * T + TP], True, False)
                    mm(mW[:, b, 256:384], C("ident"), C("neg"), False, True).then_inc(*pe_of.step("ml.logd", h))
                    if h >= 2:
                        pe.wait_ge(*dve_of.at("ml.sd", l, h - 2))
                    mm(mW[:, 2 + b, 0:256], kk[p0:p0 + 64, j, 0:P], qq[p0:p0 + 64, j, 0:TP])
                    mm(mW[:, 2 + b, 256:384], kk[p0:p0 + 64, j, P:TP], qq[p0:p0 + 64, j, P:TP])\
                        .then_inc(*pe_of.step("ml.qk", h))
                fill("ml4")
                pe.wait_ge(*dve_of.at("ml.kw", l, 3))
                for h in range(4):
                    j, p0 = h // 2, 64 * (h % 2)
                    for b, lhs in ((j, None), (2 + j, C("ones", 64))):
                        for c in range(2):
                            w = MVT[:, c, 64 * h:64 * h + 64] if lhs is None else lhs
                            ins = mm(mW[p0:p0 + 64, b, P * c:TP], w, MSD[:, h, 256 * c:256 + P * c], c == 0, c == 1)
                ins.then_inc(*pe_of.step("ml.num"))
                pe.wait_ge(*act_of.at("ml.abs", l))
                ins = spread(lambda j: 2 + j, lambda j: 0, TP, MR[0:4, 4 * T:4 * T + TP])
                ins.then_inc(*pe_of.step("ml.emb"))
                fill("ml5")
                pe.wait_ge(*dve_of.at("ml.h", l))
                for h in range(4):
                    j, p0 = h // 2, 64 * (h % 2)
                    for c in range(2):
                        mm(mW[p0:p0 + 64, 0, P * j:P * j + 64], MKT[:, c, 64 * h:64 * h + 64], MVT[:, c, 64 * h:64 * h + 64],
                           c == 0, c == 1)
                    for c in range(2):
                        ins = mm(mW[p0:p0 + 64, 0, P * j + 64:P * j + 65], MKT[:, c, 64 * h:64 * h + 64], C("ones", 1),
                                 c == 0, c == 1)
                ins.then_inc(*pe_of.step("ml.c"))
                fill("ml6")
                pe.wait_ge(*dve_of.at("ml.cout", l))
                pe.wait_ge(*dve_of.at("ml.dv", l))
                for j in range(2):
                    ins = mm(mW[:, j, :], bo, MX[:, j, :, :].rearrange("p b v -> p (b v)"))
                ins.then_inc(*pe_of.step("ml.dvb"))
                pe.wait_ge(*dve_of.at("ml.dq", l))
                for j in range(2):
                    mm(mW[:, j, :], bo, MX[:, j, :, :].rearrange("p b v -> p (b v)"))
                for j in range(2):
                    ins = mm(mW[:, 2, 8 * j:8 * j + 8], bo, MDEN[:, j, TD:2 * TD])
                ins.then_inc(*pe_of.step("ml.dnum"))
                pe.wait_ge(*dve_of.at("ml.out", l))
                head_norm("n1", (2, 3))
                pe.wait_ge(*dve_of.at("gl.ops", l))
                for c in range(2):
                    for j in range(2):
                        turn(mW[:, 0, 256 * c + P * j:256 * c + P * j + P], U[:, TGV + j, P * c:P * c + P])
                    ins = turn(mW[:, 1, P * c:P * c + P], GKH[:, P * c:P * c + P])
                ins.then_inc(*pe_of.step("gl.turn"))
                pe.wait_ge(*dve_of.at("gl.turned", l))
                for h in range(4):
                    for c in range(2):
                        ins = mm(mW[:, h, P * c:P * c + P], GK[32 * h:32 * h + 32, P * c:P * c + P],
                                 GQ[32 * h:32 * h + 32, P * c:P * c + P])
                ins.then_inc(*pe_of.step("gl.attn"))
                fill("gl1")
                pe.wait_ge(*dve_of.at("gl.attn", l))
                for c in range(NC):
                    q0 = 64 * (c % 2)
                    ins = mm(mW[:, c % 2, 256 * (c // 2):256 * (c // 2) + 256], GKT[q0:q0 + 64, c // 2, :],
                             GVT[q0:q0 + 64, c // 2, :])
                ins.then_inc(*pe_of.step("gl.kv"))
                pe.wait_ge(*dve_of.at("gl.state", l))
                for j in range(2):
                    for c2 in range(2):
                        for h in (2 * j, 2 * j + 1):
                            p0 = 64 * (h % 2)
                            mm(mW[p0:p0 + 64, 2 + j, P * c2:P * c2 + P], GVT[:, c2, 64 * h:64 * h + 64],
                               GAT[:, c2, P * h:P * h + P], True, False)
                        for c in (2 * c2, 2 * c2 + 1):
                            ins = mm(mW[:, 2 + j, CH * c:CH * c + CH], GSS[:, c, P * j:P * j + P],
                                     GQH[:, CH * c:CH * c + CH], False, c % 2 == 1)
                ins.then_inc(*pe_of.step("gl.y"))
                pe.wait_ge(*dve_of.at("gl.dv", l))
                fill("gl2")
                for j in range(2):
                    ins = mm(mW[:, 0, :], con[:, CC["gv"] + P * j:CC["gv"] + P * j + P],
                             GXX[:, j, :, :].rearrange("p b v -> p (b v)"), j == 0, j == 1)
                ins.then_inc(*pe_of.step("gl.dvb"))
                pe.wait_ge(*dve_of.at("gl.dq", l))
                for j in range(2):
                    ins = mm(mW[:, j, :], con[:, CC["gy"] + P * j:CC["gy"] + P * j + P],
                             GXX[:, 0, :, :].rearrange("p b v -> p (b v)"))
                ins.then_inc(*pe_of.step("gl.dy"))
                pe.wait_ge(*dve_of.at("gl.out", l))
                head_norm("n2", (4, 5), centre=False)
                pe.wait_ge(*dve_of.at("n2.var", l))
                pe.wait_ge(*act_of.at("rw.lora", l))
                for j in range(2):
                    mm(mW[:, j, 0:T], lora[0:32, P * j:P * j + P], TH[0:32, :])
                    ins = mm(mW[:, 2 + j, 0:T], lora[32:64, P * j:P * j + P], U[32:64, TLO, :])
                ins.then_inc(*pe_of.step("rw.wa"))
                fill("rw1")
                pe.wait_ge(*act_of.at("rw.wa", l))
                pe.wait_ge(*dve_of.at("rw.sg", l))
                for j in range(2):
                    ins = mm(mW[:, j, 0:T], lora[64:128, P * j:P * j + P], TH[64:128, :])
                ins.then_inc(*pe_of.step("rw.g"))
                for j in range(2):
                    ins = mm(mW[:, 2 + j, 0:T], bo, NRM[:, j, :])
                ins.then_inc(*pe_of.step("rw.ksum"))
                pe.wait_ge(*act_of.at("rw.g", l))
                pe.wait_ge(*dve_of.at("rw.rk", l))
                for j in range(2):
                    ins = mm(mW[:, j, 0:T], bo, RKV[:, j, :])
                ins.then_inc(*pe_of.step("rw.bonus"))
                fill("rw2")
                pe.wait_ge(*dve_of.at("rw.dx", l))
                for j in range(2):
                    mm(mW[:, j, :], bo, DX[:, j, :, :].rearrange("p b v -> p (b v)"))
                for j in range(2):
                    ins = mm(mW[:, 2 + j, :], bo, DY[:, j, :, :].rearrange("p b v -> p (b v)"))
                ins.then_inc(*pe_of.step("rw.dsa"))
                fill("rw3")
                fill("rw4")
                pe.wait_ge(*dve_of.at("rw.dr", l))
                for j in range(2):
                    ins = mm(mW[:, j, :], bo, DX[:, j, :, :].rearrange("p b v -> p (b v)"))
                ins.then_inc(*pe_of.step("rw.dy"))
                fill("rw5")
                pe.wait_ge(*dve_of.at("rw.ops", l))
                for c in range(2):
                    for j in range(2):
                        o = slice(256 * c + P * j, 256 * c + P * j + P)
                        turn(mW[:, 0, o], AR[:, j, c, 0, :])
                        turn(mW[:, 1, o], B2[:, j, P * c:P * c + P])
                        turn(mW[:, 2, o], K2[:, j, P * c:P * c + P])
                        ins = turn(mW[:, 3, o], U[:, TV + j, P * c:P * c + P])
                ins.then_inc(*pe_of.step("rw.turn"))
                pe.wait_ge(*dve_of.at("rw.turned", l))
                for g in range(2):
                    tok = slice(P * g, P * g + P)
                    if g:
                        pe.wait_ge(*dve_of.at("rw.y", l, 0))
                    for h in (0, 2, 1, 3):
                        j, e, p0 = h // 2, h % 2, 64 * (h % 2)
                        ar2 = AR[p0:p0 + 64, j, g, :, :].rearrange("p a t -> p (a t)")
                        mm(mW[:, e, 256 * j:256 * j + 256], BT[p0:p0 + 64, j, tok], ar2)
                        ins = mm(mW[:, 2 + e, 256 * j:256 * j + 256], KTL[p0:p0 + 64, j, tok], ar2)
                    ins.then_inc(*pe_of.step("rw.bk", g))
                    pe.wait_ge(*dve_of.at("rw.bk", l, g))
                    for n in range(4):
                        e, j = divmod(n, 2)
                        h = 2 * j + e
                        mm(mW[:, e, P * j:P * j + P], AR[64 * e:64 * e + 64, j, g, 0, :], BT[64 * e:64 * e + 64, j, tok])
                        ins = mm(mW[:, 2, 64 * h:64 * h + 64], MKS[:, n, 0:P], VTK[:, g, 64 * h:64 * h + 64])
                    ins.then_inc(*pe_of.step("rw.l", g))
                    fill(f"g{g}a")
                    pe.wait_ge(*dve_of.at("rw.l", l, g))

                    def four(bank, w, x):
                        for n in range(4):
                            ins = mm(mW[:, bank, P * n:P * n + P], w[:, n, 0:P], x[:, n, 0:P])
                        return ins

                    def apply(bank, w, x):
                        for n in range(4):
                            h = 2 * (n % 2) + n // 2
                            o = mW[:, bank, :].rearrange("p (a n) -> p a n", a=2)[:, :, 64 * h:64 * h + 64]
                            ins = mm(o, w[:, n, 0:P], x[:, :, 64 * h:64 * h + 64])
                        return ins

                    four(0, NB, ND)
                    four(1, ND, NB).then_inc(*pe_of.step("rw.p2", g))
                    pe.wait_ge(*act_of.at("rw.p2", l, g))
                    four(0, P2T, P2)
                    four(1, P2, P2T)
                    four(2, P2, QT).then_inc(*pe_of.step("rw.p4", g))
                    fill(f"g{g}b")
                    pe.wait_ge(*act_of.at("rw.p4", l, g))
                    pe.wait_ge(*dve_of.at("rw.q0", l, g))
                    four(0, P4T, P4)
                    four(2, P4, QT).then_inc(*pe_of.step("rw.p8", g))
                    pe.wait_ge(*act_of.at("rw.p8", l, g))
                    pe.wait_ge(*dve_of.at("rw.q1", l, g))
                    four(2, P2, QT).then_inc(*pe_of.step("rw.q", g))
                    pe.wait_ge(*dve_of.at("rw.q2", l, g))
                    four(0, NO, QT)
                    apply(1, QT, VW).then_inc(*pe_of.step("rw.et", g))
                    fill(f"g{g}c")
                    pe.wait_ge(*act_of.at("rw.et", l, g))
                    pe.wait_ge(*dve_of.at("rw.v0", l, g))
                    for k in range(3):
                        apply((3, 1, 3)[k], ET, YW if k else VW).then_inc(*pe_of.step("rw.e", 3 * g + k))
                        pe.wait_ge(*dve_of.at("rw.e", l, 3 * g + k))
                    for j in range(2):
                        ins = turn(mW[:, 2, P * j:P * j + P], YW[:, 0, P * j:P * j + P])
                    ins.then_inc(*pe_of.step("rw.wt", g))
                    fill(f"g{g}d")
                    pe.wait_ge(*act_of.at("rw.wt", l, g))
                    for c in (2 * g, 2 * g + 1):
                        q0 = 64 * (c % 2)
                        if c:
                            pe.wait_ge(*dve_of.at("rw.state", l, c - 1))
                        for n in range(4):
                            e, j = divmod(n, 2)
                            ins = mm(mW[q0:q0 + 64, 1 + 2 * e, 64 * j:64 * j + 64], WT[64 * e:64 * e + 64, j, q0:q0 + 64],
                                     SS[64 * e:64 * e + 64, j, c, :])
                        ins.then_inc(*pe_of.step("rw.z", c))
                        pe.wait_ge(*dve_of.at("rw.z", l, c))
                        for h in range(4):
                            j, e = divmod(h, 2)
                            out = mW[64 * e:64 * e + 64, 0, 64 * j:64 * j + 64]
                            mm(out, KTK[q0:q0 + 64, g, 64 * h:64 * h + 64], VTK[q0:q0 + 64, g, 64 * h:64 * h + 64], True, False)
                            ins = mm(out, BTK[q0:q0 + 64, g, 64 * h:64 * h + 64],
                                     ZZ[q0:q0 + 64, g, 64 * h:64 * h + 64], False, True)
                        ins.then_inc(*pe_of.step("rw.s", c))
                    for h in range(4):
                        j, e = divmod(h, 2)
                        n, p0 = 2 * e + j, 64 * e
                        mm(mW[p0:p0 + 64, 2, P * j:P * j + P], VTK[:, g, 64 * h:64 * h + 64], MKS[:, n, P:2 * P], True, False)
                        mm(mW[p0:p0 + 64, 2, P * j:P * j + P], ZZ[:, g, 64 * h:64 * h + 64], NB[:, n, P:2 * P], False, False)
                        for c in (0, 1):
                            ins = mm(mW[p0:p0 + 64, 2, P * j + 64 * c:P * j + 64 * c + 64], SS[p0:p0 + 64, j, 2 * g + c, :],
                                     AR[p0:p0 + 64, j, g, 1, 64 * c:64 * c + 64], False, c == 1)
                    ins.then_inc(*pe_of.step("rw.y", g))
                fill("tail")
                pe.wait_ge(*dve_of.at("rw.y", l, 1))
                head_norm("n0", (0, 1))
                fill("end")
                pe.wait_ge(*dve_of.at("ms.sum", l, 3))
                for p in range(4):
                    pair("out", "mg.out", l, 2 * p, [MG[:, k, :] for k in range(KT)])

                def norm(i):
                    for k in range(KT):
                        ins = mm(mW[:, 0, 0:T], C("mean"), SQ8[:, k, :], k == 0, k == KT - 1)
                    ins.then_inc(*pe_of.step("ln.mean", i))
                    pe.wait_ge(*act_of.at("ln.sq", l, i))
                    for k in range(KT):
                        ins = mm(mW[:, 1, 0:T], C("mean"), V8[:, k, :], k == 0, k == KT - 1)
                    ins.then_inc(*pe_of.step("ln.var", i))
                    pe.wait_ge(*act_of.at("ln.norm", l, i))

                if l == DEPTH - 1:
                    pe.wait_ge(*pe_of.at("mg.out", l, KT - 1))
                    for done in (gate_done, up_done, down_done):
                        pe.sem_inc(done, FC)
                pe.wait_ge(*dve_of.at("mg.out", l, KT - 1))
                norm(0)
                if l == 0:
                    for c in range(FC):
                        if c >= 2:
                            pe.wait_ge(*dve_of.at("ff.hid", l, c - 2))
                        for part in range(2):
                            wt = chunk()
                            for q in range(2):
                                for k in range(KT):
                                    ins = mm(ff_acc(c, 2 * part + q), wt[:, k, P * q:P * q + P], xs[k], k == 0, k == KT - 1)
                        ins.then_inc(*pe_of.step("ff.up", c))
                    pe.wait_ge(*dve_of.at("ff.hid", l, FC - 1))
                    for p in range(4):
                        ws = [chunk() for _ in range(3)]
                        for q in range(2):
                            w = [ws[k // KT][:, k % KT, P * q:P * q + P] for k in range(FT)]
                            tile("d", l, 2 * p + q, w, [HS[:, k, :] for k in range(FT)])\
                                .then_inc(*pe_of.step("ff.down", 2 * p + q))
                    pe.wait_ge(*dve_of.at("ff.down", l, KT - 1))
                else:
                    moe_tensor(pe, mm, turn)
                norm(1)



IN_SIZES = (896, 512, 256, 256, 4, 4, 128, 128, 256, 256, 16, 256, 256, 4096)


def projection_columns():
    off = np.concatenate([[0], np.cumsum(IN_SIZES)])
    rw, mqk, mv, mo, mi, mf, gq, gk, gv, gg, ga, rx, ry, gates = off[:14]
    cols = -np.ones((NM, P), np.int64)
    r = np.arange(P)
    for first, n, tile in ((rw, 7, 0), (mqk, 4, TMQ), (mv, 2, TMV), (mo, 2, TMO), (gq, 1, TGQ), (gk, 1, TGK),
                           (gv, 2, TGV), (gg, 2, TGG), (rx, 2, TRX), (ry, 2, TRY)):
        for i in range(n):
            cols[tile + i] = first + P * i + r
    cols[TMI, 0:4] = mi + np.arange(4)
    cols[TMI, 32:36] = mf + np.arange(4)
    cols[TMI, 64:80] = ga + np.arange(16)
    for i in range(NG):
        cols[NU + i] = gates + P * i + r
    return cols


def slots_of(w):
    *lead, rows, n = w.shape
    w = w.reshape(*lead, KT, P, n // 256, 256)
    k = len(lead)
    w = np.moveaxis(w, (k + 2, k + 1, k, k + 3), (k, k + 1, k + 2, k + 3))
    return w.reshape(*lead, n // 256, P, SLOT)


def by_partition(a):
    return np.swapaxes(a.reshape(*a.shape[:-1], -1, P), -1, -2)


def lay_out(i):
    f = {k: np.asarray(x) for k, x in i.items()}
    L = DEPTH
    out = {"const": constants()}
    x = np.concatenate([f["x_prompt"].reshape(TP, D), f["x_sample"].reshape(TD, D)], 0)
    out["x"] = np.ascontiguousarray(x.T.reshape(KT, P, T).transpose(1, 0, 2))
    cols = projection_columns()
    flat, there = cols.reshape(-1), cols.reshape(-1) >= 0
    w = np.zeros((L, D, NM * P), np.float32)
    w[:, :, there] = f["w_in"][:, :, flat[there]]
    out["w_in"] = slots_of(w)
    bias = np.zeros((L, NM * P), np.float32)
    bias[:, there] = f["b_in"][:, flat[there]]
    out["w_branch"] = f["w_branch"].reshape(L, 4, 2, P, D).transpose(0, 1, 3, 2, 4).reshape(L, 4, P, SLOT)
    out["w_out"] = slots_of(f["w_out"])
    up = np.stack([slots_of(f["ffn_wg"])[0], slots_of(f["ffn_wu"])[0]], 1)
    out["ffn_up"] = up.reshape(2 * FC, P, SLOT)
    down = np.zeros((3 * KT * P, D), np.float32)
    down[:FF] = f["ffn_wd"][0]
    out["ffn_down"] = np.stack([slots_of(down[D * q:D * q + D]) for q in range(3)], 1).reshape(12, P, SLOT)
    moe = np.empty((NE, FC, 3, P, SLOT), np.float32)
    moe[:, :, 0] = slots_of(f["moe_wg"][0])
    moe[:, :, 1] = slots_of(f["moe_wu"][0])
    moe[:, :, 2] = f["moe_wd"][0].reshape(NE, FC, 2, P, D).transpose(0, 1, 3, 2, 4).reshape(NE, FC, P, SLOT)
    out["moe"] = moe.reshape(NE * FC * 3, P, SLOT)
    out["router"] = np.ascontiguousarray(f["moe_router"][0].reshape(KT, P, NE).transpose(1, 0, 2))
    out["rbias"] = np.ascontiguousarray(np.broadcast_to(f["moe_router_b"], (P, NE)))

    def taps(w, n):
        return w.reshape(L, 4, n, P).transpose(0, 3, 2, 1).reshape(L, P, 4 * n)

    par = {"bin": by_partition(bias[:, :NU * P]), "bgate": by_partition(bias[:, NU * P:]), "mcw": taps(f["mlstm_conv_w"], 4),
           "rcw": taps(f["rglru_conv_w"], 2), "rk": by_partition(f["rwkv_r_k"].reshape(L, -1))}
    for name, src in (("mu", "rwkv_mu"), ("w0", "rwkv_w0"), ("a0", "rwkv_a0"), ("kk", "rwkv_k_k"), ("ka", "rwkv_k_a"),
                      ("lnw", "rwkv_ln_w"), ("lnb", "rwkv_ln_b"), ("mcb", "mlstm_conv_b"), ("mnw", "mlstm_norm_w"),
                      ("gab", "gla_alpha_b"), ("gnw", "gla_norm_w"), ("rcb", "rglru_conv_b"), ("rba", "rglru_ba"),
                      ("rbx", "rglru_bx"), ("lam", "rglru_lambda"), ("ln1g", "ln1_g"), ("ln1b", "ln1_b"),
                      ("ln2g", "ln2_g"), ("ln2b", "ln2_b")):
        par[name] = by_partition(f[src])
    out["par"] = np.concatenate([par[name] for name in PC], -1)
    out["lora"] = np.concatenate([f["rwkv_w_up"], f["rwkv_a_up"], f["rwkv_g_up"]], 1)
    alup = np.zeros((L, P, P), np.float32)
    alup[:, 64:80] = f["gla_alpha_up"]
    out["alup"] = alup
    rgw = np.zeros((L, P, 4, P), np.float32)
    for k, name in enumerate(("rglru_wa", "rglru_wx")):
        for j in range(2):
            for e in range(2):
                rgw[:, 64 * e:64 * e + 64, 2 * k + j, 64 * e:64 * e + 64] = f[name][:, 2 * j + e]
    out["rgw"] = rgw
    t = np.transpose
    out["shift"] = t(f["state_rwkv_shift"].reshape(L, TD, 7, P), (0, 3, 2, 1))
    out["mconv"] = t(f["state_mlstm_conv"].reshape(L, TD, 3, 4, P), (0, 4, 3, 2, 1))
    out["rconv"] = t(f["state_rglru_conv"].reshape(L, TD, 3, 2, P), (0, 4, 3, 2, 1))
    out["h0"] = t(f["state_rglru_h"].reshape(L, TD, 2, P), (0, 3, 2, 1))
    out["n0"] = t(f["state_mlstm_n"].reshape(L, TD, 2, P), (0, 3, 2, 1))
    out["m0"] = t(f["state_mlstm_m"], (0, 2, 1))
    for name, src in (("mC", "state_mlstm_C"), ("rS", "state_rwkv_S")):
        out[name] = t(f[src].reshape(L, TD, 2, 2, 64, 64), (0, 3, 5, 2, 1, 4)).reshape(L, P, 2, TD, 64)
    out["gS"] = t(f["state_gla_S"], (0, 2, 3, 1, 4)).reshape(L, P, TD, 64)
    return {k: np.ascontiguousarray(x) for k, x in out.items()}


OUTS = {"y": (P, KT, T), "h": (DEPTH, P, 2, 9), "rconv": (DEPTH, P, 2, 3, 9), "shift": (DEPTH, P, 7, 9), "m": (DEPTH, 4, 9),
        "mconv": (DEPTH, P, 4, 3, 9), "mC": (DEPTH, P, 2, 64), "mCs": (DEPTH, P, 2, TD, 64), "n": (DEPTH, P, 2, 9),
        "gSs": (DEPTH, P, TD, 64), "gS": (DEPTH, P, 256), "rSs": (DEPTH, P, 2, TD, 64), "rS": (DEPTH, P, 2, 64)}


def take_out(o):
    L, t = DEPTH, np.transpose
    y = t(o["y"], (2, 1, 0)).reshape(T, D)
    cols = {"shift": t(o["shift"], (0, 3, 2, 1)).reshape(L, 9, 896), "h": t(o["h"], (0, 3, 2, 1)).reshape(L, 9, 256),
            "n": t(o["n"], (0, 3, 2, 1)).reshape(L, 9, 4, 64), "m": t(o["m"], (0, 2, 1)),
            "mconv": t(o["mconv"], (0, 4, 3, 2, 1)).reshape(L, 9, 3, 512),
            "rconv": t(o["rconv"], (0, 4, 3, 2, 1)).reshape(L, 9, 3, 256)}

    def square(x, n):
        return t(x.reshape(L, 2, 64, 2, n, 64), (0, 4, 3, 1, 5, 2)).reshape(L, n, 4, 64, 64)

    def states(lo, hi, rS, mC, gS):
        c = {k: np.ascontiguousarray(a[:, lo:hi]) for k, a in cols.items()}
        return c["shift"], rS, c["mconv"], mC, c["n"], c["m"], gS, c["rconv"], c["h"]

    gp = o["gS"].reshape(L, 4, 32, 4, 64)
    gp = np.stack([gp[:, h, :, h] for h in range(4)], 1)[:, None]
    gs = t(o["gSs"].reshape(L, 4, 32, TD, 64), (0, 3, 1, 2, 4))
    prompt = states(0, 1, square(o["rS"], 1), square(o["mC"], 1), gp)
    sample = states(1, 9, square(o["rSs"], TD), square(o["mCs"], TD), gs)
    out = (y[None, :TP], y[TP:, None]) + prompt + sample
    return tuple(np.ascontiguousarray(a) for a in out)


def kernel(**inputs):
    import concourse.bacc as _bacc
    from concourse.bass_utils import run_bass_kernel_spmd as _run

    nc = _bacc.Bacc("TRN2", target_bir_lowering=False, num_devices=1)
    arrays = {f"in_{k}_dram": a for k, a in lay_out(inputs).items()}
    A = {k[3:-5]: nc.dram_tensor(k, a.shape, F32, kind="ExternalInput").ap() for k, a in arrays.items()}
    O = {k: nc.dram_tensor(f"out_{k}_dram", shape, F32, kind="ExternalOutput").ap() for k, shape in OUTS.items()}
    program(nc, A, O)
    r = _run(nc, [arrays], core_ids=[0])
    return take_out({k: r.results[0][f"out_{k}_dram"] for k in OUTS})
```

```python
from contextlib import ExitStack

import numpy as np

import concourse.bass as bass
from concourse import mybir

F32 = mybir.dt.float32
F32R = mybir.dt.float32r
I32 = mybir.dt.int32
U32 = mybir.dt.uint32
ALU = mybir.AluOpType
ACT = mybir.ActivationFunctionType
AX_X = mybir.AxisListType.X

P = 128
D = 1024
KT = D // P
DEPTH = 2
TP, TD = 256, 8
T = TP + TD
FF = 2816
NE = 8
CH = 64
NC = TP // CH
ALPHA = (2 * DEPTH) ** 0.25
LN_EPS = 1e-5

TR, TK, TV, TLO, TMI, TMQ, TMK, TMV, TGQ, TGK, TMO, TGV, TGG, TRX, TRY = 0, 2, 4, 6, 7, 8, 10, 12, 14, 15, 16, 18, 20, 22, 24
NU = 26
NG = 32
NM = NU + NG
SLOTS = 9
MSLOTS = 8
SLOT = 2048
GR = 8
RG, ML, GL, RW = 3, 1, 2, 0
FC = FF // 256
FT = FF // P

STREAM = ([("u", i) for i in (TMI - 1, TRX, TRY, TMQ, TMK, TMV, TMO, TGQ, TGV, TGG, TR, TK, TV)]
          + [("merge", g, q) for g in (RG, ML, GL) for q in range(4)]
          + [("gate", RW, q) for q in range(4)] + [("up", RW, q) for q in range(4)])
FILL = {"start": 3, "alpha": 1, "rg1": 2, "rg2": 1, "rg3": 2, "ml1": 2, "ml2": 2, "ml3": 1, "ml4": 1, "ml5": 1, "ml6": 1,
        "gl1": 1, "gl2": 1, "rw1": 0, "rw2": 1, "rw3": 0, "rw4": 1, "rw5": 3,
        "g0a": 1, "g0b": 0, "g0c": 1, "g0d": 0, "g1a": 1, "g1b": 0, "g1c": 1, "g1d": 0, "tail": 1, "end": 4}
assert sum(FILL.values()) == len(STREAM)

PAIR = 6 * FC
_short = -PAIR % MSLOTS
SLOT_OF = ([k for _ in range((PAIR - _short * (MSLOTS - 1)) // MSLOTS) for k in range(MSLOTS)]
           + [k for _ in range(_short) for k in range(MSLOTS - 1)])
assert len(SLOT_OF) == PAIR


def last_use(i):
    return max(j for j in range(i - PAIR, i) if SLOT_OF[j % PAIR] == SLOT_OF[i % PAIR])


PC = {}


def _cols():
    at = 0
    for name, n in (("bin", NU), ("bgate", NG), ("mu", 7), ("w0", 2), ("a0", 2), ("kk", 2), ("ka", 2), ("rk", 2),
                    ("lnw", 2), ("lnb", 2), ("mcw", 16), ("mcb", 4), ("mnw", 2), ("gab", 1), ("gnw", 2),
                    ("rcw", 8), ("rcb", 2), ("rba", 2), ("rbx", 2), ("lam", 2),
                    ("ln1g", KT), ("ln1b", KT), ("ln2g", KT), ("ln2b", KT)):
        PC[name] = at
        at += n
    return at


NPAR = _cols()

CC = {}


def _const_cols():
    at = 0
    for name, n in (("ident", P), ("bo", P), ("bom", P), ("mean", P), ("mb", 256), ("mk", 256), ("ml16", P), ("mlo", P),
                    ("i64", 64), ("neg", P), ("gv", 256), ("gy", 256), ("gm", 256), ("reset", TP), ("ones", TP),
                    ("tri", P), ("iota", P), ("iota8", NE), ("eps", 1)):
        CC[name] = at
        at += n
    return at


NCON = _const_cols()


def constants():
    c = np.zeros((P, NCON), np.float32)
    i = np.arange(P)
    s, t = i[:, None], i[None, :]

    def put(name, m):
        c[:m.shape[0], CC[name]:CC[name] + m.shape[1]] = m

    b64, b16 = s // 64 == t // 64, s // 16 == t // 16
    put("ident", np.eye(P))
    put("bo", b64 * 1.0)
    put("bom", b64 / 64.0)
    put("eps", np.full((P, 1), 4 * LN_EPS))
    put("mean", np.full((P, P), 1.0 / D))
    put("mb", np.concatenate([-1.0 * (b16 & (s < t)), -1.0 * (b64 & (s <= t))], 1))
    put("mk", np.concatenate([1.0 * (b64 & (s < t)), 1.0 * (b64 & (s <= t))], 1))
    put("ml16", -1.0 * (b16 & (t < s)))
    put("mlo", -1.0 * (b64 & ~b16 & (t < s)))
    put("i64", 1.0 * (i[:, None] % 64 == np.arange(64)[None]))
    put("neg", np.where(s <= t, 0.0, -1e30))
    put("gv", np.concatenate([1.0 * (2 * j + s // 64 == t // 32) for j in range(2)], 1))
    put("gy", np.concatenate([1.0 * (2 * j + t // 64 == s // 32) for j in range(2)], 1))
    put("gm", 1.0 * (i[:, None] // 32 == np.arange(256)[None] // 64))
    put("reset", np.tile(1.0 * (np.arange(TP) % CH != 0), (P, 1)))
    put("ones", np.ones((P, TP)))
    put("tri", 1.0 * (s < t))
    put("iota", np.tile(np.arange(P), (P, 1)))
    put("iota8", np.tile(np.arange(NE), (P, 1)))
    return c




class Steps:

    def __init__(self, nc, ctx, engine, table):
        self.engine = engine
        self.first, self.count, self.sem, self.fired, self.seen = {}, {}, {}, {}, {}
        for name, n in table:
            g = self.group(name, n)
            if g not in self.sem:
                self.sem[g] = ctx.enter_context(nc.semaphore(f"{g}_{engine}"))
                self.count[g] = self.fired[g] = 0
            self.first[name] = g, self.count[g]
            self.count[g] += n

    @staticmethod
    def group(name, n):
        return name.split(".")[0] if n == 1 else name

    def step(self, name, i=0):
        if RECORD:
            self.seen[name] = self.seen.get(name, 0) + 1
            return self.scratch, 1
        g, first = self.first[name]
        assert self.fired[g] % self.count[g] == first + i, (self.engine, name, i, self.fired[g], self.count[g], first)
        self.fired[g] += 1
        return self.sem[g], 1

    def at(self, name, l, i=0):
        if RECORD:
            return self.scratch, 1
        g, first = self.first[name]
        return self.sem[g], l * self.count[g] + first + i + 1


RECORD = False
PE_TABLE = (
    ("u.tile", 26), ("lg.alpha", 1), ("rg.gates", 1), ("ml.turn", 1), ("gate.tile", 32),
    ("mg.up", 32), ("ml.logd", 4), ("ml.qk", 4), ("ml.num", 1), ("ml.emb", 1),
    ("ml.c", 1), ("ml.dvb", 1), ("ml.dnum", 1), ("n1.mean", 1), ("n1.var", 1),
    ("gl.turn", 1), ("gl.attn", 1), ("gl.kv", 1), ("gl.y", 1), ("gl.dvb", 1),
    ("gl.dy", 1), ("n2.var", 1), ("rw.wa", 1), ("rw.g", 1), ("rw.ksum", 1),
    ("rw.bonus", 1), ("rw.dsa", 1), ("rw.dy", 1), ("rw.turn", 1), ("rw.bk", 2),
    ("rw.l", 2), ("rw.p2", 2), ("rw.p4", 2), ("rw.p8", 2), ("rw.q", 2),
    ("rw.et", 2), ("rw.e", 6), ("rw.wt", 2), ("rw.z", 4), ("rw.s", 4),
    ("rw.y", 2), ("n0.mean", 1), ("n0.var", 1), ("mg.out", 8), ("ln.mean", 2),
    ("ln.var", 2), ("ff.part", 30), ("ff.down", 8),
)
ACT_TABLE = (
    ("u.tile", 26), ("rg.tanh", 1), ("lg.exp", 1), ("rg.exp", 1), ("rg.gelu", 1),
    ("rg.sqrt", 1), ("ml.silu", 1), ("ml.exps", 1), ("ml.og", 1), ("gate.tile", 32),
    ("ml.d", 4), ("ml.abs", 1), ("n1.sq", 1), ("n1.sqrt", 1), ("gl.og", 1),
    ("gl.exp", 1), ("n2.sq", 1), ("n2.sqrt", 1), ("rw.lora", 1), ("rw.ksq", 1),
    ("rw.wa", 1), ("rw.g", 1), ("rw.ksqrt", 1), ("rw.exp", 1), ("rw.p2", 2),
    ("rw.p4", 2), ("rw.p8", 2), ("rw.et", 2), ("rw.wt", 2), ("n0.sq", 1),
    ("n0.sqrt", 1), ("ff.hi", 34), ("ln.sq", 4), ("ln.sqrt", 2), ("ln.half", 2),
    ("ff.xh", 2), ("ln.norm", 2), ("ff.tanh", 11),
)
DVE_TABLE = (
    ("u.half", 1), ("lg.in", 1), ("rg.conv", 1), ("rg.loga", 1), ("rg.gelu_in", 1),
    ("rg.var", 1), ("rg.out", 1), ("ml.conv", 1), ("ml.rows", 1), ("ml.qk", 1),
    ("ml.dec_rows", 1), ("ml.gcol", 1), ("mg.up", 32), ("ml.sd", 4), ("ml.kw", 4),
    ("ml.h", 1), ("ml.cout", 1), ("ml.dv", 1), ("ml.dq", 1), ("ml.out", 1),
    ("n1.centred", 1), ("gl.cum", 1), ("n1.var", 1), ("ml.branch", 1), ("gl.ops", 1),
    ("gl.turned", 1), ("gl.attn", 1), ("gl.state", 1), ("gl.dv", 1), ("gl.y", 1),
    ("rw.mixed", 1), ("gl.dec", 1), ("gl.dq", 1), ("gl.out", 1), ("n2.centred", 1),
    ("n2.var", 1), ("gl.branch", 1), ("rw.sg", 1), ("rw.rk", 1), ("rw.ksum", 1),
    ("rw.bonus", 1), ("rw.cum", 1), ("rw.dx", 1), ("rw.dec", 1), ("rw.dr", 1),
    ("rw.dout", 1), ("rw.ops", 1), ("rw.turned", 1), ("rw.bk", 2), ("rw.l", 2),
    ("rw.q0", 2), ("rw.q1", 2), ("rw.q2", 2), ("rw.v0", 2), ("rw.e", 6),
    ("rw.z", 4), ("rw.state", 4), ("rw.y", 2), ("n0.centred", 1), ("n0.var", 1),
    ("rw.branch", 1), ("ms.sum", 4), ("mg.out", 8), ("ln.centred", 4), ("ff.lo", 34),
    ("ln.scaled", 4), ("ff.xl", 2), ("ff.hid", 11), ("ff.hl", 11), ("ff.down", 8),
)

def col(ap, n):
    return ap.unsqueeze(2).broadcast_to([ap.shape[0], ap.shape[1], n])


def mid(ap, n):
    return ap.unsqueeze(1).broadcast_to([ap.shape[0], n, ap.shape[1]])


def program(nc, A, O):
    with ExitStack() as ctx:
        def sb(name, shape, dt=F32):
            return ctx.enter_context(nc.sbuf_tensor(name, shape, dt))

        def sem(name):
            return ctx.enter_context(nc.semaphore(name))

        pe_of = Steps(nc, ctx, "pe", PE_TABLE)
        act_of = Steps(nc, ctx, "act", ACT_TABLE)
        dve_of = Steps(nc, ctx, "dve", DVE_TABLE)
        if RECORD:
            for st in (pe_of, act_of, dve_of):
                st.scratch = sem(f"rec_{st.engine}")
        act_link, dve_link = sem("act_link"), sem("dve_link")
        const_in, router_in, x_in = sem("const_in"), sem("router_in"), sem("x_in")
        par_in, layer_in, state_out = sem("par_in"), sem("layer_in"), sem("state_out")
        slot_in = [sem(f"slot_in{i}") for i in range(SLOTS)]
        moe_setup_pe, moe_setup_dve, moe_setup_act = sem("moe_setup_pe"), sem("moe_setup_dve"), sem("moe_setup_act")
        rounds_known = sem("rounds_known")
        place_ready, placeT_pe, placeT_ready = sem("place_ready"), sem("placeT_pe"), sem("placeT_ready")
        gathered, gather_kept = sem("gathered"), sem("gather_kept")
        gather_split = sem("gather_split")
        split0, split1, down_done = sem("split0"), sem("split1"), sem("down_done")
        rounded0, rounded1, in0_done, in1_done = sem("rounded0"), sem("rounded1"), sem("in0_done"), sem("in1_done")
        tanh_done, hidden, down_kept = sem("tanh_done"), sem("hidden"), sem("down_kept")
        hidden_turned, turned_kept = sem("hidden_turned"), sem("turned_kept")
        scattered, scatter_added = sem("scattered"), sem("scatter_added")
        placed, gated, round_over = sem("placed"), sem("gated"), sem("round_over")

        ring = sb("ring", [P, MSLOTS, SLOT])
        con = sb("con", [P, NCON])
        par = sb("par", [P, NPAR])
        half = sb("half", [P, NPAR])
        lora = sb("lora", [P, 256])
        alup = sb("alup", [P, P])
        rgw = sb("rgw", [P, 4, P])
        X = sb("X", [P, KT, T])
        V8 = sb("V8", [P, KT, T])
        small = sb("small", [P, 612])
        count_i = sb("count_i", [1, 4], I32)
        with ExitStack() as until_experts:
            SQ8 = until_experts.enter_context(nc.sbuf_tensor("SQ8", [P, KT, T], F32))
            RTAIL = until_experts.enter_context(nc.sbuf_tensor("RTAIL", [P, SLOTS - MSLOTS, SLOT], F32))
            BIG = until_experts.enter_context(nc.sbuf_tensor("BIG", [P, (NU + GR + KT) * T], F32))
            SCR = until_experts.enter_context(nc.sbuf_tensor("SCR", [P, 12416], F32))
        with ExitStack() as until_layer_1:
            def split_pair(name, shape):
                return [until_layer_1.enter_context(nc.sbuf_tensor(name + part, shape, F32R)) for part in "HL"]

            XH = until_layer_1.enter_context(nc.sbuf_tensor("XH", [P, KT, T], F32R))
            until_layer_1.enter_context(nc.sbuf_tensor("ring_end", [P, SLOTS - MSLOTS, SLOT], F32))
            XL = until_layer_1.enter_context(nc.sbuf_tensor("XL", [P, KT, T], F32R))
            HH, HL = split_pair("F", [P, FT, T])
            FWH, FWL = split_pair("FW", [P, 2, SLOT])
        sb("SQ8_again", [P, KT, T])
        WH, WL = sb("WH", [P, 2, SLOT], F32R), sb("WL", [P, 2, SLOT], F32R)
        XEH, XEL = sb("XEH", [P, 2, KT, P], F32R), sb("XEL", [P, 2, KT, P], F32R)

        def ring_slot(k):
            return ring[:, k, :] if k < MSLOTS else RTAIL[:, k - MSLOTS, :]

        U = BIG[:, 0:NU * T].rearrange("p (n t) -> p n t", t=T)
        GT = BIG[:, NU * T:(NU + GR) * T].rearrange("p (n t) -> p n t", t=T)
        MG = BIG[:, (NU + GR) * T:(NU + GR + KT) * T].rearrange("p (n t) -> p n t", t=T)
        mA = ctx.enter_context(nc.psum_tensor("mA", [P, 4, 512], F32))
        mW = ctx.enter_context(nc.psum_tensor("mW", [P, 4, 512], F32))
        WF = mW[:, :, :].rearrange("p a b -> p (a b)")

        def C(name, n=P, rows=P):
            return con[0:rows, CC[name]:CC[name] + n]

        def pc(name, i=0, lo=0, hi=P, src=par):
            return src[lo:hi, PC[name] + i:PC[name] + i + 1]

        def hc(name, i=0, lo=0, hi=P):
            return pc(name, i, lo, hi, half)

        class Area:

            def __init__(self, base, at=0):
                self.base, self.at = base, at

            def __call__(self, *shape, rows=P):
                n = int(np.prod(shape))
                assert self.at + n <= self.base.shape[1], (self.at + n, self.base.shape)
                a = self.base[0:rows, self.at:self.at + n]
                self.at += n
                if len(shape) > 1:
                    k = "abcd"[:len(shape)]
                    a = a.rearrange(f"p ({' '.join(k)}) -> p {' '.join(k)}", **dict(zip(k, shape)))
                return a

        sm = Area(small)
        shift_in = sm(7, TD)
        shift_out = sm(7, 9)
        mbuf = sm(4, 3, TD)
        rbuf = sm(2, 3, TD)
        h0 = sm(2, TD)
        n0 = sm(2, TD)
        m0 = sm(TD, rows=P)[0:4, :]
        n_out = sm(2, 9)
        m_out = sm(9, rows=P)[0:4, :]
        h_out = sm(2, 9)
        mconv_out = sm(4, 3, 9)
        rconv_out = sm(2, 3, 9)
        lam4 = sm(2)
        GYD = sm(2, TD)
        PLAST = sm(2, NC)
        router = sm(KT, NE)
        rbias = sm(NE)
        sq8 = SQ8[:, :, :].rearrange("p a b -> p (a b)")

        ar = Area(SCR)
        LGN = 2 * T + 2
        LG, LE, LY, LZ = ar(LGN), ar(LGN), ar(LGN), ar(LGN)
        RC, RT, RA, RL, RE, RX = ar(2, T), ar(4, T), ar(2, T), ar(2, T), ar(2, T), ar(2, T)
        RS, RH = ar(2, T), ar(2, T)
        assert ar.at < 12416

        ar = Area(SCR, 2 * LGN)
        CV, TQ = ar(4, T), ar(4, T)
        MVT, MKT = ar(2, 256), ar(2, 256)
        MSD = ar(4, 384)
        MD = ar(2, 384)
        MR = ar(6 * T)
        MDEN = ar(2, T)
        MGC = ar(2, 4)
        MDC = ar(2, 3, TD)
        ar_m = ar.at
        MS = ar(2, TD, 64)
        MX = ar(2, TD, 64)
        MCO = ar(2, 64)
        assert ar.at <= 12416, ar.at

        ar = Area(SCR, 2 * LGN)
        GB, GX = ar(TP), ar(4, TP)
        GQ, GK, GQH, GKH = ar(TP), ar(TP), ar(TP), ar(TP)
        GVT, GKT = ar(2, 256), ar(2, P)
        GAT = ar(2, 512)
        GKV = ar(NC, 256)
        GSS = ar(NC + 1, 256)
        GDX = ar(TD)
        GS, GXX = ar(TD, 64), ar(2, TD, 64)
        assert ar.at <= 12416, ar.at

        ar = Area(SCR)
        DL = ar(7, T)
        LW, AA, GG, TH = DL[:, 0:2, :], DL[:, 2:4, :], DL[:, 4:6, :], DL[:, 6, :]
        KKN, K4, RKV, NRM = ar(2, T), ar(2, T), ar(2, T), ar(2, T)
        AR = ar(2, 2, 2, P)
        BT, KTL, B2, K2 = ar(2, TP), ar(2, TP), ar(2, TP), ar(2, TP)
        ar_r = ar.at
        ATK, BTK, KTK, VTK = ar(2, 256), ar(2, 256), ar(2, 256), ar(2, 256)
        NB, MKS = ar(4, 256), ar(4, 256)
        VW = BIG[:, TRX * T:TRX * T + 512].rearrange("p (a b) -> p a b", a=2)
        WT = ar(2, P)
        ZZ = BIG[:, TGV * T:TGV * T + 512].rearrange("p (a b) -> p a b", a=2)
        SS = ar(2, NC + 1, 64)
        assert ar.at <= 12416, ar.at
        ar = Area(SCR, ar_r)
        DS, DX, DY = ar(2, TD, 64), ar(2, TD, 64), ar(2, TD, 64)
        DW = ar(2, TD)
        DKA = ar(2, TD)
        dead = BIG[:, TMQ * T:TMO * T]
        ND, NO, P2, P2T = (dead[:, 512 * i:512 * i + 512].rearrange("p (a b) -> p a b", a=4) for i in range(4))
        P4, P4T, QT, ET = (sq8[:, 512 * i:512 * i + 512].rearrange("p (a b) -> p a b", a=4) for i in range(4))
        EXPS = dead[:, 0:3 * 512].rearrange("p (a b t) -> p a b t", a=3, t=TP)

        OO = V8[:, 0:6, :]
        OT = SQ8[:, 0:6, :]
        MOG, GGS = U[:, TMO:TMO + 2, :], U[:, TGG:TGG + 2, :]
        RGY = U[:, TRY:TRY + 2, :]
        GTH = U[:, TRX:TRX + 2, :]
        YW = sq8[:, 0:512].rearrange("p (a b) -> p a b", a=2)
        BRANCH = {RG: RGY, ML: MOG, GL: GGS, RW: U[:, TR:TR + 2, :]}
        HF, FTH = (V8[:, i:i + 4, :].rearrange("p (a b) t -> p a b t", a=2) for i in (0, 4))

        ar = Area(SCR)
        XT = ar(3, D)
        HT = ar(2, 256)
        HE = ar(2, 256)
        YE = ar(D)
        PL = ar(3, P)
        PG = ar(3, P)
        PGT = ar(2, T)
        LOG, TOP = ar(3, NE), ar(3, 8)
        TIX = ar(24).bitcast(U32).rearrange("p (a b) -> p a b", a=3)
        IXF = ar(3, 8)
        TW = ar(3, 2)
        MASK, TMPE = ar(3, NE), ar(3, NE)
        GATE, RANK = ar(3, 3 * NE + 1), ar(3, 3 * NE + 1)
        ETH = ar(2, 256)
        CNT = ar(8)

        chunks = []
        for l in range(DEPTH):
            tiles = gates = 0
            for item in STREAM:
                if item[0] == "u":
                    tiles += 2
                    chunks.append((A["w_in"][l, item[1] // 2], pe_of.at("u.tile", l, tiles - 1)))
                    continue
                kind, g, q = item
                if q == 0 and kind != "gate":
                    chunks.append((A["w_branch"][l, g], pe_of.at("mg.up", l, KT * (RG, ML, GL, RW).index(g) + KT - 1)))
                if kind != "up":
                    gates += 2
                    chunks.append((A["w_in"][l, NU // 2 + 4 * g + q], pe_of.at("gate.tile", l, gates - 1)))
            chunks += [(A["w_out"][l, p], pe_of.at("mg.out", l, 2 * p + 1)) for p in range(4)]
            if l == 0:
                ffn_at = len(chunks)
                chunks += [(A["ffn_up"][i], dve_of.at("ff.lo", l, i)) for i in range(2 * FC)]
                chunks += [(A["ffn_down"][i], dve_of.at("ff.lo", l, 2 * FC + i)) for i in range(12)]
        uses0 = [len(range(k, len(chunks), SLOTS)) for k in range(SLOTS)]

        def landed(m, i):
            if i >= PAIR:
                return landed(m + 1, i - PAIR)
            k = SLOT_OF[i]
            return slot_in[k], (m * SLOT_OF.count(k) + (uses0[k] + SLOT_OF[:i + 1].count(k))) * 16

        def ffn_landed(i):
            return slot_in[(ffn_at + i) % SLOTS], 16 * ((ffn_at + i) // SLOTS + 1)

        def ffn_used(i):
            p, w = divmod(i - 2 * FC, 3)
            if p >= 0 and w == 2:
                return pe_of.at("ff.down", 0, 2 * p + 1)
            return pe_of.at("ff.part", 0, i - max(p, 0))

        block = ctx.enter_context(nc.Block())

        def rounds_of(eng):
            eng.wait_ge(rounds_known, 1)
            return eng.value_load(count_i[0:1, 0:1], min_val=1, max_val=3)

        @block.sync
        def _(sp):
            sp.dma_start(X[:, :, :], A["x"]).then_inc(x_in, 16)
            for i, (src, _) in enumerate(chunks):
                if i >= SLOTS:
                    sp.wait_ge(*chunks[i - SLOTS][1])
                sp.dma_start(ring_slot(i % SLOTS), src).then_inc(slot_in[i % SLOTS], 16)
                if i == 1:
                    sp.dma_start(con[:, :], A["const"]).then_inc(const_in, 16)

            def load_expert(m, row, i):
                k, last = SLOT_OF[i % PAIR], last_use(i)
                sp.wait_ge((split0, split1, down_done)[last % 3], m * (2 * FC) + max(last // 3 + 1 + FC, 1))
                sp.dma_start(ring[:, k, :], A["moe"][bass.ds(row + i, 1), :, :].rearrange("a p n -> (a p) n"))\
                    .then_inc(slot_in[k], 16)

            for i in range(2):
                load_expert(0, 0, i)
            R = rounds_of(sp) if not RECORD else 1
            with sp.Fori(0, R) as r:
                with sp.Fori(0, NE // 2) as e2:
                    for i in range(2, PAIR + 2):
                        load_expert(r * (NE // 2) + e2, e2 * PAIR, i)
            sp.wait_ge(*act_of.at("ln.half", 1, 1))
            sp.dma_start(O["y"][:, 0:4, :], X[:, 0:4, :]).then_inc(state_out, 16)
            sp.wait_ge(*act_of.at("ln.norm", 1, 1))
            sp.dma_start(O["y"][:, 4:8, :], X[:, 4:8, :]).then_inc(state_out, 16)
            sp.wait_ge(state_out, 16 * (12 * DEPTH + 2))

        @block.gpsimd
        def _(pool):
            for l in range(DEPTH):
                if l:
                    pool.wait_ge(*act_of.at("ln.norm", l - 1, 1))
                pool.dma_start(par[:, :], A["par"][l]).then_inc(par_in, 16)
                for dst, src in ((lora[:, :], "lora"), (alup[:, :], "alup"), (rgw[:, :, :], "rgw"), (shift_in, "shift"),
                                 (mbuf, "mconv"), (rbuf, "rconv"), (h0, "h0"), (n0, "n0"), (m0, "m0")):
                    pool.dma_start(dst, A[src][l]).then_inc(layer_in, 16)
                if l == 0:
                    pool.dma_start(router, A["router"]).then_inc(router_in, 16)
                    pool.dma_start(rbias, A["rbias"]).then_inc(router_in, 16)
                pool.wait_ge(*dve_of.at("rg.out", l))
                pool.dma_start(MS, A["mC"][l]).then_inc(layer_in, 16)
                pool.wait_ge(*dve_of.at("ml.out", l))
                pool.wait_ge(*pe_of.at("ml.c", l))
                pool.wait_ge(state_out, 16 * (12 * l + 7))
                pool.dma_start(GS, A["gS"][l]).then_inc(layer_in, 16)
                pool.wait_ge(*dve_of.at("gl.out", l))
                pool.wait_ge(state_out, 16 * (12 * l + 9))
                pool.dma_start(DS, A["rS"][l]).then_inc(layer_in, 16)

        LAYER_LOADS = 12

        def loads(l, n):
            return layer_in, 16 * (LAYER_LOADS * l + n)

        numbers, emptied = {}, []

        def number(kind, l, i, emptied_by):
            numbers[kind, l, i] = len(emptied)
            emptied.append(emptied_by)

        for l in range(DEPTH):
            tiles = gates = ups = 0
            for item in STREAM:
                for _ in range(2):
                    if item[0] == "u":
                        number("u", l, tiles, act_of.at("u.tile", l, tiles))
                        tiles += 1
                for _ in range(2):
                    if item[0] in ("merge", "gate"):
                        number("gate", l, gates, act_of.at("gate.tile", l, gates))
                        gates += 1
                for _ in range(2):
                    if item[0] in ("merge", "up"):
                        number("up", l, ups, dve_of.at("mg.up", l, ups))
                        ups += 1
            for i in range(KT):
                number("out", l, i, dve_of.at("mg.out", l, i))
            if l == 0:
                for i in range(KT):
                    number("d", l, i, dve_of.at("ff.down", l, i))

        def acc(kind, l, i):
            return mA[:, numbers[kind, l, i] % 4, 0:T]

        def ff_acc(c, i):
            return (mW, mA)[c % 2][:, i, 0:T]

        def filler(do):
            at = {"n": 0, "u": 0, "gate": 0, "up": 0}

            def fill(point):
                for _ in range(FILL[point]):
                    item = STREAM[at["n"]]
                    at["n"] += 1
                    kinds = {"u": ("u",), "merge": ("gate", "up"), "gate": ("gate",), "up": ("up",)}[item[0]]
                    for kind in kinds:
                        do(kind, at[kind], item)
                        at[kind] += 2
            return fill

        @block.scalar
        def _(act):
            nact = nc.scalar
            linked = [0]

            def link(ins):
                linked[0] += 1
                ins.then_inc(act_link, 1)
                act.wait_ge(act_link, linked[0])

            def store(dst, src):
                act.dma_start(dst, src).then_inc(state_out, 16)

            for l in range(DEPTH):
                act.wait_ge(par_in, 16 * (l + 1))
                if l:
                    act.wait_ge(state_out, 16 * 12 * l)
                act.wait_ge(*dve_of.at("u.half", l))

                def streamed(kind, i, item):
                    for q in range(2):
                        if kind == "u":
                            act.wait_ge(*pe_of.at("u.tile", l, i + q))
                            nact.activation(U[:, item[1] + q, :], acc("u", l, i + q), ACT.Identity, bias=pc("bin", item[1] + q))\
                                .then_inc(*act_of.step("u.tile", i + q))
                        if kind == "gate":
                            act.wait_ge(*pe_of.at("gate.tile", l, i + q))
                            if i + q >= GR:
                                act.wait_ge(*dve_of.at("mg.up", l, i + q - GR))
                            nact.activation(GT[:, (i + q) % GR, :], acc("gate", l, i + q), ACT.Tanh, scale=0.5,
                                            bias=hc("bgate", KT * item[1] + 2 * item[2] + q)).then_inc(*act_of.step("gate.tile", i + q))

                fill = filler(streamed)

                def head_norm(name, tiles):
                    act.wait_ge(*dve_of.at(f"{name}.centred", l))
                    nact.activation(OT[:, tiles, :], OO[:, tiles, :], ACT.Square).then_inc(*act_of.step(f"{name}.sq"))
                    act.wait_ge(*dve_of.at(f"{name}.var", l))
                    nact.activation(OT[:, tiles, :], OT[:, tiles, :], ACT.Sqrt).then_inc(*act_of.step(f"{name}.sqrt"))

                fill("start")
                act.wait_ge(*act_of.at("u.tile", l, 5))
                link(nact.activation(RX, RGY, ACT.Square))
                fill("alpha")
                act.wait_ge(*pe_of.at("rg.gates", l))
                for j in range(4):
                    ins = nact.activation(RT[:, j, :], mW[:, j, 0:T], ACT.Tanh, scale=0.5,
                                          bias=hc("rba", j) if j < 2 else hc("rbx", j - 2))
                ins.then_inc(*act_of.step("rg.tanh"))
                act.wait_ge(*dve_of.at("lg.in", l))
                link(nact.activation(LE, LG, ACT.Abs))
                nact.activation(LE, LE, ACT.Exp, scale=-1.0).then_inc(*act_of.step("lg.exp"))
                fill("rg1")
                act.wait_ge(*dve_of.at("rg.loga", l))
                nact.activation(RE, RL, ACT.Exp, scale=2.0)
                nact.activation(RS, RL, ACT.Tanh)
                nact.activation(RA, RL, ACT.Exp).then_inc(*act_of.step("rg.exp"))
                act.wait_ge(*dve_of.at("rg.gelu_in", l))
                nact.activation(RX, RX, ACT.Tanh, scale=0.7978845608028654).then_inc(*act_of.step("rg.gelu"))
                fill("rg2")
                act.wait_ge(*dve_of.at("rg.var", l))
                nact.activation(RE, RE, ACT.Sqrt, scale=-1.0).then_inc(*act_of.step("rg.sqrt"))
                fill("rg3")
                act.wait_ge(*dve_of.at("ml.conv", l))
                nact.activation(TQ, CV, ACT.Tanh, scale=0.5).then_inc(*act_of.step("ml.silu"))
                fill("ml1")
                act.wait_ge(*dve_of.at("ml.rows", l))
                nact.activation(MR[0:4, 4 * T:5 * T], MR[0:4, T:2 * T], ACT.Exp, scale=-1.0)
                nact.activation(MR[0:4, 5 * T:5 * T + 16], MR[0:4, 5 * T:5 * T + 16], ACT.Exp)\
                    .then_inc(*act_of.step("ml.exps"))
                nact.activation(MOG, MOG, ACT.Tanh, scale=0.5).then_inc(*act_of.step("ml.og"))
                store(O["h"][l], h_out)
                store(O["rconv"][l], rconv_out)
                fill("ml2")
                store(O["m"][l], m_out)
                store(O["mconv"][l], mconv_out)
                fill("ml3")
                for h in range(4):
                    act.wait_ge(*pe_of.at("ml.logd", l, h))
                    if h >= 2:
                        act.wait_ge(*dve_of.at("ml.sd", l, h - 2))
                        act.wait_ge(*dve_of.at("ml.kw", l, h - 2))
                    act.wait_ge(*dve_of.at("ml.gcol", l))
                    nact.activation(MD[:, h % 2, 0:256], mW[:, h % 2, 0:256], ACT.Exp, bias=MGC[:, 0, h:h + 1])
                    nact.activation(MD[:, h % 2, 256:384], mW[:, h % 2, 256:384], ACT.Exp, bias=MGC[:, 1, h:h + 1])\
                        .then_inc(*act_of.step("ml.d", h))
                fill("ml4")
                act.wait_ge(*pe_of.at("ml.num", l))
                nact.activation(MDEN[:, :, 0:256], mW[:, 2:4, 0:256], ACT.Abs).then_inc(*act_of.step("ml.abs"))
                fill("ml5")
                fill("ml6")
                act.wait_ge(*dve_of.at("ml.out", l))
                store(O["mC"][l], MCO)
                store(O["mCs"][l], MS)
                store(O["n"][l], n_out)
                head_norm("n1", slice(2, 4))
                nact.activation(GTH, GGS, ACT.Tanh, scale=0.5).then_inc(*act_of.step("gl.og"))
                act.wait_ge(*dve_of.at("gl.cum", l))
                nact.activation(GDX, LG[:, TP:T], ACT.Exp)
                nact.activation(GX, GX, ACT.Exp).then_inc(*act_of.step("gl.exp"))
                fill("gl1")
                act.wait_ge(*dve_of.at("gl.state", l))
                store(O["gS"][l], GSS[:, NC, :])
                fill("gl2")
                act.wait_ge(*dve_of.at("gl.dec", l))
                store(O["gSs"][l], GS)
                head_norm("n2", slice(4, 6))
                act.wait_ge(*dve_of.at("rw.mixed", l))
                nact.activation(TH[0:32, :], U[0:32, TLO, :], ACT.Tanh)
                nact.activation(TH[64:128, :], U[64:128, TLO, :], ACT.Tanh, scale=0.5).then_inc(*act_of.step("rw.lora"))
                nact.activation(NRM[:, 0, :], U[:, TK, :], ACT.Square, scale=pc("kk", 0))
                nact.activation(NRM[:, 1, :], U[:, TK + 1, :], ACT.Square, scale=pc("kk", 1)).then_inc(*act_of.step("rw.ksq"))
                fill("rw1")
                act.wait_ge(*pe_of.at("rw.wa", l))
                for j in range(2):
                    nact.activation(LW[:, j, :], mW[:, j, 0:T], ACT.Tanh, scale=0.5, bias=hc("w0", j))
                    ins = nact.activation(AA[:, j, :], mW[:, 2 + j, 0:T], ACT.Tanh, scale=0.5, bias=hc("a0", j))
                ins.then_inc(*act_of.step("rw.wa"))
                act.wait_ge(*pe_of.at("rw.g", l))
                nact.activation(GG, mW[:, 0:2, 0:T], ACT.Copy).then_inc(*act_of.step("rw.g"))
                act.wait_ge(*dve_of.at("rw.ksum", l))
                store(O["shift"][l], shift_out)
                nact.activation(NRM, NRM, ACT.Sqrt).then_inc(*act_of.step("rw.ksqrt"))
                fill("rw2")
                act.wait_ge(*dve_of.at("rw.cum", l))
                nact.activation(DW, LW[:, :, TP:T], ACT.Exp)
                nact.activation(EXPS[:, 0, :, :], RKV[:, :, 0:TP], ACT.Exp)
                nact.activation(EXPS[:, 1, :, :], RKV[:, :, 0:TP], ACT.Exp, scale=-1.0)
                nact.activation(EXPS[:, 2, :, :], BT, ACT.Exp).then_inc(*act_of.step("rw.exp"))
                fill("rw3")
                act.wait_ge(*dve_of.at("rw.dec", l))
                store(O["rSs"][l], DS)
                fill("rw4")
                fill("rw5")
                for g in range(2):
                    fill(f"g{g}a")
                    act.wait_ge(*pe_of.at("rw.p2", l, g))
                    nact.activation(P2, mW[:, 0, :], ACT.Copy)
                    nact.activation(P2T, mW[:, 1, :], ACT.Copy).then_inc(*act_of.step("rw.p2", g))
                    act.wait_ge(*pe_of.at("rw.p4", l, g))
                    nact.activation(P4, mW[:, 0, :], ACT.Copy)
                    nact.activation(P4T, mW[:, 1, :], ACT.Copy).then_inc(*act_of.step("rw.p4", g))
                    fill(f"g{g}b")
                    act.wait_ge(*pe_of.at("rw.p8", l, g))
                    nact.activation(P2, mW[:, 0, :], ACT.Copy).then_inc(*act_of.step("rw.p8", g))
                    act.wait_ge(*pe_of.at("rw.et", l, g))
                    nact.activation(ET, mW[:, 0, :], ACT.Copy).then_inc(*act_of.step("rw.et", g))
                    fill(f"g{g}c")
                    act.wait_ge(*pe_of.at("rw.wt", l, g))
                    nact.activation(WT, mW[:, 2, 0:256], ACT.Copy).then_inc(*act_of.step("rw.wt", g))
                    fill(f"g{g}d")
                fill("tail")
                act.wait_ge(*dve_of.at("rw.state", l, NC - 1))
                store(O["rS"][l], SS[:, :, NC, :])
                head_norm("n0", slice(0, 2))
                fill("end")

                def norm(i):
                    for h in range(2):
                        act.wait_ge(*dve_of.at("ln.centred", l, 2 * i + h))
                        nact.activation(V8[:, 4 * h:4 * h + 4, :], SQ8[:, 4 * h:4 * h + 4, :], ACT.Square)\
                            .then_inc(*act_of.step("ln.sq", 2 * i + h))
                    act.wait_ge(*pe_of.at("ln.var", l, i))
                    nact.activation(V8[:, 1, :], mW[:, 1, 0:T], ACT.Sqrt, bias=C("eps", 1)).then_inc(*act_of.step("ln.sqrt", i))
                    for j in range(KT):
                        if j % 4 == 0:
                            act.wait_ge(*dve_of.at("ln.scaled", l, 2 * i + j // 4))
                        ins = nact.activation(X[:, j, :], SQ8[:, j, :], ACT.Identity, scale=pc(f"ln{i + 1}g", j),
                                              bias=pc(f"ln{i + 1}b", j))
                        if j % 4 == 3:
                            ins.then_inc(*act_of.step(("ln.half", "ln.norm")[j // 4], i))
                            if l == i == 0:
                                act.wait_ge(*act_of.at(("ln.half", "ln.norm")[j // 4], l, i))
                                nact.activation(XH[:, j - 3:j + 1, :], X[:, j - 3:j + 1, :], ACT.Copy)\
                                    .then_inc(*act_of.step("ff.xh", j // 4))

                def round_ffn(i):
                    act.wait_ge(*ffn_landed(i))
                    if i >= 2:
                        act.wait_ge(*ffn_used(i - 2))
                    nact.activation(FWH[:, i % 2, :], ring_slot((ffn_at + i) % SLOTS), ACT.Copy).then_inc(*act_of.step("ff.hi", i))

                if l == 0:
                    act.wait_ge(*dve_of.at("rw.branch", l))
                    round_ffn(0)
                    round_ffn(1)
                norm(0)
                if l == 0:
                    for c in range(FC):
                        round_ffn(2 * c + 2)
                        act.wait_ge(*pe_of.at("ff.part", l, 2 * c))
                        if c >= 2:
                            act.wait_ge(*dve_of.at("ff.hid", l, c - 2))
                        for q in range(2):
                            ins = nact.activation(FTH[:, c % 2, q, :], ff_acc(c, q), ACT.Tanh, scale=0.5)
                        ins.then_inc(*act_of.step("ff.tanh", c))
                        round_ffn(2 * c + 3)
                    for i in range(2 * FC + 2, 2 * FC + 12):
                        round_ffn(i)
                else:
                    act.wait_ge(moe_setup_dve, 6)
                    for i in range(3):
                        n = P if i < 2 else TD
                        ins = nact.activation(TW[0:n, i, 0:1], TW[0:n, i, 0:1], ACT.Exp)
                    ins.then_inc(moe_setup_act, 1)
                    R = rounds_of(act)
                    halves_of = lambda x: (x[:, 0:4, :], x[:, 4:8, :])

                    def round_tokens(n, u, part):
                        act.wait_ge(gathered, 2 * n + (part + 1))
                        nact.activation(halves_of(XEH[:, u, :, :])[part], mW[:, 3 - part, :], ACT.Copy)\
                            .then_inc(gather_kept, 1)

                    def round_weights(m, step, done, part):
                        act.wait_ge(*landed(m, 3 * step + part))
                        act.wait_ge((in0_done, in1_done)[part], done)
                        nact.activation(WH[:, part, :], ring[:, SLOT_OF[(3 * step + part) % PAIR], :], ACT.Copy)\
                            .then_inc((rounded0, rounded1)[part], 1)

                    def keep_turned(n, u, c):
                        b = (FC * u + c) % 2
                        act.wait_ge(hidden_turned, n * FC + (c + 1))
                        act.wait_ge(down_done, n * FC + (c - 1 + FC))
                        nact.activation(HE[:, b, :], mA[:, 2 + b, 0:256], ACT.Copy).then_inc(turned_kept, 1)

                    for part in range(2):
                        round_weights(0, 0, 0, part)
                        round_tokens(0, 0, part)
                    with act.Fori(0, R * (NE // 2)) as m:
                        for u in range(2):
                            n = 2 * m + u
                            for c in range(FC):
                                b = (FC * u + c) % 2
                                if c:
                                    keep_turned(n, u, c - 1)
                                round_weights(m, FC * u + c + 1, n * FC + (c + 1), 0)
                                act.wait_ge(in1_done, n * FC + (c + 1))
                                act.wait_ge(hidden, n * FC + max(c - 1, 0))
                                nact.activation(ETH[:, b, :], mA[:, b, 0:256], ACT.Tanh, scale=0.5).then_inc(tanh_done, 1)
                                round_weights(m, FC * u + c + 1, n * FC + (c + 1), 1)
                                if c == FC - 2:
                                    round_tokens(n + 1, 1 - u, 0)
                            keep_turned(n, u, FC - 1)
                            round_tokens(n + 1, 1 - u, 1)
                            act.wait_ge(down_done, n * FC + 2 * FC)
                            nact.activation(YE, WF[:, 0:1024], ACT.Copy).then_inc(down_kept, 1)
                norm(1)


        def moe_vector(dve, v, link, linked):
            MUL, ADD, SUB, MAX, EQ = ALU.mult, ALU.add, ALU.subtract, ALU.max, ALU.is_equal
            v.memset(MASK, 0.0)
            v.memset(GATE, 0.0)
            v.memset(YE, 0.0)
            v.memset(PGT[:, 1, :], 0.0)
            link(v.memset(RANK, -1.0))
            link(v.tensor_scalar(SQ8[:, :, :], X[:, :, :], 2 * ALPHA, None, MUL))
            for i in range(3):
                n = P if i < 2 else TD
                dve.wait_ge(moe_setup_pe, i + 1)
                v.tensor_copy(XT[0:n, i, :], WF[0:n, 1024 * (i % 2):1024 * (i % 2) + 1024]).then_inc(moe_setup_dve, 1)
            dve.wait_ge(moe_setup_pe, 4)
            dve.wait_ge(router_in, 32)
            for i in range(3):
                n = P if i < 2 else TD
                link(v.tensor_tensor(LOG[0:n, i, :], mA[0:n, 0, NE * i:NE * i + NE], rbias[0:n, :], ADD))
                link(v.max(TOP[0:n, i, :], LOG[0:n, i, :]))
                link(v.max_index(TIX[0:n, i, :], TOP[0:n, i, :], LOG[0:n, i, :]))
                v.tensor_copy(IXF[0:n, i, :], TIX[0:n, i, :])
                ins = v.tensor_tensor(TW[0:n, i, 0:1], TOP[0:n, i, 1:2], TOP[0:n, i, 0:1], SUB)
                ins.then_inc(moe_setup_dve, 1)
            dve.wait_ge(moe_setup_act, 1)
            for i in range(3):
                n = P if i < 2 else TD
                link(v.tensor_scalar(TW[0:n, i, 1:2], TW[0:n, i, 0:1], 1.0, None, ADD))
                link(v.reciprocal(TW[0:n, i, 1:2], TW[0:n, i, 1:2]))
                link(v.tensor_tensor(TW[0:n, i, 0:1], TW[0:n, i, 0:1], TW[0:n, i, 1:2], MUL))
                i8 = C("iota8", NE, n)
                v.tensor_scalar(MASK[0:n, i, :], i8, IXF[0:n, i, 0:1], None, EQ)
                v.tensor_scalar(TMPE[0:n, i, :], i8, IXF[0:n, i, 1:2], None, EQ)
                v.tensor_scalar(GATE[0:n, i, 0:NE], i8, IXF[0:n, i, 0:1], TW[0:n, i, 1:2], EQ, MUL)
                link(v.tensor_scalar(LOG[0:n, i, :], i8, IXF[0:n, i, 1:2], TW[0:n, i, 0:1], EQ, MUL))
                v.tensor_tensor(GATE[0:n, i, 0:NE], GATE[0:n, i, 0:NE], LOG[0:n, i, :], ADD)
                v.tensor_tensor(MASK[0:n, i, :], MASK[0:n, i, :], TMPE[0:n, i, :], ADD).then_inc(moe_setup_dve, 1)
            dve.wait_ge(moe_setup_pe, 5)
            for i in range(3):
                n = P if i < 2 else TD
                ins = v.scalar_tensor_tensor(RANK[0:n, i, 0:NE], mA[0:n, 1, NE * i:NE * i + NE], 1.0, MASK[0:n, i, :], ADD, MUL)
            link(ins)
            for k in (1, 2):
                v.tensor_copy(GATE[:, :, NE * k:NE * k + NE], GATE[:, :, 0:NE])
            for i in range(3):
                n = P if i < 2 else TD
                link(v.tensor_scalar(RANK[0:n, i, 0:NE], RANK[0:n, i, 0:NE], -1.0, None, ADD))
            for k in (1, 2):
                v.tensor_scalar(RANK[:, :, NE * k:NE * k + NE], RANK[:, :, 0:NE], -float(P * k), None, ADD)
            link(v.tensor_reduce(CNT[0:1, 0:1], mA[0:1, 1, 3 * NE:4 * NE], AX_X, MAX))
            v.tensor_scalar(CNT[0:1, 1:2], CNT[0:1, 0:1], float(P), 1.0, ALU.is_gt, ADD)
            link(v.tensor_scalar(CNT[0:1, 2:3], CNT[0:1, 0:1], float(2 * P), None, ALU.is_gt))
            link(v.tensor_tensor(CNT[0:1, 1:2], CNT[0:1, 1:2], CNT[0:1, 2:3], ADD))
            v.tensor_copy(count_i[0:1, 0:1], CNT[0:1, 1:2]).then_inc(rounds_known, 1)
            R = rounds_of(dve)

            def place(n):
                dve.wait_ge(gathered, 2 * n)
                for i in range(3):
                    ins = v.tensor_scalar(PL[:, i, :], C("iota"), RANK[:, i, bass.ds(n, 1)], None, EQ)
                ins.then_inc(placed, 1)
                dve.wait_ge(placed, n + 1)
                for i in range(3):
                    ins = v.tensor_scalar(PG[:, i, :], PL[:, i, :], GATE[:, i, bass.ds(n, 1)], None, MUL)
                ins.then_inc(place_ready, 1)

            def turned(n, u):
                dve.wait_ge(placeT_pe, n + 1)
                v.tensor_copy(PGT[:, u, :], mW[:, 2, 0:T]).then_inc(placeT_ready, 1)

            def add(n, i):
                dve.wait_ge(scattered, n * KT + (i + 2))
                v.tensor_tensor(SQ8[:, i:i + 2, :], SQ8[:, i:i + 2, :], mW[:, 2:4, 0:T], ADD).then_inc(scatter_added, 1)

            def split_tokens(n, u, part):
                dve.wait_ge(gather_kept, 2 * n + (part + 1))
                v.tensor_tensor(XEL[:, u, 4 * part:4 * part + 4, :], mW[:, 3 - part, :].rearrange("p (k n) -> p k n", k=4),
                                XEH[:, u, 4 * part:4 * part + 4, :].bitcast(F32), SUB).then_inc(gather_split, 1)

            def split_weights(step, done, part):
                dve.wait_ge((rounded0, rounded1)[part], done + 1)
                v.tensor_tensor(WL[:, part, :], ring[:, SLOT_OF[(3 * step + part) % PAIR], :], WH[:, part, :].bitcast(F32), SUB)\
                    .then_inc((split0, split1)[part], 1)

            dve.wait_ge(dve_link, linked[0])
            place(0)
            turned(0, 0)
            for part in range(2):
                split_weights(0, 0, part)
                split_tokens(0, 0, part)
            with dve.Fori(0, R * (NE // 2)) as m:
                for u in range(2):
                    n = 2 * m + u
                    for c in range(FC):
                        if 2 <= c < 6:
                            add(n, 2 * (c - 2))
                        if c == 6:
                            place(n + 1)
                        split_weights(FC * u + c + 1, n * FC + (c + 1), 0)
                        if c == 7:
                            dve.wait_ge(scatter_added, n * 4 + 4)
                            turned(n + 1, 1 - u)
                        b = (FC * u + c) % 2
                        dve.wait_ge(tanh_done, n * FC + (c + 1))
                        v.scalar_tensor_tensor(ETH[:, b, :], ETH[:, b, :], 1.0, mA[:, b, 0:256], ADD, MUL).then_inc(gated, 1)
                        dve.wait_ge(gated, n * FC + (c + 1))
                        dve.wait_ge(hidden_turned, n * FC + max(c - 1, 0))
                        v.tensor_tensor(HT[:, b, :], ETH[:, b, :], mA[:, b, 256:512], MUL).then_inc(hidden, 1)
                        split_weights(FC * u + c + 1, n * FC + (c + 1), 1)
                        if c == FC - 2:
                            split_tokens(n + 1, 1 - u, 0)
                    split_tokens(n + 1, 1 - u, 1)
            for i in range(0, KT, 2):
                add(R * NE, i)
            dve.wait_ge(scatter_added, R * (NE * 4) + 4)

        @block.vector
        def _(dve):
            v = nc.vector
            linked = [0]

            def link(ins):
                linked[0] += 1
                ins.then_inc(dve_link, 1)
                dve.wait_ge(dve_link, linked[0])

            def done(ins, name, i=0):
                ins.then_inc(*dve_of.step(name, i))
                dve.wait_ge(*dve_of.at(name, layer[0], i))

            layer = [0]
            MUL, ADD, SUB, MAX = ALU.mult, ALU.add, ALU.subtract, ALU.max

            def conv(dst, src, buf, w, b, n):
                for i in range(n):
                    ins = v.tensor_scalar(dst[:, i, :], src[:, i, :], pc(w, 4 * i + 3), pc(b, i), MUL, ADD)
                link(ins)
                for back in range(1, 4):
                    for i in range(n):
                        v.scalar_tensor_tensor(dst[:, i, back:TP], src[:, i, 0:TP - back], pc(w, 4 * i + 3 - back),
                                               dst[:, i, back:TP], MUL, ADD)
                        ins = v.scalar_tensor_tensor(dst[:, i, TP:T], buf[:, i, 3 - back, :], pc(w, 4 * i + 3 - back),
                                                     dst[:, i, TP:T], MUL, ADD)
                    if back < 3:
                        link(ins)
                return ins

            def last_rows(out, buf, src):
                v.tensor_copy(out[:, :, :, 0], src[:, :, TP - 3:TP])
                v.tensor_copy(out[:, :, 0:2, 1:9], buf[:, :, 1:3, :])
                return v.tensor_copy(out[:, :, 2, 1:9], src[:, :, TP:T])

            def over_v(x):
                return x.unsqueeze(3).broadcast_to([P, x.shape[1], TD, 64])

            def unit():
                return C("i64", 64).unsqueeze(1).unsqueeze(1).broadcast_to([P, 2, TD, 64])

            def w4(a, n=2):
                return WF[:, 512 * a:512 * (a + n)].rearrange("p (j b v) -> p j b v", j=n, b=TD)

            def streamed(kind, i, item):
                if kind != "up":
                    return
                l, (_, g, q2) = layer[0], item
                for q in range(2):
                    dt = 2 * q2 + q
                    dve.wait_ge(*pe_of.at("mg.up", l, i + q))
                    dve.wait_ge(*act_of.at("gate.tile", l, i + q))
                    dst = MG[:, dt, :] if g == RG else V8[:, 6 + q, :]
                    ins = v.scalar_tensor_tensor(dst, GT[:, (i + q) % GR, :], 1.0, acc("up", l, i + q), ADD, MUL)
                    ins.then_inc(*dve_of.step("mg.up", i + q))
                if g != RG:
                    dve.wait_ge(*dve_of.at("mg.up", l, i + 1))
                    ins = v.tensor_tensor(MG[:, 2 * q2:2 * q2 + 2, :], MG[:, 2 * q2:2 * q2 + 2, :], V8[:, 6:8, :], ADD)
                    if g == RW:
                        done(ins, "ms.sum", q2)
                    else:
                        link(ins)

            def head_norm(name, tiles, eps, centre=True, meanwhile=None):
                l = layer[0]
                if centre:
                    dve.wait_ge(*pe_of.at(f"{name}.mean", l))
                    done(v.tensor_tensor(OO[:, tiles, :], OO[:, tiles, :], mW[:, 0:2, 0:T], SUB), f"{name}.centred")
                else:
                    done(v.tensor_copy(OO[:, tiles, TP:T], GYD), f"{name}.centred")
                if meanwhile:
                    meanwhile()
                dve.wait_ge(*pe_of.at(f"{name}.var", l))
                done(v.tensor_scalar(OT[:, tiles, :], mW[:, 2:4, 0:T], eps, None, ADD), f"{name}.var")
                dve.wait_ge(*act_of.at(f"{name}.sqrt", l))
                link(v.reciprocal(OT[:, tiles, :], OT[:, tiles, :]))
                link(v.tensor_tensor(OO[:, tiles, :], OO[:, tiles, :], OT[:, tiles, :], MUL))

            for l in range(DEPTH):
                layer[0] = l
                fill = filler(streamed)
                dve.wait_ge(par_in, 16 * (l + 1))
                done(v.tensor_scalar(half[:, :], par[:, :], 0.5, None, MUL), "u.half")
                dve.wait_ge(*loads(l, 9))
                dve.wait_ge(const_in, 16)
                if l:
                    dve.wait_ge(*act_of.at("ln.norm", l - 1, 1))
                link(v.memset(LG[:, T:2 * T], 0.0))
                v.tensor_copy(LG[:, 2 * T:2 * T + 2], par[:, PC["lam"]:PC["lam"] + 2])
                dve.wait_ge(*act_of.at("u.tile", l, 1))
                v.tensor_copy(LG[0:4, T:2 * T], U[32:36, TMI, :])
                dve.wait_ge(*pe_of.at("lg.alpha", l))
                done(v.tensor_scalar(LG[:, 0:T], mW[:, 0, 0:T], pc("gab"), None, ADD), "lg.in")
                dve.wait_ge(*act_of.at("u.tile", l, 5))
                fill("start")
                fill("alpha")
                done(conv(RC, U[:, TRX:TRX + 2, :], rbuf, "rcw", "rcb", 2), "rg.conv")
                last_rows(rconv_out, rbuf, U[:, TRX:TRX + 2, :])
                dve.wait_ge(*act_of.at("lg.exp", l))
                link(v.tensor_scalar(LY, LE, 2.0, None, ADD))
                link(v.reciprocal(LY, LY))
                link(v.tensor_tensor(LY, LE, LY, MUL))
                link(v.tensor_tensor(LZ, LY, LY, MUL))
                link(v.tensor_scalar(LE, LZ, 1.0 / 15, None, MUL))
                for k in (13, 11, 9, 7, 5, 3):
                    link(v.scalar_tensor_tensor(LE, LE, 1.0 / k, LZ, ADD, MUL))
                v.tensor_scalar(LG, LG, 0.0, None, ALU.min)
                link(v.scalar_tensor_tensor(LE, LE, 1.0, LY, ADD, MUL))
                link(v.scalar_tensor_tensor(LG, LE, -2.0, LG, MUL, ADD))
                link(v.tensor_scalar(lam4, LG[:, 2 * T:2 * T + 2], 4.0, None, MUL))
                dve.wait_ge(*act_of.at("rg.tanh", l))
                for j in range(2):
                    ins = v.tensor_scalar(RL[:, j, :], RT[:, j, :], 1.0, lam4[:, j:j + 1], ADD, MUL)
                done(ins, "rg.loga")
                v.scalar_tensor_tensor(RT[:, 2:4, :], RT[:, 2:4, :], 1.0, RC, ADD, MUL)
                link(v.tensor_scalar(RX, RX, 0.044715, 1.0, MUL, ADD))
                done(v.tensor_tensor(RX, RX, RGY, MUL), "rg.gelu_in")
                dve.wait_ge(*act_of.at("rg.exp", l))
                done(v.scalar_tensor_tensor(RE, RE, 1.0, RS, ADD, MUL), "rg.var")
                dve.wait_ge(*act_of.at("rg.sqrt", l))
                link(v.scalar_tensor_tensor(RS, RE, 0.5, RT[:, 2:4, :], MUL, MUL))
                for j in range(2):
                    v.tensor_tensor_scan(RH[:, j, 0:TP], RA[:, j, 0:TP], RS[:, j, 0:TP], 0.0, MUL, ADD)
                link(v.tensor_tensor(RH[:, :, TP:T], RA[:, :, TP:T], h0, MUL))
                link(v.tensor_tensor(RH[:, :, TP:T], RH[:, :, TP:T], RS[:, :, TP:T], ADD))
                v.tensor_copy(h_out, RH[:, :, TP - 1:T])
                dve.wait_ge(*act_of.at("rg.gelu", l))
                link(v.scalar_tensor_tensor(RX, RX, 1.0, RGY, ADD, MUL))
                done(v.scalar_tensor_tensor(RGY, RH, 0.5, RX, MUL, MUL), "rg.out")
                for point in ("rg1", "rg2", "rg3"):
                    fill(point)
                dve.wait_ge(*act_of.at("u.tile", l, 9))
                done(conv(CV, U[:, TMQ:TMQ + 4, :], mbuf, "mcw", "mcb", 4), "ml.conv")
                last_rows(mconv_out, mbuf, U[:, TMQ:TMQ + 4, :])
                f, ip = LG[0:4, T:2 * T], U[0:4, TMI, :]

                def row(k, lo=0, hi=TP):
                    return MR[0:4, k * T + lo:k * T + hi]

                v.tensor_tensor_scan(row(0), C("ones", TP, 4), f[:, 0:TP], 0.0, MUL, ADD)
                v.tensor_tensor_scan(row(1), f[:, 0:TP], ip[:, 0:TP], 0.0, ADD, MAX)
                link(v.tensor_tensor(row(5, 0, TD), f[:, TP:T], m0, ADD))
                link(v.tensor_tensor(row(1, TP, T), row(5, 0, TD), ip[:, TP:T], MAX))
                v.tensor_tensor(row(5, 0, TD), row(5, 0, TD), row(1, TP, T), SUB)
                v.tensor_tensor(row(5, TD, 2 * TD), ip[:, TP:T], row(1, TP, T), SUB)
                v.tensor_tensor(row(2), ip[:, 0:TP], row(0), SUB)
                v.tensor_tensor(row(3), row(0), row(1), SUB)
                done(v.tensor_copy(m_out, row(1, TP - 1, T)), "ml.rows")
                dve.wait_ge(*act_of.at("ml.silu", l))
                link(v.scalar_tensor_tensor(CV, TQ, 1.0, CV, ADD, MUL))
                v.tensor_scalar(CV[:, 0:2, :], CV[:, 0:2, :], 0.5, None, MUL)
                done(v.tensor_scalar(CV[:, 2:4, :], CV[:, 2:4, :], 0.5 * 64 ** -0.5, None, MUL), "ml.qk")
                dve.wait_ge(*act_of.at("ml.exps", l))
                done(v.tensor_copy(row(5, 2 * TD, 3 * TD), row(4, TP, T)), "ml.dec_rows")
                fill("ml1")
                fill("ml2")
                dve.wait_ge(*pe_of.at("ml.turn", l))
                v.tensor_copy(MVT, mW[:, 0, :].rearrange("p (a b) -> p a b", a=2))
                v.tensor_copy(MKT, mW[:, 1, :].rearrange("p (a b) -> p a b", a=2))
                v.tensor_copy(MGC, mW[:, 2, 0:8].rearrange("p (a b) -> p a b", a=2))
                done(v.tensor_copy(MDC, mW[:, 3, 0:48].rearrange("p (a b c) -> p a b c", a=2, b=3)), "ml.gcol")
                fill("ml3")
                for h in range(4):
                    dve.wait_ge(*pe_of.at("ml.qk", l, h))
                    dve.wait_ge(*act_of.at("ml.d", l, h))
                    v.tensor_tensor(MSD[:, h, :], mW[:, 2 + h % 2, 0:384], MD[:, h % 2, :], MUL)\
                        .then_inc(*dve_of.step("ml.sd", h))
                    v.tensor_scalar(MKT[:, 0, 64 * h:64 * h + 64], MKT[:, 0, 64 * h:64 * h + 64], MD[:, h % 2, 255:256], None, MUL)
                    done(v.tensor_scalar(MKT[:, 1, 64 * h:64 * h + 64], MKT[:, 1, 64 * h:64 * h + 64],
                                         MD[:, h % 2, 383:384], None, MUL), "ml.kw", h)
                fill("ml4")
                dve.wait_ge(*pe_of.at("ml.emb", l))
                link(v.tensor_tensor(MDEN[:, :, 0:TP], MDEN[:, :, 0:TP], mW[:, 2:4, 0:TP], MAX))
                link(v.reciprocal(MDEN[:, :, 0:TP], MDEN[:, :, 0:TP]))
                done(v.tensor_tensor(OO[:, 2:4, 0:TP], mW[:, 0:2, 0:TP], MDEN[:, :, 0:TP], MUL), "ml.h")
                fill("ml5")
                dve.wait_ge(*pe_of.at("ml.c", l))
                v.tensor_copy(n_out[:, :, 0], mW[:, 0, 0:256].rearrange("p (j v) -> p j v", j=2)[:, :, 64])
                done(v.tensor_copy(MCO, mW[:, 0, 0:256].rearrange("p (j v) -> p j v", j=2)[:, :, 0:64]), "ml.cout")
                qd, kd, vd = CV[:, 0:2, TP:T], CV[:, 2:4, TP:T], U[:, TMV:TMV + 2, TP:T]
                done(v.tensor_tensor(MX, unit(), over_v(vd), MUL), "ml.dv")
                link(v.tensor_tensor(MDEN[:, :, 0:TD], kd, MDC[:, :, 1, :], MUL))
                link(v.tensor_tensor(n_out[:, :, 1:9], n0, MDC[:, :, 0, :], MUL))
                link(v.tensor_tensor(n_out[:, :, 1:9], n_out[:, :, 1:9], MDEN[:, :, 0:TD], ADD))
                link(v.tensor_tensor(MDEN[:, :, TD:2 * TD], n_out[:, :, 1:9], qd, MUL))
                dve.wait_ge(*loads(l, 10))
                link(v.tensor_tensor(MS, MS, over_v(MDC[:, :, 0, :]), MUL))
                fill("ml6")
                dve.wait_ge(*pe_of.at("ml.dvb", l))
                link(v.tensor_tensor(MX, w4(0), over_v(MDEN[:, :, 0:TD]), MUL))
                link(v.tensor_tensor(MS, MS, MX, ADD))
                done(v.tensor_tensor(MX, MS, over_v(qd), MUL), "ml.dq")
                dve.wait_ge(*pe_of.at("ml.dnum", l))
                link(v.tensor_tensor(MX, w4(0), unit(), MUL))
                v.tensor_reduce(MDEN[:, :, 2 * TD:3 * TD], MX, AX_X, ADD)
                den = MDEN[:, :, 3 * TD:4 * TD]
                link(v.tensor_copy(den, mW[:, 2, 0:16].rearrange("p (j b) -> p j b", j=2)))
                link(v.scalar_tensor_tensor(den, den, -1.0, den, MUL, MAX))
                link(v.tensor_tensor(den, den, MDC[:, :, 2, :], MAX))
                link(v.reciprocal(den, den))
                done(v.tensor_tensor(OO[:, 2:4, TP:T], MDEN[:, :, 2 * TD:3 * TD], den, MUL), "ml.out")
                la = LG[:, 0:T]

                def chunks4(x):
                    return x.rearrange("p (c t) -> p c t", c=NC)

                def at_chunk(x, t):
                    return chunks4(x)[:, :, t:t + 1].broadcast_to([P, NC, CH])

                def gla_decays():
                    link(v.tensor_scalar(la, la, 1.0 / 16, None, MUL))
                    link(v.tensor_tensor_scan(GB, C("reset", TP), la[:, 0:TP], 0.0, MUL, ADD))
                    link(v.tensor_tensor(chunks4(GX[:, 0, :]), chunks4(GB), at_chunk(GB, CH // 2 - 1), SUB))
                    v.tensor_scalar(GX[:, 1, :], GX[:, 0, :], -1.0, None, MUL)
                    v.tensor_copy(GX[:, 2, :], GB)
                    done(v.tensor_tensor(chunks4(GX[:, 3, :]), at_chunk(GB, CH - 1), chunks4(GB), SUB), "gl.cum")

                head_norm("n1", slice(2, 4), 1e-6, meanwhile=gla_decays)
                link(v.tensor_scalar(MOG, MOG, 0.5, 0.5, MUL, ADD))
                for j in range(2):
                    ins = v.scalar_tensor_tensor(MOG[:, j, :], OO[:, 2 + j, :], pc("mnw", j), MOG[:, j, :], MUL, MUL)
                done(ins, "ml.branch")
                dve.wait_ge(*act_of.at("gl.og", l))
                link(v.scalar_tensor_tensor(GGS, GTH, 1.0, GGS, ADD, MUL))
                v.tensor_scalar(GGS, GGS, 0.5, None, MUL)
                dve.wait_ge(state_out, 16 * (12 * l + 7))
                dve.wait_ge(*act_of.at("gl.exp", l))
                q, k = U[:, TGQ, :], U[:, TGK, :]
                v.scalar_tensor_tensor(GQ, q[:, 0:TP], 32 ** -0.5, GX[:, 0, :], MUL, MUL)
                v.tensor_tensor(GK, k[:, 0:TP], GX[:, 1, :], MUL)
                v.scalar_tensor_tensor(GQH, q[:, 0:TP], 32 ** -0.5, GX[:, 2, :], MUL, MUL)
                done(v.tensor_tensor(GKH, k[:, 0:TP], GX[:, 3, :], MUL), "gl.ops")
                dve.wait_ge(*pe_of.at("gl.turn", l))
                v.tensor_copy(GVT, mW[:, 0, :].rearrange("p (a b) -> p a b", a=2))
                done(v.tensor_copy(GKT, mW[:, 1, 0:256].rearrange("p (a b) -> p a b", a=2)), "gl.turned")
                dve.wait_ge(*pe_of.at("gl.attn", l))
                for c2 in range(2):
                    ins = v.tensor_tensor(GAT[:, c2, :].rearrange("p (h t) -> p h t", h=4),
                                          mW[:, :, P * c2:P * c2 + P],
                                          mid(con[:, CC["mk"] + P:CC["mk"] + 2 * P], 4), MUL)
                done(ins, "gl.attn")
                fill("gl1")
                dve.wait_ge(*pe_of.at("gl.kv", l))
                v.memset(GSS[:, 0, :], 0.0)
                for e in range(2):
                    ins = v.tensor_tensor(GKV[:, e::2, :], mW[:, e, :].rearrange("p (c n) -> p c n", c=2), mid(C("gm", 256), 2), MUL)
                link(ins)
                for c in range(NC):
                    ins = v.scalar_tensor_tensor(GSS[:, c + 1, :], GSS[:, c, :], GX[:, 2, CH * c + CH - 1:CH * c + CH],
                                                 GKV[:, c, :], MUL, ADD)
                    if c < NC - 1:
                        link(ins)
                done(ins, "gl.state")
                done(v.tensor_tensor(GXX, unit(), over_v(U[:, TGV:TGV + 2, TP:T]), MUL), "gl.dv")
                dve.wait_ge(*pe_of.at("gl.y", l))
                done(v.tensor_copy(OO[:, 4:6, 0:TP], mW[:, 2:4, 0:TP]), "gl.y")
                um = U[:, 0:7, :]
                dve.wait_ge(*act_of.at("u.tile", l, NU - 1))
                v.tensor_copy(shift_out, U[:, 0:7, TP - 1:T])
                v.tensor_tensor(DL[:, :, 1:TP], um[:, :, 0:TP - 1], um[:, :, 1:TP], SUB)
                v.tensor_scalar(DL[:, :, 0:1], um[:, :, 0:1], -1.0, None, MUL)
                link(v.tensor_tensor(DL[:, :, TP:T], shift_in, um[:, :, TP:T], SUB))
                for i in range(7):
                    ins = v.scalar_tensor_tensor(um[:, i, :], DL[:, i, :], pc("mu", i), um[:, i, :], MUL, ADD)
                done(ins, "rw.mixed")

                def over_gv(x):
                    return x.unsqueeze(2).broadcast_to([P, TD, 64])

                fill("gl2")
                dve.wait_ge(*loads(l, 11))
                link(v.tensor_tensor(GS, GS, over_gv(GDX), MUL))
                dve.wait_ge(*pe_of.at("gl.dvb", l))
                g3 = mW[:, 0, :].rearrange("p (b v) -> p b v", b=TD)
                link(v.tensor_tensor(GXX[:, 0, :, :], g3, over_gv(k[:, TP:T]), MUL))
                done(v.tensor_tensor(GS, GS, GXX[:, 0, :, :], ADD), "gl.dec")
                link(v.tensor_tensor(GXX[:, 0, :, :], GS, over_gv(q[:, TP:T]), MUL))
                done(v.tensor_scalar(GXX[:, 0, :, :], GXX[:, 0, :, :], 32 ** -0.5, None, MUL), "gl.dq")
                dve.wait_ge(*pe_of.at("gl.dy", l))
                link(v.tensor_tensor(GXX, w4(0), unit(), MUL))
                done(v.tensor_reduce(GYD, GXX, AX_X, ADD), "gl.out")
                head_norm("n2", slice(4, 6), 1e-6, centre=False)
                for j in range(2):
                    ins = v.scalar_tensor_tensor(GGS[:, j, :], OO[:, 4 + j, :], pc("gnw", j), GGS[:, j, :], MUL, MUL)
                done(ins, "gl.branch")
                dve.wait_ge(state_out, 16 * (12 * l + 9))
                rr, kx, vv = U[:, TR:TR + 2, :], U[:, TK:TK + 2, :], U[:, TV:TV + 2, :]
                dve.wait_ge(*act_of.at("rw.lora", l))
                done(v.tensor_scalar(TH[64:128, :], TH[64:128, :], 0.5, 0.5, MUL, ADD), "rw.sg")
                fill("rw1")
                dve.wait_ge(*act_of.at("rw.wa", l))
                v.tensor_scalar(LW, LW, 1.0, -0.5 * float(np.exp(-0.5)), ADD, MUL)
                link(v.tensor_scalar(AA, AA, 0.5, 0.5, MUL, ADD))
                for j in range(2):
                    ins = v.tensor_scalar(K4[:, j, :], AA[:, j, :], -1.0, pc("ka", j), ADD, MUL)
                link(ins)
                link(v.scalar_tensor_tensor(K4, K4, 1.0, kx, ADD, MUL))
                for j in range(2):
                    ins = v.scalar_tensor_tensor(RKV[:, j, :], rr[:, j, :], pc("rk", j), K4[:, j, :], MUL, MUL)
                done(ins, "rw.rk")
                dve.wait_ge(*pe_of.at("rw.ksum", l))
                done(v.tensor_scalar(NRM, mW[:, 2:4, 0:T], 1e-24, None, MAX), "rw.ksum")
                dve.wait_ge(*act_of.at("rw.ksqrt", l))
                link(v.reciprocal(NRM, NRM))
                for j in range(2):
                    ins = v.scalar_tensor_tensor(KKN[:, j, :], kx[:, j, :], pc("kk", j), NRM[:, j, :], MUL, MUL)
                link(ins)
                dve.wait_ge(*pe_of.at("rw.bonus", l))
                done(v.tensor_tensor(kx, mW[:, 0:2, 0:T], vv, MUL), "rw.bonus")
                for j in range(2):
                    ins = v.tensor_tensor_scan(RKV[:, j, 0:TP], C("reset", TP), LW[:, j, 0:TP], 0.0, MUL, ADD)
                link(ins)
                done(v.tensor_tensor(BT, RKV[:, :, 0:TP], LW[:, :, 0:TP], SUB), "rw.cum")
                fill("rw2")
                v.tensor_tensor(DKA, KKN[:, :, TP:T], AA[:, :, TP:T], MUL)
                link(v.tensor_tensor(DY, unit(), over_v(vv[:, :, TP:T]), MUL))
                dve.wait_ge(*loads(l, 12))
                done(v.tensor_tensor(DX, DS, over_v(KKN[:, :, TP:T]), MUL), "rw.dx")
                dve.wait_ge(*act_of.at("rw.exp", l))
                fill("rw3")
                link(v.tensor_tensor(DS, DS, over_v(DW), MUL))
                dve.wait_ge(*pe_of.at("rw.dsa", l))
                link(v.tensor_tensor(DX, w4(0), over_v(DKA), MUL))
                link(v.tensor_tensor(DS, DS, DX, SUB))
                link(v.tensor_tensor(DX, w4(2), over_v(K4[:, :, TP:T]), MUL))
                done(v.tensor_tensor(DS, DS, DX, ADD), "rw.dec")
                done(v.tensor_tensor(DX, DS, over_v(rr[:, :, TP:T]), MUL), "rw.dr")
                fill("rw4")
                dve.wait_ge(*pe_of.at("rw.dy", l))
                link(v.tensor_tensor(DX, w4(0), unit(), MUL))
                done(v.tensor_reduce(OO[:, 0:2, TP:T], DX, AX_X, ADD), "rw.dout")

                def halves(x):
                    return x[:, :, 0:TP].rearrange("p j (c t) -> p j c t", c=2)

                e_in, e_neg, e_ex = EXPS[:, 0, :, :], EXPS[:, 1, :, :], EXPS[:, 2, :, :]
                v.tensor_tensor(AR[:, :, :, 0, :], halves(KKN), halves(e_ex), MUL)
                v.tensor_tensor(AR[:, :, :, 1, :], halves(rr), halves(e_in), MUL)
                v.tensor_tensor(KTL, K4[:, :, 0:TP], e_neg, MUL)
                v.tensor_copy(PLAST, e_in.rearrange("p j (c t) -> p j c t", c=NC)[:, :, :, CH - 1])
                link(v.tensor_tensor(NRM[:, :, 0:TP], KKN[:, :, 0:TP], AA[:, :, 0:TP], MUL))
                link(v.tensor_tensor(BT, NRM[:, :, 0:TP], e_neg, MUL))
                for j in range(2):
                    plast = PLAST[:, j, :].unsqueeze(2).broadcast_to([P, NC, CH])
                    v.scalar_tensor_tensor(chunks4(B2[:, j, :]), chunks4(BT[:, j, :]), -1.0, plast, MUL, MUL)
                    ins = v.tensor_tensor(chunks4(K2[:, j, :]), chunks4(KTL[:, j, :]), plast, MUL)
                done(ins, "rw.ops")
                fill("rw5")
                dve.wait_ge(*pe_of.at("rw.turn", l))
                dve.wait_ge(state_out, 16 * (12 * l + 11))
                for i, dst in enumerate((ATK, BTK, KTK, VTK)):
                    v.tensor_copy(dst, mW[:, i, :].rearrange("p (a b) -> p a b", a=2))
                done(v.memset(SS[:, :, 0, :], 0.0), "rw.turned")
                for g in range(2):
                    dve.wait_ge(*pe_of.at("rw.bk", l, g))
                    if g:
                        dve.wait_ge(*pe_of.at("rw.y", l, 0))
                    v.tensor_tensor(NB, WF[:, 0:1024].rearrange("p (h t) -> p h t", h=4), mid(C("mb", 256), 4), MUL)
                    done(v.tensor_tensor(MKS, WF[:, 1024:2048].rearrange("p (h t) -> p h t", h=4), mid(C("mk", 256), 4), MUL),
                         "rw.bk", g)
                    dve.wait_ge(*pe_of.at("rw.l", l, g))
                    for e in range(2):
                        m2 = mW[:, e, 0:256].rearrange("p (h t) -> p h t", h=2)
                        v.tensor_tensor(ND[:, 2 * e:2 * e + 2, :], m2, mid(C("ml16"), 2), MUL)
                        v.tensor_tensor(NO[:, 2 * e:2 * e + 2, :], m2, mid(C("mlo"), 2), MUL)
                    v.tensor_tensor(QT, NB[:, :, 0:P], mid(C("ident"), 4), ADD)
                    v.tensor_copy(VW[:, 0, :], ATK[:, g, :])
                    done(v.tensor_copy(VW[:, 1, :], mW[:, 2, 0:256]), "rw.l", g)
                    fill(f"g{g}a")
                    b2 = mW[:, 2, :].rearrange("p (h t) -> p h t", h=4)
                    for k in range(3):
                        dve.wait_ge(*pe_of.at(("rw.p4", "rw.p8", "rw.q")[k], l, g))
                        done(v.tensor_tensor(QT, QT, b2, ADD), f"rw.q{k}", g)
                    fill(f"g{g}b")
                    b1 = mW[:, 1, :].rearrange("p (a n) -> p a n", a=2)
                    b3 = mW[:, 3, :].rearrange("p (a n) -> p a n", a=2)
                    dve.wait_ge(*pe_of.at("rw.et", l, g))
                    done(v.tensor_copy(VW, b1), "rw.v0", g)
                    for k in range(3):
                        dve.wait_ge(*pe_of.at("rw.e", l, 3 * g + k))
                        done(v.tensor_tensor(YW, (b3, b1, b3)[k], VW, ADD), "rw.e", 3 * g + k)
                    fill(f"g{g}c")
                    fill(f"g{g}d")
                    for c in (2 * g, 2 * g + 1):
                        q0 = 64 * (c % 2)
                        dve.wait_ge(*pe_of.at("rw.z", l, c))
                        done(v.tensor_tensor(ZZ[q0:q0 + 64, g, :].rearrange("p (j e d) -> p e j d", e=2, j=2),
                                             mW[q0:q0 + 64, 1:4:2, 0:128].rearrange("p e (j d) -> p e j d", j=2),
                                             YW[q0:q0 + 64, 1, :].rearrange("p (j e d) -> p e j d", e=2, j=2), ADD),
                             "rw.z", c)
                        dve.wait_ge(*pe_of.at("rw.s", l, c))
                        for j in range(2):
                            ins = v.scalar_tensor_tensor(SS[:, j, c + 1, :], SS[:, j, c, :], PLAST[:, j, c:c + 1],
                                                         mW[:, 0, 64 * j:64 * j + 64], MUL, ADD)
                        done(ins, "rw.state", c)
                    dve.wait_ge(*pe_of.at("rw.y", l, g))
                    done(v.tensor_copy(OO[:, 0:2, P * g:P * g + P], mW[:, 2, 0:256].rearrange("p (j t) -> p j t", j=2)),
                         "rw.y", g)
                fill("tail")
                head_norm("n0", slice(0, 2), 64e-5)
                for j in range(2):
                    ins = v.tensor_scalar(OO[:, j, :], OO[:, j, :], pc("lnw", j), pc("lnb", j), MUL, ADD)
                link(ins)
                link(v.tensor_tensor(OO[:, 0:2, :], OO[:, 0:2, :], kx, ADD))
                done(v.tensor_tensor(rr, OO[:, 0:2, :], GG, MUL), "rw.branch")
                fill("end")
                for i in range(KT):
                    dve.wait_ge(*pe_of.at("mg.out", l, i))
                    done(v.scalar_tensor_tensor(SQ8[:, i, :], X[:, i, :], 2 * ALPHA, acc("out", l, i), MUL, ADD), "mg.out", i)

                def split_ffn(i):
                    dve.wait_ge(*act_of.at("ff.hi", l, i))
                    v.tensor_tensor(FWL[:, i % 2, :], ring_slot((ffn_at + i) % SLOTS), FWH[:, i % 2, :].bitcast(F32), SUB)\
                        .then_inc(*dve_of.step("ff.lo", i))

                def norm(i):
                    halves = [slice(0, 4), slice(4, 8)]
                    dve.wait_ge(*pe_of.at("ln.mean", l, i))
                    for h in range(2):
                        v.tensor_tensor(SQ8[:, halves[h], :], SQ8[:, halves[h], :], mid(mW[:, 0, 0:T], 4), SUB)\
                            .then_inc(*dve_of.step("ln.centred", 2 * i + h))
                    dve.wait_ge(*dve_of.at("ln.centred", l, 2 * i + 1))
                    if l == i == 0:
                        split_ffn(0)
                    dve.wait_ge(*act_of.at("ln.sqrt", l, i))
                    link(v.reciprocal(V8[:, 1, :], V8[:, 1, :]))
                    for h in range(2):
                        v.tensor_tensor(SQ8[:, halves[h], :], SQ8[:, halves[h], :], mid(V8[:, 1, :], 4), MUL)\
                            .then_inc(*dve_of.step("ln.scaled", 2 * i + h))
                    if l or i:
                        dve.wait_ge(*act_of.at("ln.norm", l, i))

                norm(0)
                if l == 0:
                    for h in range(2):
                        dve.wait_ge(*act_of.at("ff.xh", l, h))
                        v.tensor_tensor(XL[:, 4 * h:4 * h + 4, :], X[:, 4 * h:4 * h + 4, :],
                                        XH[:, 4 * h:4 * h + 4, :].bitcast(F32), SUB).then_inc(*dve_of.step("ff.xl", h))
                    split_ffn(1)
                    for c in range(FC):
                        split_ffn(2 * c + 2)
                        dve.wait_ge(*act_of.at("ff.tanh", l, c))
                        for q in range(2):
                            ins = v.scalar_tensor_tensor(FTH[:, c % 2, q, :], FTH[:, c % 2, q, :], 1.0,
                                                         ff_acc(c, q), ADD, MUL)
                        link(ins)
                        dve.wait_ge(*pe_of.at("ff.part", l, 2 * c + 1))
                        for q in range(2):
                            ins = v.tensor_tensor(HF[:, c % 2, q, :], FTH[:, c % 2, q, :], ff_acc(c, 2 + q), MUL)
                        done(ins, "ff.hid", c)
                        tiles = slice(2 * c, 2 * c + 2)
                        link(v.tensor_copy(HH[:, tiles, :], HF[:, c % 2, :, :]))
                        v.tensor_tensor(HL[:, tiles, :], HF[:, c % 2, :, :], HH[:, tiles, :].bitcast(F32), SUB)\
                            .then_inc(*dve_of.step("ff.hl", c))
                        split_ffn(2 * c + 3)
                    split_ffn(2 * FC + 2)
                    for p in range(4):
                        if p < 3:
                            split_ffn(2 * FC + 3 * p + 3)
                        for i in range(2 * p, 2 * p + 2):
                            dve.wait_ge(*pe_of.at("ff.down", l, i))
                            done(v.scalar_tensor_tensor(SQ8[:, i, :], X[:, i, :], 2 * ALPHA, acc("d", l, i), MUL, ADD),
                                 "ff.down", i)
                        if p < 3:
                            split_ffn(2 * FC + 3 * p + 4)
                            split_ffn(2 * FC + 3 * p + 5)
                else:
                    moe_vector(dve, v, link, linked)
                norm(1)


        def moe_tensor(pe, mm, mean):
            for i in range(3):
                n = P if i < 2 else TD
                if i == 2:
                    pe.wait_ge(moe_setup_dve, 1)
                for k in range(KT):
                    ins = nc.tensor.transpose(WF[0:n, 1024 * (i % 2) + P * k:1024 * (i % 2) + P * k + P],
                                              X[:, k, P * i:P * i + n], C("ident"))
                ins.then_inc(moe_setup_pe, 1)
            pe.wait_ge(router_in, 32)
            for i in range(3):
                n = P if i < 2 else TD
                for k in range(KT):
                    ins = mm(mA[0:n, 0, NE * i:NE * i + NE], X[:, k, P * i:P * i + n], router[:, k, :], k == 0, k == KT - 1)
            ins.then_inc(moe_setup_pe, 1)
            pe.wait_ge(moe_setup_dve, 9)
            ones = C("ones", P)
            for i in range(4):
                m = (P, P, TD, P)[i]
                for k in range(min(i + 1, 3)):
                    n = P if k < 2 else TD
                    w = C("tri", m, n) if k == i else con[0:n, CC["ones"]:CC["ones"] + m]
                    ins = mm(mA[0:m, 1, NE * i:NE * i + NE], w, MASK[0:n, k, :], k == 0, k == min(i, 2))
            ins.then_inc(moe_setup_pe, 1)
            R = rounds_of(pe)

            def turn_placement(n):
                pe.wait_ge(place_ready, n + 1)
                for i in range(3):
                    m = P if i < 2 else TD
                    ins = nc.tensor.transpose(mW[:, 2, P * i:P * i + m], PG[0:m, i, :], C("ident", m, m))
                ins.then_inc(placeT_pe, 1)

            def gather(n, part, tiles=range(4)):
                if part and tiles[0] == 0:
                    pe.wait_ge(placeT_ready, n + 1)
                for k in tiles:
                    for i in range(3):
                        m = P if i < 2 else TD
                        f = P * (4 * part + k)
                        ins = mm(mW[:, 3 - part, P * k:P * k + P], XT[0:m, i, f:f + P], PL[0:m, i, :], i == 0, i == 2)
                if tiles[-1] == 3:
                    ins.then_inc(gathered, 1)

            def scatter(n, i, placed):
                pe.wait_ge(scatter_added, n * 4 + i // 2)
                for q in range(2):
                    mm(mW[:, 2 + q, 0:T], YE[:, P * (i + q):P * (i + q) + P], placed).then_inc(scattered, 1)

            turn_placement(0)
            gather(0, 0)
            gather(0, 1)
            with pe.Fori(0, R * (NE // 2)) as m:
                for u in range(2):
                    n = 2 * m + u

                    def turn_hidden(c):
                        pe.wait_ge(hidden, n * FC + (c + 1))
                        b = (FC * u + c) % 2
                        for q in range(2):
                            ins = nc.tensor.transpose(mA[:, 2 + b, P * q:P * q + P], HT[:, b, P * q:P * q + P], C("ident"))
                        ins.then_inc(hidden_turned, 1)

                    def down(c):
                        pe.wait_ge(turned_kept, n * FC + (c + 1))
                        if c == 0:
                            pe.wait_ge(down_kept, n)
                        i = 3 * (FC * u + c) + 2
                        pe.wait_ge(*landed(m, i))
                        wt = ring[:, SLOT_OF[i], :]
                        for q in range(2):
                            for b in range(2):
                                ins = mm(mW[:, b, :], HE[:, (FC * u + c) % 2, P * q:P * q + P],
                                         wt[:, D * q + 512 * b:D * q + 512 * b + 512], c == 0 and q == 0, c == FC - 1 and q == 1)
                        ins.then_inc(down_done, 1)

                    for c in range(FC):
                        if 2 <= c < 6:
                            pe.wait_ge(down_kept, n)
                            scatter(n, 2 * (c - 2), PGT[:, 1 - u, :])
                        if c == 7:
                            pe.wait_ge(scatter_added, n * 4 + 4)
                            turn_placement(n + 1)
                        out = mA[:, (FC * u + c) % 2, :]
                        for part in range(2):
                            if c == 0:
                                pe.wait_ge(gather_split, 2 * n + (part + 1))
                            pe.wait_ge((split0, split1)[part], n * FC + (c + 1 + FC))
                            for k in range(4):
                                for x, w in ((XEH, WH), (XEH, WL), (XEL, WH)):
                                    ins = mm(out, x[:, u, 4 * part + k, :], w[:, part, 512 * k:512 * k + 512],
                                             part == k == 0 and x is XEH and w is WH, part == 1 and k == 3 and x is XEL)
                            ins.then_inc((in0_done, in1_done)[part], 1)
                            if part == 0 and c:
                                turn_hidden(c - 1)
                        if c:
                            down(c - 1)
                        if c == FC - 2:
                            gather(n + 1, 0)
                    gather(n + 1, 1, range(0, 2))
                    turn_hidden(FC - 1)
                    gather(n + 1, 1, range(2, 4))
                    down(FC - 1)
            pe.wait_ge(down_kept, R * NE)
            pe.wait_ge(gather_split, R * (2 * NE) + 2)
            for i in range(0, KT, 2):
                scatter(R * NE, i, PGT[:, 1, :])
                if i:
                    mean(1, i - 2)
            pe.wait_ge(scatter_added, R * (NE * 4) + 4)
            mean(1, KT - 2)

        @block.tensor
        def _(pe):
            ck = [0]

            def mm(out, w, x, start=True, stop=True):
                return nc.tensor.matmul(out, w, x, start=start, stop=stop, skip_group_check=True)

            def turn(out, x, n=P):
                return nc.tensor.transpose(out, x, C("ident", n, n))

            def chunk():
                i = ck[0]
                ck[0] += 1
                pe.wait_ge(slot_in[i % SLOTS], 16 * (i // SLOTS + 1))
                return ring_slot(i % SLOTS).rearrange("p (k n) -> p k n", k=KT)

            def free(n):
                if n >= 4:
                    pe.wait_ge(*emptied[n - 4])

            def tile(kind, l, i, w, x):
                free(numbers[kind, l, i])
                for k, (wk, xk) in enumerate(zip(w, x)):
                    if k == 4 and rest_of_x:
                        pe.wait_ge(*rest_of_x.pop())
                    ins = mm(acc(kind, l, i), wk, xk, k == 0, k == len(w) - 1)
                return ins

            def pair(kind, name, l, i0, x, rows=KT):
                wt = chunk()
                for q in range(2):
                    tile(kind, l, i0 + q, [wt[:, k, P * q:P * q + P] for k in range(rows)], x)\
                        .then_inc(*pe_of.step(name, i0 + q))

            rest_of_x = []
            bo = C("bo")
            pe.wait_ge(x_in, 16)
            for l in range(DEPTH):
                xs = [X[:, k, :] for k in range(KT)]
                if l:
                    pe.wait_ge(*act_of.at("ln.half", l - 1, 1))
                slot_of = {}

                def mean(i, k0):
                    for k in (k0, k0 + 1):
                        ins = mm(mW[:, 0, 0:T], C("mean"), SQ8[:, k, :], k == 0, k == KT - 1)
                    if k == KT - 1:
                        ins.then_inc(*pe_of.step("ln.mean", i))

                def streamed(kind, i, item):
                    if kind == "u":
                        pair("u", "u.tile", l, i, xs)
                        return
                    _, g, q2 = item
                    if q2 == 0 and item[0] != "gate" and g not in slot_of:
                        slot_of[g] = chunk().rearrange("p k n -> p (k n)").rearrange("p (k n) -> p k n", k=2)
                        pe.wait_ge(*dve_of.at({RG: "rg.out", ML: "ml.branch", GL: "gl.branch", RW: "rw.branch"}[g], l))
                    if kind == "gate":
                        pair("gate", "gate.tile", l, i, xs)
                        return
                    for q in range(2):
                        f = P * (2 * q2 + q)
                        tile("up", l, i + q, [slot_of[g][:, k, f:f + P] for k in range(2)], [BRANCH[g][:, k, :] for k in range(2)])\
                            .then_inc(*pe_of.step("mg.up", i + q))

                fill = filler(streamed)

                def head_norm(name, tiles, centre=True):
                    if centre:
                        for k, i in enumerate(tiles):
                            ins = mm(mW[:, k, 0:T], C("bom"), OO[:, i, :])
                        ins.then_inc(*pe_of.step(f"{name}.mean"))
                    pe.wait_ge(*act_of.at(f"{name}.sq", l))
                    for k, i in enumerate(tiles):
                        ins = mm(mW[:, 2 + k, 0:T], C("bom"), OT[:, i, :])
                    ins.then_inc(*pe_of.step(f"{name}.var"))

                fill("start")
                pe.wait_ge(*loads(l, 9))
                pe.wait_ge(const_in, 16)
                pe.wait_ge(*act_of.at("u.tile", l, 1))
                mm(mW[:, 0, 0:T], alup[64:80, :], U[64:80, TMI, :]).then_inc(*pe_of.step("lg.alpha"))
                fill("alpha")
                pe.wait_ge(*dve_of.at("rg.conv", l))
                pe.wait_ge(*dve_of.at("lg.in", l))
                for j in range(4):
                    ins = mm(mW[:, j, 0:T], rgw[:, j, :], RC[:, j % 2, :])
                ins.then_inc(*pe_of.step("rg.gates"))
                for point in ("rg1", "rg2", "rg3", "ml1"):
                    fill(point)
                pe.wait_ge(*dve_of.at("ml.qk", l))
                pe.wait_ge(*act_of.at("rg.tanh", l))
                for j in range(2):
                    for c in range(2):
                        turn(mW[:, 0, 256 * c + P * j:256 * c + P * j + P], U[:, TMV + j, P * c:P * c + P])
                        turn(mW[:, 1, 256 * c + P * j:256 * c + P * j + P], CV[:, 2 + j, P * c:P * c + P])
                pe.wait_ge(*dve_of.at("ml.rows", l))
                pe.wait_ge(*act_of.at("ml.exps", l))
                for c in range(2):
                    turn(mW[:, 2, 4 * c:4 * c + 4], MR[0:4, 2 * T + P * c:2 * T + P * c + P], 4)
                fill("ml2")
                pe.wait_ge(*dve_of.at("ml.dec_rows", l))

                def spread(bank, at, width, x):
                    for h in range(4):
                        j, p0 = h // 2, 64 * (h % 2)
                        one = con[0:4, CC["ident"] + h:CC["ident"] + h + 1].broadcast_to([4, 64])
                        ins = mm(mW[p0:p0 + 64, bank(j), at(j):at(j) + width], one, x)
                    return ins

                ins = spread(lambda j: 3, lambda j: 24 * j, 24, MR[0:4, 5 * T:5 * T + 24])
                ins.then_inc(*pe_of.step("ml.turn"))
                fill("ml3")
                pe.wait_ge(*dve_of.at("ml.gcol", l))
                qq, kk = CV[:, 0:2, :], CV[:, 2:4, :]
                for h in range(4):
                    j, p0, b = h // 2, 64 * (h % 2), h % 2
                    if h >= 2:
                        pe.wait_ge(*act_of.at("ml.d", l, h - 2))
                    one = con[0:4, CC["ident"] + h:CC["ident"] + h + 1].broadcast_to([4, P])
                    mm(mW[:, b, 0:256], one, MR[0:4, 3 * T:3 * T + TP], True, False)
                    mm(mW[:, b, 0:128], C("ident"), C("neg"), False, True)
                    mm(mW[:, b, 256:384], one, MR[0:4, 3 * T + P:3 * T + TP], True, False)
                    mm(mW[:, b, 256:384], C("ident"), C("neg"), False, True).then_inc(*pe_of.step("ml.logd", h))
                    if h >= 2:
                        pe.wait_ge(*dve_of.at("ml.sd", l, h - 2))
                    mm(mW[:, 2 + b, 0:256], kk[p0:p0 + 64, j, 0:P], qq[p0:p0 + 64, j, 0:TP])
                    mm(mW[:, 2 + b, 256:384], kk[p0:p0 + 64, j, P:TP], qq[p0:p0 + 64, j, P:TP])\
                        .then_inc(*pe_of.step("ml.qk", h))
                fill("ml4")
                pe.wait_ge(*dve_of.at("ml.kw", l, 3))
                for h in range(4):
                    j, p0 = h // 2, 64 * (h % 2)
                    for b, lhs in ((j, None), (2 + j, C("ones", 64))):
                        for c in range(2):
                            w = MVT[:, c, 64 * h:64 * h + 64] if lhs is None else lhs
                            ins = mm(mW[p0:p0 + 64, b, P * c:TP], w, MSD[:, h, 256 * c:256 + P * c], c == 0, c == 1)
                ins.then_inc(*pe_of.step("ml.num"))
                pe.wait_ge(*act_of.at("ml.abs", l))
                ins = spread(lambda j: 2 + j, lambda j: 0, TP, MR[0:4, 4 * T:4 * T + TP])
                ins.then_inc(*pe_of.step("ml.emb"))
                fill("ml5")
                pe.wait_ge(*dve_of.at("ml.h", l))
                for h in range(4):
                    j, p0 = h // 2, 64 * (h % 2)
                    for c in range(2):
                        mm(mW[p0:p0 + 64, 0, P * j:P * j + 64], MKT[:, c, 64 * h:64 * h + 64], MVT[:, c, 64 * h:64 * h + 64],
                           c == 0, c == 1)
                    for c in range(2):
                        ins = mm(mW[p0:p0 + 64, 0, P * j + 64:P * j + 65], MKT[:, c, 64 * h:64 * h + 64], C("ones", 1),
                                 c == 0, c == 1)
                ins.then_inc(*pe_of.step("ml.c"))
                fill("ml6")
                pe.wait_ge(*dve_of.at("ml.cout", l))
                pe.wait_ge(*dve_of.at("ml.dv", l))
                for j in range(2):
                    ins = mm(mW[:, j, :], bo, MX[:, j, :, :].rearrange("p b v -> p (b v)"))
                ins.then_inc(*pe_of.step("ml.dvb"))
                pe.wait_ge(*dve_of.at("ml.dq", l))
                for j in range(2):
                    mm(mW[:, j, :], bo, MX[:, j, :, :].rearrange("p b v -> p (b v)"))
                for j in range(2):
                    ins = mm(mW[:, 2, 8 * j:8 * j + 8], bo, MDEN[:, j, TD:2 * TD])
                ins.then_inc(*pe_of.step("ml.dnum"))
                pe.wait_ge(*dve_of.at("ml.out", l))
                head_norm("n1", (2, 3))
                pe.wait_ge(*dve_of.at("gl.ops", l))
                for c in range(2):
                    for j in range(2):
                        turn(mW[:, 0, 256 * c + P * j:256 * c + P * j + P], U[:, TGV + j, P * c:P * c + P])
                    ins = turn(mW[:, 1, P * c:P * c + P], GKH[:, P * c:P * c + P])
                ins.then_inc(*pe_of.step("gl.turn"))
                pe.wait_ge(*dve_of.at("gl.turned", l))
                for h in range(4):
                    for c in range(2):
                        ins = mm(mW[:, h, P * c:P * c + P], GK[32 * h:32 * h + 32, P * c:P * c + P],
                                 GQ[32 * h:32 * h + 32, P * c:P * c + P])
                ins.then_inc(*pe_of.step("gl.attn"))
                fill("gl1")
                pe.wait_ge(*dve_of.at("gl.attn", l))
                for c in range(NC):
                    q0 = 64 * (c % 2)
                    ins = mm(mW[:, c % 2, 256 * (c // 2):256 * (c // 2) + 256], GKT[q0:q0 + 64, c // 2, :],
                             GVT[q0:q0 + 64, c // 2, :])
                ins.then_inc(*pe_of.step("gl.kv"))
                pe.wait_ge(*dve_of.at("gl.state", l))
                for j in range(2):
                    for c2 in range(2):
                        for h in (2 * j, 2 * j + 1):
                            p0 = 64 * (h % 2)
                            mm(mW[p0:p0 + 64, 2 + j, P * c2:P * c2 + P], GVT[:, c2, 64 * h:64 * h + 64],
                               GAT[:, c2, P * h:P * h + P], True, False)
                        for c in (2 * c2, 2 * c2 + 1):
                            ins = mm(mW[:, 2 + j, CH * c:CH * c + CH], GSS[:, c, P * j:P * j + P],
                                     GQH[:, CH * c:CH * c + CH], False, c % 2 == 1)
                ins.then_inc(*pe_of.step("gl.y"))
                pe.wait_ge(*dve_of.at("gl.dv", l))
                fill("gl2")
                for j in range(2):
                    ins = mm(mW[:, 0, :], con[:, CC["gv"] + P * j:CC["gv"] + P * j + P],
                             GXX[:, j, :, :].rearrange("p b v -> p (b v)"), j == 0, j == 1)
                ins.then_inc(*pe_of.step("gl.dvb"))
                pe.wait_ge(*dve_of.at("gl.dq", l))
                for j in range(2):
                    ins = mm(mW[:, j, :], con[:, CC["gy"] + P * j:CC["gy"] + P * j + P],
                             GXX[:, 0, :, :].rearrange("p b v -> p (b v)"))
                ins.then_inc(*pe_of.step("gl.dy"))
                pe.wait_ge(*dve_of.at("gl.out", l))
                head_norm("n2", (4, 5), centre=False)
                pe.wait_ge(*dve_of.at("n2.var", l))
                pe.wait_ge(*act_of.at("rw.lora", l))
                for j in range(2):
                    mm(mW[:, j, 0:T], lora[0:32, P * j:P * j + P], TH[0:32, :])
                    ins = mm(mW[:, 2 + j, 0:T], lora[32:64, P * j:P * j + P], U[32:64, TLO, :])
                ins.then_inc(*pe_of.step("rw.wa"))
                fill("rw1")
                pe.wait_ge(*act_of.at("rw.wa", l))
                pe.wait_ge(*dve_of.at("rw.sg", l))
                for j in range(2):
                    ins = mm(mW[:, j, 0:T], lora[64:128, P * j:P * j + P], TH[64:128, :])
                ins.then_inc(*pe_of.step("rw.g"))
                for j in range(2):
                    ins = mm(mW[:, 2 + j, 0:T], bo, NRM[:, j, :])
                ins.then_inc(*pe_of.step("rw.ksum"))
                pe.wait_ge(*act_of.at("rw.g", l))
                pe.wait_ge(*dve_of.at("rw.rk", l))
                for j in range(2):
                    ins = mm(mW[:, j, 0:T], bo, RKV[:, j, :])
                ins.then_inc(*pe_of.step("rw.bonus"))
                fill("rw2")
                pe.wait_ge(*dve_of.at("rw.dx", l))
                for j in range(2):
                    mm(mW[:, j, :], bo, DX[:, j, :, :].rearrange("p b v -> p (b v)"))
                for j in range(2):
                    ins = mm(mW[:, 2 + j, :], bo, DY[:, j, :, :].rearrange("p b v -> p (b v)"))
                ins.then_inc(*pe_of.step("rw.dsa"))
                fill("rw3")
                fill("rw4")
                pe.wait_ge(*dve_of.at("rw.dr", l))
                for j in range(2):
                    ins = mm(mW[:, j, :], bo, DX[:, j, :, :].rearrange("p b v -> p (b v)"))
                ins.then_inc(*pe_of.step("rw.dy"))
                fill("rw5")
                pe.wait_ge(*dve_of.at("rw.ops", l))
                for c in range(2):
                    for j in range(2):
                        o = slice(256 * c + P * j, 256 * c + P * j + P)
                        turn(mW[:, 0, o], AR[:, j, c, 0, :])
                        turn(mW[:, 1, o], B2[:, j, P * c:P * c + P])
                        turn(mW[:, 2, o], K2[:, j, P * c:P * c + P])
                        ins = turn(mW[:, 3, o], U[:, TV + j, P * c:P * c + P])
                ins.then_inc(*pe_of.step("rw.turn"))
                pe.wait_ge(*dve_of.at("rw.turned", l))
                for g in range(2):
                    tok = slice(P * g, P * g + P)
                    if g:
                        pe.wait_ge(*dve_of.at("rw.y", l, 0))
                    for h in (0, 2, 1, 3):
                        j, e, p0 = h // 2, h % 2, 64 * (h % 2)
                        ar2 = AR[p0:p0 + 64, j, g, :, :].rearrange("p a t -> p (a t)")
                        mm(mW[:, e, 256 * j:256 * j + 256], BT[p0:p0 + 64, j, tok], ar2)
                        ins = mm(mW[:, 2 + e, 256 * j:256 * j + 256], KTL[p0:p0 + 64, j, tok], ar2)
                    ins.then_inc(*pe_of.step("rw.bk", g))
                    pe.wait_ge(*dve_of.at("rw.bk", l, g))
                    for n in range(4):
                        e, j = divmod(n, 2)
                        h = 2 * j + e
                        mm(mW[:, e, P * j:P * j + P], AR[64 * e:64 * e + 64, j, g, 0, :], BT[64 * e:64 * e + 64, j, tok])
                        ins = mm(mW[:, 2, 64 * h:64 * h + 64], MKS[:, n, 0:P], VTK[:, g, 64 * h:64 * h + 64])
                    ins.then_inc(*pe_of.step("rw.l", g))
                    fill(f"g{g}a")
                    pe.wait_ge(*dve_of.at("rw.l", l, g))

                    def four(bank, w, x):
                        for n in range(4):
                            ins = mm(mW[:, bank, P * n:P * n + P], w[:, n, 0:P], x[:, n, 0:P])
                        return ins

                    def apply(bank, w, x):
                        for n in range(4):
                            h = 2 * (n % 2) + n // 2
                            o = mW[:, bank, :].rearrange("p (a n) -> p a n", a=2)[:, :, 64 * h:64 * h + 64]
                            ins = mm(o, w[:, n, 0:P], x[:, :, 64 * h:64 * h + 64])
                        return ins

                    four(0, NB, ND)
                    four(1, ND, NB).then_inc(*pe_of.step("rw.p2", g))
                    pe.wait_ge(*act_of.at("rw.p2", l, g))
                    four(0, P2T, P2)
                    four(1, P2, P2T)
                    four(2, P2, QT).then_inc(*pe_of.step("rw.p4", g))
                    fill(f"g{g}b")
                    pe.wait_ge(*act_of.at("rw.p4", l, g))
                    pe.wait_ge(*dve_of.at("rw.q0", l, g))
                    four(0, P4T, P4)
                    four(2, P4, QT).then_inc(*pe_of.step("rw.p8", g))
                    pe.wait_ge(*act_of.at("rw.p8", l, g))
                    pe.wait_ge(*dve_of.at("rw.q1", l, g))
                    four(2, P2, QT).then_inc(*pe_of.step("rw.q", g))
                    pe.wait_ge(*dve_of.at("rw.q2", l, g))
                    four(0, NO, QT)
                    apply(1, QT, VW).then_inc(*pe_of.step("rw.et", g))
                    fill(f"g{g}c")
                    pe.wait_ge(*act_of.at("rw.et", l, g))
                    pe.wait_ge(*dve_of.at("rw.v0", l, g))
                    for k in range(3):
                        apply((3, 1, 3)[k], ET, YW if k else VW).then_inc(*pe_of.step("rw.e", 3 * g + k))
                        pe.wait_ge(*dve_of.at("rw.e", l, 3 * g + k))
                    for j in range(2):
                        ins = turn(mW[:, 2, P * j:P * j + P], YW[:, 0, P * j:P * j + P])
                    ins.then_inc(*pe_of.step("rw.wt", g))
                    fill(f"g{g}d")
                    pe.wait_ge(*act_of.at("rw.wt", l, g))
                    for c in (2 * g, 2 * g + 1):
                        q0 = 64 * (c % 2)
                        if c:
                            pe.wait_ge(*dve_of.at("rw.state", l, c - 1))
                        for n in range(4):
                            e, j = divmod(n, 2)
                            ins = mm(mW[q0:q0 + 64, 1 + 2 * e, 64 * j:64 * j + 64], WT[64 * e:64 * e + 64, j, q0:q0 + 64],
                                     SS[64 * e:64 * e + 64, j, c, :])
                        ins.then_inc(*pe_of.step("rw.z", c))
                        pe.wait_ge(*dve_of.at("rw.z", l, c))
                        for h in range(4):
                            j, e = divmod(h, 2)
                            out = mW[64 * e:64 * e + 64, 0, 64 * j:64 * j + 64]
                            mm(out, KTK[q0:q0 + 64, g, 64 * h:64 * h + 64], VTK[q0:q0 + 64, g, 64 * h:64 * h + 64], True, False)
                            ins = mm(out, BTK[q0:q0 + 64, g, 64 * h:64 * h + 64],
                                     ZZ[q0:q0 + 64, g, 64 * h:64 * h + 64], False, True)
                        ins.then_inc(*pe_of.step("rw.s", c))
                    for h in range(4):
                        j, e = divmod(h, 2)
                        n, p0 = 2 * e + j, 64 * e
                        mm(mW[p0:p0 + 64, 2, P * j:P * j + P], VTK[:, g, 64 * h:64 * h + 64], MKS[:, n, P:2 * P], True, False)
                        mm(mW[p0:p0 + 64, 2, P * j:P * j + P], ZZ[:, g, 64 * h:64 * h + 64], NB[:, n, P:2 * P], False, False)
                        for c in (0, 1):
                            ins = mm(mW[p0:p0 + 64, 2, P * j + 64 * c:P * j + 64 * c + 64], SS[p0:p0 + 64, j, 2 * g + c, :],
                                     AR[p0:p0 + 64, j, g, 1, 64 * c:64 * c + 64], False, c == 1)
                    ins.then_inc(*pe_of.step("rw.y", g))
                fill("tail")
                pe.wait_ge(*dve_of.at("rw.y", l, 1))
                head_norm("n0", (0, 1))
                fill("end")
                pe.wait_ge(*dve_of.at("ms.sum", l, 3))
                for p in range(4):
                    pair("out", "mg.out", l, 2 * p, [MG[:, k, :] for k in range(KT)])
                    if p:
                        pe.wait_ge(*dve_of.at("mg.out", l, 2 * p - 1))
                        mean(0, 2 * p - 2)

                def norm(i):
                    for k in range(KT):
                        if k % 4 == 0:
                            pe.wait_ge(*act_of.at("ln.sq", l, 2 * i + k // 4))
                        ins = mm(mW[:, 1, 0:T], C("mean"), V8[:, k, :], k == 0, k == KT - 1)
                    ins.then_inc(*pe_of.step("ln.var", i))
                    pe.wait_ge(*act_of.at("ln.half", l, i))
                    rest_of_x.append(act_of.at("ln.norm", l, i))

                if l == DEPTH - 1:
                    pe.wait_ge(*pe_of.at("mg.out", l, KT - 1))
                    for done in (split0, split1, down_done):
                        pe.sem_inc(done, FC)
                pe.wait_ge(*dve_of.at("mg.out", l, KT - 1))
                mean(0, KT - 2)
                norm(0)
                if l == 0:
                    rest_of_x[:] = [dve_of.at("ff.xl", l, 1)]
                    pe.wait_ge(*dve_of.at("ff.xl", l, 0))
                    for c in range(FC):
                        if c >= 2:
                            pe.wait_ge(*dve_of.at("ff.hid", l, c - 2))
                        for part in range(2):
                            i = 2 * c + part
                            ck[0] += 1
                            pe.wait_ge(*dve_of.at("ff.lo", l, i))
                            wh, wl = (w[:, i % 2, :].rearrange("p (k n) -> p k n", k=KT) for w in (FWH, FWL))
                            for q in range(2):
                                for k in range(KT):
                                    if k == 4 and rest_of_x:
                                        pe.wait_ge(*rest_of_x.pop())
                                    for w, x in ((wh, XH), (wh, XL), (wl, XH)):
                                        ins = mm(ff_acc(c, 2 * part + q), w[:, k, P * q:P * q + P], x[:, k, :],
                                                 k == 0 and w is wh and x is XH, k == KT - 1 and w is wl)
                            ins.then_inc(*pe_of.step("ff.part", i))
                    pe.wait_ge(*dve_of.at("ff.hid", l, FC - 2))
                    for p in range(4):
                        for w in range(3):
                            i = 2 * FC + 3 * p + w
                            ck[0] += 1
                            pe.wait_ge(*dve_of.at("ff.lo", l, i))
                            tiles = range(KT * w, min(KT * w + KT, FT))
                            pe.wait_ge(*dve_of.at("ff.hl", l, tiles[-1] // 2))
                            wh, wl = (x[:, i % 2, :].rearrange("p (k n) -> p k n", k=KT) for x in (FWH, FWL))
                            for q in range(2):
                                if w == 0:
                                    free(numbers["d", l, 2 * p + q])
                                for k in tiles:
                                    for a, x in ((wh, HH), (wh, HL), (wl, HH)):
                                        ins = mm(acc("d", l, 2 * p + q), a[:, k % KT, P * q:P * q + P], x[:, k, :],
                                                 k == 0 and a is wh and x is HH, k == FT - 1 and a is wl)
                                if w == 2:
                                    ins.then_inc(*pe_of.step("ff.down", 2 * p + q))
                            if w < 2:
                                ins.then_inc(*pe_of.step("ff.part", i - p))
                        if p:
                            pe.wait_ge(*dve_of.at("ff.down", l, 2 * p - 1))
                            mean(1, 2 * p - 2)
                    pe.wait_ge(*dve_of.at("ff.down", l, KT - 1))
                    mean(1, KT - 2)
                else:
                    pe.wait_ge(*rest_of_x.pop())
                    moe_tensor(pe, mm, mean)
                norm(1)



IN_SIZES = (896, 512, 256, 256, 4, 4, 128, 128, 256, 256, 16, 256, 256, 4096)


def projection_columns():
    off = np.concatenate([[0], np.cumsum(IN_SIZES)])
    rw, mqk, mv, mo, mi, mf, gq, gk, gv, gg, ga, rx, ry, gates = off[:14]
    cols = -np.ones((NM, P), np.int64)
    r = np.arange(P)
    for first, n, tile in ((rw, 7, 0), (mqk, 4, TMQ), (mv, 2, TMV), (mo, 2, TMO), (gq, 1, TGQ), (gk, 1, TGK),
                           (gv, 2, TGV), (gg, 2, TGG), (rx, 2, TRX), (ry, 2, TRY)):
        for i in range(n):
            cols[tile + i] = first + P * i + r
    cols[TMI, 0:4] = mi + np.arange(4)
    cols[TMI, 32:36] = mf + np.arange(4)
    cols[TMI, 64:80] = ga + np.arange(16)
    for i in range(NG):
        cols[NU + i] = gates + P * i + r
    return cols


def slots_of(w):
    *lead, rows, n = w.shape
    w = w.reshape(*lead, KT, P, n // 256, 256)
    k = len(lead)
    w = np.moveaxis(w, (k + 2, k + 1, k, k + 3), (k, k + 1, k + 2, k + 3))
    return w.reshape(*lead, n // 256, P, SLOT)


def by_partition(a):
    return np.swapaxes(a.reshape(*a.shape[:-1], -1, P), -1, -2)


def lay_out(i):
    f = {k: np.asarray(x) for k, x in i.items()}
    L = DEPTH
    out = {"const": constants()}
    x = np.concatenate([f["x_prompt"].reshape(TP, D), f["x_sample"].reshape(TD, D)], 0)
    out["x"] = np.ascontiguousarray(x.T.reshape(KT, P, T).transpose(1, 0, 2))
    cols = projection_columns()
    flat, there = cols.reshape(-1), cols.reshape(-1) >= 0
    w = np.zeros((L, D, NM * P), np.float32)
    w[:, :, there] = f["w_in"][:, :, flat[there]]
    out["w_in"] = slots_of(w)
    bias = np.zeros((L, NM * P), np.float32)
    bias[:, there] = f["b_in"][:, flat[there]]
    out["w_branch"] = f["w_branch"].reshape(L, 4, 2, P, D).transpose(0, 1, 3, 2, 4).reshape(L, 4, P, SLOT)
    out["w_out"] = slots_of(f["w_out"])
    up = np.stack([slots_of(f["ffn_wg"])[0], slots_of(f["ffn_wu"])[0]], 1)
    out["ffn_up"] = up.reshape(2 * FC, P, SLOT)
    down = np.zeros((3 * KT * P, D), np.float32)
    down[:FF] = f["ffn_wd"][0]
    out["ffn_down"] = np.stack([slots_of(down[D * q:D * q + D]) for q in range(3)], 1).reshape(12, P, SLOT)
    moe = np.empty((NE, FC, 3, P, SLOT), np.float32)
    gu = np.stack([f[w][0].reshape(NE, 2, 4, P, FC, 256) for w in ("moe_wg", "moe_wu")], 5)
    moe[:, :, 0:2] = gu.transpose(0, 4, 1, 3, 2, 5, 6).reshape(NE, FC, 2, P, SLOT)
    moe[:, :, 2] = f["moe_wd"][0].reshape(NE, FC, 2, P, D).transpose(0, 1, 3, 2, 4).reshape(NE, FC, P, SLOT)
    moe = moe.reshape(NE * FC * 3, P, SLOT)
    out["moe"] = np.concatenate([moe, moe[0:2]])
    out["router"] = np.ascontiguousarray(f["moe_router"][0].reshape(KT, P, NE).transpose(1, 0, 2))
    out["rbias"] = np.ascontiguousarray(np.broadcast_to(f["moe_router_b"], (P, NE)))

    def taps(w, n):
        return w.reshape(L, 4, n, P).transpose(0, 3, 2, 1).reshape(L, P, 4 * n)

    par = {"bin": by_partition(bias[:, :NU * P]), "bgate": by_partition(bias[:, NU * P:]), "mcw": taps(f["mlstm_conv_w"], 4),
           "rcw": taps(f["rglru_conv_w"], 2), "rk": by_partition(f["rwkv_r_k"].reshape(L, -1))}
    for name, src in (("mu", "rwkv_mu"), ("w0", "rwkv_w0"), ("a0", "rwkv_a0"), ("kk", "rwkv_k_k"), ("ka", "rwkv_k_a"),
                      ("lnw", "rwkv_ln_w"), ("lnb", "rwkv_ln_b"), ("mcb", "mlstm_conv_b"), ("mnw", "mlstm_norm_w"),
                      ("gab", "gla_alpha_b"), ("gnw", "gla_norm_w"), ("rcb", "rglru_conv_b"), ("rba", "rglru_ba"),
                      ("rbx", "rglru_bx"), ("lam", "rglru_lambda"), ("ln1g", "ln1_g"), ("ln1b", "ln1_b"),
                      ("ln2g", "ln2_g"), ("ln2b", "ln2_b")):
        par[name] = by_partition(f[src])
    out["par"] = np.concatenate([par[name] for name in PC], -1)
    out["lora"] = np.concatenate([f["rwkv_w_up"], f["rwkv_a_up"], f["rwkv_g_up"]], 1)
    alup = np.zeros((L, P, P), np.float32)
    alup[:, 64:80] = f["gla_alpha_up"]
    out["alup"] = alup
    rgw = np.zeros((L, P, 4, P), np.float32)
    for k, name in enumerate(("rglru_wa", "rglru_wx")):
        for j in range(2):
            for e in range(2):
                rgw[:, 64 * e:64 * e + 64, 2 * k + j, 64 * e:64 * e + 64] = f[name][:, 2 * j + e]
    out["rgw"] = rgw
    t = np.transpose
    out["shift"] = t(f["state_rwkv_shift"].reshape(L, TD, 7, P), (0, 3, 2, 1))
    out["mconv"] = t(f["state_mlstm_conv"].reshape(L, TD, 3, 4, P), (0, 4, 3, 2, 1))
    out["rconv"] = t(f["state_rglru_conv"].reshape(L, TD, 3, 2, P), (0, 4, 3, 2, 1))
    out["h0"] = t(f["state_rglru_h"].reshape(L, TD, 2, P), (0, 3, 2, 1))
    out["n0"] = t(f["state_mlstm_n"].reshape(L, TD, 2, P), (0, 3, 2, 1))
    out["m0"] = t(f["state_mlstm_m"], (0, 2, 1))
    for name, src in (("mC", "state_mlstm_C"), ("rS", "state_rwkv_S")):
        out[name] = t(f[src].reshape(L, TD, 2, 2, 64, 64), (0, 3, 5, 2, 1, 4)).reshape(L, P, 2, TD, 64)
    out["gS"] = t(f["state_gla_S"], (0, 2, 3, 1, 4)).reshape(L, P, TD, 64)
    return {k: np.ascontiguousarray(x) for k, x in out.items()}


OUTS = {"y": (P, KT, T), "h": (DEPTH, P, 2, 9), "rconv": (DEPTH, P, 2, 3, 9), "shift": (DEPTH, P, 7, 9), "m": (DEPTH, 4, 9),
        "mconv": (DEPTH, P, 4, 3, 9), "mC": (DEPTH, P, 2, 64), "mCs": (DEPTH, P, 2, TD, 64), "n": (DEPTH, P, 2, 9),
        "gSs": (DEPTH, P, TD, 64), "gS": (DEPTH, P, 256), "rSs": (DEPTH, P, 2, TD, 64), "rS": (DEPTH, P, 2, 64)}


def take_out(o):
    L, t = DEPTH, np.transpose
    y = t(o["y"], (2, 1, 0)).reshape(T, D)
    cols = {"shift": t(o["shift"], (0, 3, 2, 1)).reshape(L, 9, 896), "h": t(o["h"], (0, 3, 2, 1)).reshape(L, 9, 256),
            "n": t(o["n"], (0, 3, 2, 1)).reshape(L, 9, 4, 64), "m": t(o["m"], (0, 2, 1)),
            "mconv": t(o["mconv"], (0, 4, 3, 2, 1)).reshape(L, 9, 3, 512),
            "rconv": t(o["rconv"], (0, 4, 3, 2, 1)).reshape(L, 9, 3, 256)}

    def square(x, n):
        return t(x.reshape(L, 2, 64, 2, n, 64), (0, 4, 3, 1, 5, 2)).reshape(L, n, 4, 64, 64)

    def states(lo, hi, rS, mC, gS):
        c = {k: np.ascontiguousarray(a[:, lo:hi]) for k, a in cols.items()}
        return c["shift"], rS, c["mconv"], mC, c["n"], c["m"], gS, c["rconv"], c["h"]

    gp = o["gS"].reshape(L, 4, 32, 4, 64)
    gp = np.stack([gp[:, h, :, h] for h in range(4)], 1)[:, None]
    gs = t(o["gSs"].reshape(L, 4, 32, TD, 64), (0, 3, 1, 2, 4))
    prompt = states(0, 1, square(o["rS"], 1), square(o["mC"], 1), gp)
    sample = states(1, 9, square(o["rSs"], TD), square(o["mCs"], TD), gs)
    out = (y[None, :TP], y[TP:, None]) + prompt + sample
    return tuple(np.ascontiguousarray(a) for a in out)


def kernel(**inputs):
    import concourse.bacc as _bacc
    from concourse.bass_utils import run_bass_kernel_spmd as _run

    nc = _bacc.Bacc("TRN2", target_bir_lowering=False, num_devices=1)
    arrays = {f"in_{k}_dram": a for k, a in lay_out(inputs).items()}
    A = {k[3:-5]: nc.dram_tensor(k, a.shape, F32, kind="ExternalInput").ap() for k, a in arrays.items()}
    O = {k: nc.dram_tensor(f"out_{k}_dram", shape, F32, kind="ExternalOutput").ap() for k, shape in OUTS.items()}
    program(nc, A, O)
    r = _run(nc, [arrays], core_ids=[0])
    return take_out({k: r.results[0][f"out_{k}_dram"] for k in OUTS})
```
